# Optimizing a Trainium2 kernel written in Bass

```python
import jax, jax.numpy as jnp
from jax import lax
import numpy as np

D_MODEL = 1024
BATCH = 1
SEQ = 512
DEPTH = 1
DEC_BATCH = 8
DEC_SEQ = 1
PAST_LEN = 2048
PAGE_SIZE = 128

MIX_WIDTH = D_MODEL
N_ATT_HEADS = 8
QK_NOPE = 64
QK_ROPE = 32
V_HEAD = 64
ATT_WIDTH = N_ATT_HEADS * V_HEAD
Q_LORA = 384
KV_LORA = 256
ROPE_THETA = 10000.0
SM_SCALE = (QK_NOPE + QK_ROPE) ** -0.5
REC_WIDTH = MIX_WIDTH - ATT_WIDTH
REC_BLOCKS = 8
REC_BLOCK_W = REC_WIDTH // REC_BLOCKS
CONV_W = 4
LRU_C = 8.0
N_GROUPS = 4
EXPERTS_PER_GROUP = 8
N_EXPERTS = N_GROUPS * EXPERTS_PER_GROUP
TOP_K = 2
D_EXPERT = 256
Q_BLOCK = 128
ALPHA = (2.0 * DEPTH) ** 0.25
BETA = (8.0 * DEPTH) ** -0.25
LN_EPS = 1e-5
RMS_EPS = 1e-6
NEG_INF = -1e30
IN_WIDTH = Q_LORA + KV_LORA + QK_ROPE + 2 * REC_WIDTH
_SPLITS = (Q_LORA, Q_LORA + KV_LORA, Q_LORA + KV_LORA + QK_ROPE, Q_LORA + KV_LORA + QK_ROPE + REC_WIDTH)

kernel_name = "hymba_mla_rglru_hmoe_deepnorm_step"

def _rmsnorm(x, g):
    xf = x.astype(jnp.float32)
    y = xf * lax.rsqrt(jnp.mean(xf * xf, axis=-1, keepdims=True) + RMS_EPS)
    return (y * g.astype(jnp.float32)).astype(x.dtype)

def _layernorm(x, g, b):
    xf = x.astype(jnp.float32)
    mu = jnp.mean(xf, axis=-1, keepdims=True)
    xc = xf - mu
    var = jnp.mean(xc * xc, axis=-1, keepdims=True)
    return (xc * lax.rsqrt(var + LN_EPS) * g.astype(jnp.float32) + b.astype(jnp.float32)).astype(x.dtype)

def _rope_tables(pos):
    half = QK_ROPE // 2
    inv = ROPE_THETA ** (-(jnp.arange(half, dtype=jnp.float32) * 2.0 / QK_ROPE))
    ang = pos.astype(jnp.float32)[:, None] * inv[None, :]
    return jnp.cos(ang), jnp.sin(ang)

def _rope(x, cos, sin):
    x1, x2 = jnp.split(x.astype(jnp.float32), 2, axis=-1)
    return jnp.concatenate([x1 * cos - x2 * sin, x2 * cos + x1 * sin], axis=-1).astype(x.dtype)

def _project(x, pos, w_in, q_norm_g, w_uq, kv_norm_g):
    z = jnp.einsum('btd,de->bte', x, w_in)
    q_lat, kv_lat, k_pe, rec_x, rec_gate = jnp.split(z, _SPLITS, axis=-1)
    q = jnp.einsum('btq,qhe->bthe', _rmsnorm(q_lat, q_norm_g), w_uq)
    q_nope, q_pe = q[..., :QK_NOPE], q[..., QK_NOPE:]
    cos, sin = _rope_tables(pos)
    q_pe = _rope(q_pe, cos[None, :, None, :], sin[None, :, None, :])
    k_pe = _rope(k_pe, cos[None], sin[None])
    c_kv = _rmsnorm(kv_lat, kv_norm_g)
    return q_nope, q_pe, c_kv, k_pe, rec_x, rec_gate

def _mla_prompt(q_nope, q_pe, c_kv, k_pe, w_uk, w_uv):
    B, S = c_kv.shape[0], c_kv.shape[1]
    k_nope = jnp.einsum('bsc,chn->bshn', c_kv, w_uk)
    v = jnp.einsum('bsc,chv->bshv', c_kv, w_uv)
    nb = S // Q_BLOCK
    qn = q_nope.reshape(B, nb, Q_BLOCK, N_ATT_HEADS, QK_NOPE).transpose(1, 0, 2, 3, 4)
    qp = q_pe.reshape(B, nb, Q_BLOCK, N_ATT_HEADS, QK_ROPE).transpose(1, 0, 2, 3, 4)
    kpos = jnp.arange(S)

    def block(args):
        qn_b, qp_b, i = args
        s = (jnp.einsum('bqhn,bkhn->bhqk', qn_b, k_nope)
             + jnp.einsum('bqhr,bkr->bhqk', qp_b, k_pe)).astype(jnp.float32) * SM_SCALE
        qpos = i * Q_BLOCK + jnp.arange(Q_BLOCK)
        s = jnp.where(kpos[None, :] <= qpos[:, None], s, NEG_INF)
        p = jax.nn.softmax(s, axis=-1).astype(v.dtype)
        return jnp.einsum('bhqk,bkhv->bqhv', p, v)

    o = lax.map(block, (qn, qp, jnp.arange(nb)))
    return o.transpose(1, 0, 2, 3, 4).reshape(B, S, N_ATT_HEADS * V_HEAD)

def _mla_sample(q_nope, q_pe, c_new, kpe_new, cache_kv_latent, cache_k_rope, page_table, w_uk, w_uv):
    Bd, T = c_new.shape[0], c_new.shape[1]
    c_past = cache_kv_latent[page_table].reshape(Bd, -1, KV_LORA)
    kpe_past = cache_k_rope[page_table].reshape(Bd, -1, QK_ROPE)
    P = c_past.shape[1]
    q_lat = jnp.einsum('bthn,chn->bthc', q_nope, w_uk)
    s_past = (jnp.einsum('bthc,bpc->bhtp', q_lat, c_past)
              + jnp.einsum('bthr,bpr->bhtp', q_pe, kpe_past)).astype(jnp.float32)
    s_new = (jnp.einsum('bthc,buc->bhtu', q_lat, c_new)
             + jnp.einsum('bthr,bur->bhtu', q_pe, kpe_new)).astype(jnp.float32)
    causal = jnp.arange(T)[None, :] <= jnp.arange(T)[:, None]
    s_new = jnp.where(causal, s_new, NEG_INF)
    p = jax.nn.softmax(jnp.concatenate([s_past, s_new], axis=-1) * SM_SCALE, axis=-1)
    p_past = p[..., :P].astype(c_past.dtype)
    p_new = p[..., P:].astype(c_new.dtype)
    o_lat = (jnp.einsum('bhtp,bpc->bthc', p_past, c_past)
             + jnp.einsum('bhtu,buc->bthc', p_new, c_new))
    o = jnp.einsum('bthc,chv->bthv', o_lat, w_uv)
    return o.reshape(Bd, T, N_ATT_HEADS * V_HEAD)

def _rglru_block(rec_x, rec_gate, conv_state, h0, conv_w, conv_b, w_rg, b_rg, w_ig, b_ig, lru_lambda):
    B, T = rec_x.shape[0], rec_x.shape[1]
    xp = jnp.concatenate([conv_state.astype(rec_x.dtype), rec_x], axis=1)
    xc = conv_b + sum(xp[:, k:k + T] * conv_w[k] for k in range(CONV_W))
    new_conv = xp[:, T:]
    xb = xc.reshape(B, T, REC_BLOCKS, REC_BLOCK_W)
    r = jax.nn.sigmoid((jnp.einsum('btnd,nde->btne', xb, w_rg).reshape(B, T, REC_WIDTH) + b_rg).astype(jnp.float32))
    i = jax.nn.sigmoid((jnp.einsum('btnd,nde->btne', xb, w_ig).reshape(B, T, REC_WIDTH) + b_ig).astype(jnp.float32))
    log_a = -LRU_C * jax.nn.softplus(-lru_lambda.astype(jnp.float32)) * r
    a = jnp.exp(log_a)
    u = jnp.sqrt(-jnp.expm1(2.0 * log_a)) * (i * xc.astype(jnp.float32))

    def step(h, au):
        a_t, u_t = au
        h = a_t * h + u_t
        return h, h

    h_last, hs = lax.scan(step, h0.astype(jnp.float32), (jnp.swapaxes(a, 0, 1), jnp.swapaxes(u, 0, 1)))
    y = jnp.swapaxes(hs, 0, 1) * jax.nn.gelu(rec_gate.astype(jnp.float32))
    return y.astype(rec_x.dtype), new_conv, h_last.astype(h0.dtype)

def _hier_moe(x, w_group, b_group, w_expert, b_expert, w_gate_up, w_down):
    B, T, D = x.shape
    xt = x.reshape(B * T, D)
    n = xt.shape[0]
    rows = jnp.arange(n)
    g_logits = jnp.einsum('nd,dg->ng', xt, w_group).astype(jnp.float32)
    g_prob = jax.nn.softmax(g_logits, axis=-1)
    g_sel = jnp.argmax(g_logits + b_group.astype(jnp.float32), axis=-1)
    e_logits = jnp.einsum('nd,de->ne', xt, w_expert).astype(jnp.float32).reshape(n, N_GROUPS, EXPERTS_PER_GROUP)
    e_sel = e_logits[rows, g_sel]
    e_bias = b_expert.astype(jnp.float32).reshape(N_GROUPS, EXPERTS_PER_GROUP)[g_sel]
    _, top_i = lax.top_k(e_sel + e_bias, TOP_K)
    top_p = jax.nn.softmax(jnp.take_along_axis(e_sel, top_i, axis=-1), axis=-1)
    gates_k = g_prob[rows, g_sel][:, None] * top_p
    expert_idx = g_sel[:, None] * EXPERTS_PER_GROUP + top_i
    gate = jnp.sum(jax.nn.one_hot(expert_idx, N_EXPERTS, dtype=jnp.float32) * gates_k[..., None], axis=1)
    y = jnp.zeros((n, D), jnp.float32)
    for e in range(N_EXPERTS):
        gu = xt @ w_gate_up[e]
        h = jax.nn.silu(gu[:, :D_EXPERT]) * gu[:, D_EXPERT:]
        y = y + gate[:, e:e + 1] * (h @ w_down[e]).astype(jnp.float32)
    return y.astype(x.dtype).reshape(B, T, D)

def _merge_and_ffn(x, att_o, rec_o, att_out_g, rec_out_g, w_out, ln1_g, ln1_b,
                   w_group, b_group, w_expert, b_expert, w_gate_up, w_down, ln2_g, ln2_b):
    mixed = jnp.concatenate([_rmsnorm(att_o, att_out_g), _rmsnorm(rec_o, rec_out_g)], axis=-1)
    mix = jnp.einsum('bte,ed->btd', mixed, w_out)
    x1 = _layernorm(ALPHA * x + mix, ln1_g, ln1_b)
    ffn = _hier_moe(x1, w_group, b_group, w_expert, b_expert, w_gate_up, w_down)
    return _layernorm(ALPHA * x1 + ffn, ln2_g, ln2_b)

def setup_inputs(seed: int = 0) -> dict:
    key = jax.random.key(seed)
    ks = jax.random.split(key, 40)
    f32 = jnp.float32
    n_pages = PAST_LEN // PAGE_SIZE
    n_used = DEC_BATCH * n_pages
    n_pool = (n_used * 5) // 4

    def nrm(k, shape, scale):
        return jax.random.normal(k, shape, f32) * scale

    u = jax.random.uniform(ks[19], (REC_WIDTH,), f32, 0.9, 0.999)
    a0 = u ** (1.0 / LRU_C)
    return {
        'x_prompt': nrm(ks[0], (BATCH, SEQ, D_MODEL), 1.0),
        'x_sample': nrm(ks[1], (DEC_BATCH, DEC_SEQ, D_MODEL), 1.0),
        'cache_kv_latent': nrm(ks[2], (n_pool, PAGE_SIZE, KV_LORA), 1.0),
        'cache_k_rope': nrm(ks[3], (n_pool, PAGE_SIZE, QK_ROPE), 1.0),
        'state_conv': nrm(ks[4], (DEC_BATCH, CONV_W - 1, REC_WIDTH), 1.0),
        'state_rec': nrm(ks[5], (DEC_BATCH, REC_WIDTH), 0.5),
        'page_table': jax.random.permutation(ks[6], n_pool)[:n_used].reshape(DEC_BATCH, n_pages).astype(jnp.int32),
        'w_in': nrm(ks[7], (D_MODEL, IN_WIDTH), D_MODEL ** -0.5),
        'q_norm_g': 1.0 + nrm(ks[8], (Q_LORA,), 0.01),
        'w_uq': nrm(ks[9], (Q_LORA, N_ATT_HEADS, QK_NOPE + QK_ROPE), Q_LORA ** -0.5),
        'kv_norm_g': 1.0 + nrm(ks[10], (KV_LORA,), 0.01),
        'w_uk': nrm(ks[11], (KV_LORA, N_ATT_HEADS, QK_NOPE), KV_LORA ** -0.5),
        'w_uv': nrm(ks[12], (KV_LORA, N_ATT_HEADS, V_HEAD), KV_LORA ** -0.5 * BETA),
        'conv_w': nrm(ks[13], (CONV_W, REC_WIDTH), CONV_W ** -0.5),
        'conv_b': nrm(ks[14], (REC_WIDTH,), 0.01),
        'w_rg': nrm(ks[15], (REC_BLOCKS, REC_BLOCK_W, REC_BLOCK_W), REC_BLOCK_W ** -0.5),
        'b_rg': nrm(ks[16], (REC_WIDTH,), 0.01),
        'w_ig': nrm(ks[17], (REC_BLOCKS, REC_BLOCK_W, REC_BLOCK_W), REC_BLOCK_W ** -0.5),
        'b_ig': nrm(ks[18], (REC_WIDTH,), 0.01),
        'lru_lambda': jnp.log(a0) - jnp.log1p(-a0),
        'att_out_g': 1.0 + nrm(ks[20], (ATT_WIDTH,), 0.01),
        'rec_out_g': 1.0 + nrm(ks[21], (REC_WIDTH,), 0.01),
        'w_out': nrm(ks[22], (MIX_WIDTH, D_MODEL), MIX_WIDTH ** -0.5 * BETA),
        'ln1_g': 1.0 + nrm(ks[23], (D_MODEL,), 0.01),
        'ln1_b': nrm(ks[24], (D_MODEL,), 0.01),
        'w_group': nrm(ks[25], (D_MODEL, N_GROUPS), D_MODEL ** -0.5),
        'b_group': nrm(ks[26], (N_GROUPS,), 0.01),
        'w_expert': nrm(ks[27], (D_MODEL, N_EXPERTS), D_MODEL ** -0.5),
        'b_expert': nrm(ks[28], (N_EXPERTS,), 0.01),
        'w_gate_up': nrm(ks[29], (N_EXPERTS, D_MODEL, 2 * D_EXPERT), D_MODEL ** -0.5 * BETA),
        'w_down': nrm(ks[30], (N_EXPERTS, D_EXPERT, D_MODEL), D_EXPERT ** -0.5 * BETA),
        'ln2_g': 1.0 + nrm(ks[31], (D_MODEL,), 0.01),
        'ln2_b': nrm(ks[32], (D_MODEL,), 0.01),
    }

def reference(x_prompt, x_sample, cache_kv_latent, cache_k_rope, state_conv, state_rec, page_table,
              w_in, q_norm_g, w_uq, kv_norm_g, w_uk, w_uv, conv_w, conv_b, w_rg, b_rg, w_ig, b_ig,
              lru_lambda, att_out_g, rec_out_g, w_out, ln1_g, ln1_b, w_group, b_group, w_expert,
              b_expert, w_gate_up, w_down, ln2_g, ln2_b):
    past_len = page_table.shape[1] * PAGE_SIZE
    y_p, y_s = x_prompt, x_sample
    for _layer in range(DEPTH):
        Bp, Sp = y_p.shape[0], y_p.shape[1]
        pos_p = jnp.arange(Sp, dtype=jnp.int32)
        qn, qp, c_p, kpe_p, rx, rg = _project(y_p, pos_p, w_in, q_norm_g, w_uq, kv_norm_g)
        att_p = _mla_prompt(qn, qp, c_p, kpe_p, w_uk, w_uv)
        conv0 = jnp.zeros((Bp, CONV_W - 1, REC_WIDTH), rx.dtype)
        h0 = jnp.zeros((Bp, REC_WIDTH), state_rec.dtype)
        rec_p, conv_p, h_p = _rglru_block(rx, rg, conv0, h0, conv_w, conv_b, w_rg, b_rg, w_ig, b_ig, lru_lambda)
        y_p = _merge_and_ffn(y_p, att_p, rec_p, att_out_g, rec_out_g, w_out, ln1_g, ln1_b,
                             w_group, b_group, w_expert, b_expert, w_gate_up, w_down, ln2_g, ln2_b)
        pos_s = past_len + jnp.arange(y_s.shape[1], dtype=jnp.int32)
        qn, qp, c_s, kpe_s, rx, rg = _project(y_s, pos_s, w_in, q_norm_g, w_uq, kv_norm_g)
        att_s = _mla_sample(qn, qp, c_s, kpe_s, cache_kv_latent, cache_k_rope, page_table, w_uk, w_uv)
        rec_s, conv_s, h_s = _rglru_block(rx, rg, state_conv, state_rec, conv_w, conv_b, w_rg, b_rg, w_ig, b_ig, lru_lambda)
        y_s = _merge_and_ffn(y_s, att_s, rec_s, att_out_g, rec_out_g, w_out, ln1_g, ln1_b,
                             w_group, b_group, w_expert, b_expert, w_gate_up, w_down, ln2_g, ln2_b)
    return (y_p, y_s, c_p, kpe_p, conv_p, h_p, c_s, kpe_s, conv_s, h_s)


_drawn_inputs = setup_inputs


def setup_inputs(seed=0):
    import zlib

    import numpy as np

    out = dict(_drawn_inputs(seed))
    spreads = {}
    factors = {'q_norm_g': 8.0,
     'kv_norm_g': 5.466,
     'b_rg': 8.0,
     'b_ig': 8.0,
     'att_out_g': 8.0,
     'rec_out_g': 8.0,
     'ln1_g': 5.433,
     'ln1_b': 5.234,
     'b_group': 29.81,
     'b_expert': 34.365,
     'ln2_g': 33.431,
     'ln2_b': 31.788}
    for name, (base, spread) in spreads.items():
        noise = np.random.default_rng([zlib.crc32(name.encode()), seed]).standard_normal(out[name].shape)
        drawn = base * np.exp(spread * noise) if base else spread * noise
        out[name] = __import__('jax').numpy.asarray(drawn.astype(out[name].dtype))
    for name, factor in factors.items():
        out[name] = (out[name] * factor).astype(out[name].dtype)
    return out
```

```python
from contextlib import ExitStack

import numpy as np

import concourse.bass as bass
from concourse import mybir

ACT = mybir.ActivationFunctionType
ALU = mybir.AluOpType
AX_X = mybir.AxisListType.X
F32 = mybir.dt.float32
BF16 = mybir.dt.bfloat16
I32 = mybir.dt.int32
U32 = mybir.dt.uint32

P = 128
D = 1024
KD = D // P
SEQ = 512
DEC = 8
TOK = SEQ + DEC
HALF = TOK // 2
PAST, PAGE = 2048, 128
N_PAGES = PAST // PAGE
NPOOL = DEC * N_PAGES * 5 // 4
NH, NOPE, ROPE, VH = 8, 64, 32, 64
QL, KVL, REC = 384, 256, 512
KQ, KKV, KR = QL // P, KVL // P, REC // P
CONV = 4
NG, EPG, NE, DE = 4, 8, 32, 256
SM = float((NOPE + ROPE) ** -0.5)
ALPHA = float(2.0 ** 0.25)
LN_EPS, RMS_EPS = 1e-5, 1e-6
NEG = -1e30
TT = 5
ROWS = [P, P, P, P, DEC]
SHIFT = SEQ // 2
WIN = TOK - SHIFT

CAP = 64
GRP = 4
NGRP = NE // GRP
MAXR = -(-TOK // CAP)
BLK = CAP * GRP
NTAB = (MAXR * NGRP + 1) * BLK
FREE_SLOT = 8191
HALF_ID = 1024

V_QG, V_KVG, V_CW, V_CB, V_BR, V_BI, V_LAM, V_AG, V_RG = 0, 3, 5, 21, 25, 29, 33, 37, 41
NV = 45

U_RX, U_KV, U_KPE, U_Q, U_R, U_I, U_NQ, U_NKV, U_G, U_UQ, U_UK, U_V = 0, 4, 6, 7, 10, 14, 18, 19, 20, 24, 32, 36
N_UNITS = 40
CHUNK_OF = {**{U_RX + c: c for c in range(4)}, U_KV: 4, U_KV + 1: 5, U_Q: 6, U_Q + 1: 7, U_Q + 2: 8,
            **{U_G + c: 9 + c for c in range(4)}}
N_CHUNKS = 13
LAND_OF = [0, 1, 2, 3, 4, 5, 6, 6, 6, 7, 7, 7, 7]

W_X = N_CHUNKS * D + KD * 64
W_SLOT = KD * 2 * DE + 2 * D
W_LEN = 3 * W_SLOT
W_P, W_PT = 2 * W_SLOT, 2 * W_SLOT + 2 * 1280
CB = 16 * (KVL + ROPE)
W_OP = 2 * CB
W_KT = 2 * W_SLOT
W_RT, W_DP, W_DPT = W_KT + 4096, W_KT + 4608, W_KT + 5120
O_UQ, O_UK, O_UV, O_UKT, O_GATE = 0, 3072, 4096, 5120, 7168
O_LEN = KD * D
S_QH, S_KH, S_V, S_ATT, S_REC, S_XC, S_XP, S_TMP = 0, 4160, 8256, 10304, 12384, 14464, 16544, 18624
S_QZ, S_KVZ, S_RQ, S_RKV, S_KPE = 20184, 21744, 22784, 23304, 23824
S_LEN = 24344
S_SQ0 = S_KH
S_QQ, S_QS = S_XC, S_XC + 8 * 192
S_X1, S_UV2, S_SQ = 0, 9280, 5120
S_RT = 9280
S_X1T = S_XC
S_WR = S_TMP
S_LN = 19392
S_T = S_KVZ
S_XG, S_YB, S_E = 5120, S_ATT, S_XC

OFF = [0, 128, 384, 768]
POFF = [0, 512, 896, 1152]


def hymba_step(nc, xT, x_tok, kv_cache, rope_cache, conv_st, rec_st, page_rep, lane, w_in, w_kpe, w_uq, w_uk,
               w_uv, w_ukT, vecs, gates, cs_tab, w_out, w_router, r_bias, lns, ids, eoff, w_gu, w_dn,
               y_out, ckv_out, kpe_out, conv_p_out, rec_p_out, conv_s_out, rec_s_out):
    x1_rows = nc.dram_tensor("x1_rows", (TOK, D), F32, kind="Internal").ap()
    pair_rows = nc.dram_tensor("pair_rows", (2 * HALF_ID, D), F32, kind="Internal").ap()
    slot_table = nc.dram_tensor("slot_table", (NTAB, 1), I32, kind="Internal").ap()
    kv_rows = kv_cache.rearrange("n (c j) e -> (n c) (j e)", c=8)
    rope_rows = rope_cache.rearrange("n (c j) e -> (n c) (j e)", c=8)

    with ExitStack() as ctx:
        def sb(name, shape, dt=F32):
            return ctx.enter_context(nc.sbuf_tensor(name, shape, dt))

        def sem(name):
            return ctx.enter_context(nc.semaphore(name))

        ps = ctx.enter_context(nc.psum_tensor("ps", [P, 8, 512], F32))
        arena_w = sb("arena_w", [P, W_LEN])
        arena_o = sb("arena_o", [P, O_LEN])
        arena_s = sb("arena_s", [P, S_LEN])

        def part(arena, at, *dims):
            n = int(np.prod(dims))
            v = arena[:, at:at + n]
            if len(dims) == 2:
                v = v.rearrange("p (a b) -> p a b", a=dims[0])
            if len(dims) == 3:
                v = v.rearrange("p (a b c) -> p a b c", a=dims[0], b=dims[1])
            return v

        ident = sb("ident", [P, P])
        identb = sb("identb", [P, P], BF16)
        maskb = sb("maskb", [P, P], BF16)
        trib = sb("trib", [P, P], BF16)
        onesb = sb("onesb", [P, P], BF16)
        ones = sb("ones", [P, P])
        cs = sb("cs", [P, TOK])
        vec = sb("vec", [P, NV])
        lam = sb("lam", [P, 8, KR])
        nsp = sb("nsp", [P, 2, KR])
        bh = sb("bh", [P, 2, KR])
        eps = sb("eps", [P, 2])
        cdec = sb("cdec", [P, KR, CONV, DEC])
        conv_tail = sb("conv_tail", [P, KR, CONV - 1])
        rec_last = sb("rec_last", [P, KR])
        rst = sb("rst", [P, KR, DEC])
        rbias = sb("rbias", [P, NG + NE])
        stat = sb("stat", [P, 2, 4])
        mx = sb("mx", [P, DEC])
        ls = sb("ls", [P, DEC])
        nmd = sb("nmd", [P, 2])
        pages = sb("pages", [P, DEC], I32)
        lane_sb = sb("lane_sb", [P, 1], I32)
        kpn = sb("kpn", [ROPE, DEC])
        sel = sb("sel", [P, 32])
        wcol = sb("wcol", [P, DEC])
        rinv = sb("rinv", [P, 2, 2, 2])
        rinv4 = sb("rinv4", [DEC, 2])
        bn = sb("bn", [P, 2, 6])
        mv = sb("mv", [P, 4])
        gpad = sb("gpad", [P, TT, 8])
        top8 = sb("top8", [P, TT, 8])
        idx8 = sb("idx8", [P, TT, 8], U32)
        rs = sb("rs", [P, 16, TT])
        ohb = sb("ohb", [P, TT, NE], BF16)
        ohg = sb("ohg", [P, TT, NG])
        id_sb = sb("id_sb", [P, 2 * TT], I32)
        eoff_sb = sb("eoff_sb", [P, 2 * NE])
        valid = sb("valid", [P, TT])
        posi = sb("posi", [P, 2, TT], I32)
        posj = sb("posj", [P, 2, TT], I32)
        rounds = sb("rounds", [P, 2], I32)
        raw4 = sb("raw4", [CAP, GRP], I32)
        gidx = sb("gidx", [CAP, GRP], I32)
        sidx = sb("sidx", [CAP, GRP], I32)
        empty = sb("empty", [P, NTAB // P], I32)

        xTv = part(arena_w, W_X, KD, TOK)
        w_chunk = [part(arena_w, c * D, KD, P) for c in range(N_CHUNKS)]
        w_kpev = part(arena_w, N_CHUNKS * D, KD, 64)
        uq, uk, uv = part(arena_o, O_UQ, KQ, NH, P), part(arena_o, O_UK, KKV, 512), part(arena_o, O_UV, KKV, 512)
        ukT = part(arena_o, O_UKT, NH, KVL)
        gw = part(arena_o, O_GATE, 2, KR, P)
        wo = part(arena_o, 0, KD, D)
        qh, kh, v = part(arena_s, S_QH, NH, TOK), part(arena_s, S_KH, NH, SEQ), part(arena_s, S_V, 4, 512)
        attT, recT = part(arena_s, S_ATT, KR, TOK), part(arena_s, S_REC, KR, TOK)
        tr, xc, xp = attT, part(arena_s, S_XC, KR, TOK), part(arena_s, S_XP, KR, TOK)
        tmp = part(arena_s, S_TMP, 3, TOK)
        qz, kvz = part(arena_s, S_QZ, KQ, TOK), part(arena_s, S_KVZ, KKV, TOK)
        rq, rkv, kpe = part(arena_s, S_RQ, TOK), part(arena_s, S_RKV, TOK), part(arena_s, S_KPE, TOK)
        sq0 = part(arena_s, S_SQ0, KQ + KKV, TOK)
        Pb = [part(arena_w, W_P + 1280 * b, 1280) for b in range(2)]
        PTb = [part(arena_w, W_PT + 1280 * b, 1280) for b in range(2)]
        cache = [part(arena_w, CB * b, 16, KVL) for b in range(2)]
        crope = [part(arena_w, CB * b + 16 * KVL, 4, P) for b in range(2)]
        KT, ropeT = part(arena_w, W_KT, KKV, PAST), part(arena_w, W_RT, 512)
        dP, dPT = part(arena_w, W_DP, 512), part(arena_w, W_DPT, 512)
        op = part(arena_w, W_OP, DEC, KVL)
        qq, qs = part(arena_s, S_QQ, DEC, 192), part(arena_s, S_QS, 2, 192)
        qlt = part(arena_s, S_TMP, 512)
        fin = arena_s[0:DEC, S_RQ:S_RQ + 512]
        osum, tn, oT = part(arena_s, S_TMP, 512), part(arena_s, S_TMP + 512, KKV, DEC, NH), part(arena_s, S_TMP + 640, KKV, NH, DEC)
        uv2 = part(arena_s, S_UV2, KKV, 512)
        x1, sq = part(arena_s, S_X1, TT, D), part(arena_s, S_SQ, KD, TOK)
        L, Lb = part(arena_s, S_RT, TT, NG + NE), part(arena_s, S_RT + 180, TT, NG + NE)
        me, oh1, oh2, rt_t = (part(arena_s, S_RT + 360 + 160 * n, TT, NE) for n in range(4))
        x1T = part(arena_s, S_X1T, KD, TOK)
        wr = part(arena_s, S_WR, KD, 64)
        lng = part(arena_s, S_LN, 2, D)
        tb = [part(arena_s, S_T + D * b, D) for b in range(2)]
        ss, rt = part(arena_s, S_T, WIN), part(arena_s, S_T, WIN)
        slot = [arena_w[:, W_SLOT * n:W_SLOT * (n + 1)] for n in range(3)] + [arena_o[:, 0:W_SLOT]]
        gu_w = [s[:, 0:KD * 2 * DE].rearrange("p (k n) -> p k n", k=KD) for s in slot]
        dn_w = [s[:, KD * 2 * DE:W_SLOT].rearrange("p (k n) -> p k n", k=2) for s in slot]
        xg = [part(arena_s, S_XG + D * b, D) for b in range(GRP)]
        yb = [part(arena_s, S_YB + D * b, D) for b in range(GRP)]
        xgT = [part(arena_s, S_E + 512 * b, KD, CAP) for b in range(2)]
        sg = [part(arena_s, S_E + 1024 + DE * b, DE) for b in range(2)]
        hx = [part(arena_s, S_E + 1536 + DE * b, DE) for b in range(2)]
        hT = [part(arena_s, S_E + 2048 + P * b, 2, CAP) for b in range(2)]
        y1 = [part(arena_w, 2 * D * b, D) for b in range(2)]
        y2 = [part(arena_w, 2 * D * b + D, D) for b in range(2)]

        def pair(u, cols=HALF):
            b = 2 * (u % 4)
            return ps[:, b:b + 2, 0:cols]

        x_landed = [sem(f"x_landed{n}") for n in range(4)]
        win_landed = [sem(f"win_landed{n}") for n in range(8)]
        kpe_w_landed, gates_landed, uq_landed = sem("kpe_w_landed"), sem("gates_landed"), sem("uq_landed")
        ukv_landed, params_landed, cs_landed = sem("ukv_landed"), sem("params_landed"), sem("cs_landed")
        pages_landed, ids_landed = sem("pages_landed"), sem("ids_landed")
        wo_landed, uv2_landed, xtok_landed = sem("wo_landed"), sem("uv2_landed"), sem("xtok_landed")
        ln1_landed, ln2_landed = sem("ln1_landed"), sem("ln2_landed")
        cache_landed = [sem(f"cache_landed{b}") for b in range(2)]
        expert_landed = [sem(f"expert_landed{b}") for b in range(GRP)]
        table_empty, scattered_ids = sem("table_empty"), sem("scattered_ids")
        raw_landed = sem("raw_landed")
        gathered = [sem(f"gathered{b}") for b in range(GRP)]
        scattered = [sem(f"scattered{b}") for b in range(GRP)]
        x1_stored = sem("x1_stored")
        y_landed = [sem(f"y_landed{b}") for b in range(2)]
        y_stored = [sem(f"y_stored{b}") for b in range(2)]
        outs_stored = sem("outs_stored")
        dve_step, act_step, pool_step = sem("dve_step"), sem("act_step"), sem("pool_step")
        const_ready, ones_ready = sem("const_ready"), sem("ones_ready")
        unit_done = sem("unit_done")
        evac = [sem(f"evac{n}") for n in range(4)]
        conv_done, kpe_done, squares, wuq_scaled = sem("conv_done"), sem("kpe_done"), sem("squares"), sem("wuq_scaled")
        rms_root, ckv_done, rq_done = sem("rms_root"), sem("ckv_done"), sem("rq_done")
        gate_in, a_done, th_done, a2_done, w_done, root_w = (sem(n) for n in (
            "gate_in", "a_done", "th_done", "a2_done", "w_done", "root_w"))
        ix_done, h_done, rec_done = sem("ix_done"), sem("h_done"), sem("rec_done")
        lam_ready, eps_ready, sp_exp = sem("lam_ready"), sem("eps_ready"), sem("sp_exp")
        swap_done, qrope_done, khrope_done = sem("swap_done"), sem("qrope_done"), sem("khrope_done")
        s_done, nm_done, exp_done, p_done, t_done = (sem(n) for n in ("s_done", "nm_done", "exp_done", "p_done", "t_done"))
        pt_act, pt_dve, pv_done, att_done = sem("pt_act"), sem("pt_dve"), sem("pv_done"), sem("att_done")
        ql_done, ql_evac, qlT_done, qq_done = sem("ql_done"), sem("ql_evac"), sem("qlT_done"), sem("qq_done")
        kt_done, qs_done, sc_done, dmx_done, dexp_done = (sem(n) for n in ("kt_done", "qs_done", "sc_done", "dmx_done", "dexp_done"))
        kt_evac = [sem(f"kt_evac{n}") for n in range(3)]
        dpt_done, dpt_evac, op_done, op_evac = sem("dpt_done"), sem("dpt_evac"), sem("op_done"), sem("op_evac")
        cidx_ready, dmax_raw, diff_ready = sem("cidx_ready"), sem("dmax_raw"), sem("diff_ready")
        wr_landed, idx_half, idx_copied = sem("wr_landed"), sem("idx_half"), sem("idx_copied")
        f_pe, f_act, f_dve = sem("f_pe"), sem("f_act"), sem("f_dve")
        sq_done, wo_scaled, xa_done = sem("sq_done"), sem("wo_scaled"), sem("xa_done")
        d_pe, d_act, d_dve = sem("d_pe"), sem("d_act"), sem("d_dve")
        o_done, oA_done, oR_done, x1_sum, ln_norm, ln_g, x1_done = (sem(n) for n in (
            "o_done", "oA_done", "oR_done", "x1_sum", "ln_norm", "ln_g", "x1_done"))
        ln_var, ln_root = sem("ln_var"), sem("ln_root")
        x1T_ps, x1T_act, x1T_dve = sem("x1T_ps"), sem("x1T_act"), sem("x1T_dve")
        r_pe, r_act, r_dve, pos_ready = sem("r_pe"), sem("r_act"), sem("r_dve"), sem("pos_ready")
        xg_zero = sem("xg_zero")
        xt_ps, xt_sb, gu_ps, silu_done, h_ready, ht_ps, ht_sb, dn_ps, ya_done, yd_done = (sem(n) for n in (
            "xt_ps", "xt_sb", "gu_ps", "silu_done", "h_ready", "ht_ps", "ht_sb", "dn_ps", "ya_done", "yd_done"))
        g1_done, y_sum, v2_done, root2, n2_done, g2_done, y_ready = (sem(n) for n in (
            "g1_done", "y_sum", "v2_done", "root2", "n2_done", "g2_done", "y_ready"))

        block = ctx.enter_context(nc.Block())

        def landed(eng, s, n=1):
            eng.wait_ge(s, 16 * n)

        def store_y(sp, t):
            sp.dma_start(y_out[P * t:P * t + ROWS[t], :], y1[t % 2][0:ROWS[t], :]).then_inc(y_stored[t % 2], 16)

        @block.sync
        def _(sp):
            def chunk(c):
                sp.dma_start(arena_w[:, c * D:(c + 1) * D], w_in[c]).then_inc(win_landed[LAND_OF[c]], 16)
            sp.dma_start(xTv[:, 0:2, :], xT[:, 0:2, :]).then_inc(x_landed[0], 16)
            chunk(0)
            for n in range(1, 4):
                sp.dma_start(xTv[:, 2 * n:2 * n + 2, :], xT[:, 2 * n:2 * n + 2, :]).then_inc(x_landed[n], 16)
            for c in range(1, 6):
                chunk(c)
            sp.dma_start(arena_w[:, N_CHUNKS * D:W_X], w_kpe).then_inc(kpe_w_landed, 16)
            sp.dma_start(arena_o[:, O_GATE:O_GATE + 1024], gates).then_inc(gates_landed, 16)
            for c in range(6, N_CHUNKS):
                chunk(c)
            sp.dma_start(arena_o[:, O_UQ:O_UQ + 3072], w_uq).then_inc(uq_landed, 16)
            sp.dma_start(arena_o[:, O_UK:O_UK + 1024], w_uk).then_inc(ukv_landed, 16)
            sp.dma_start(arena_o[:, O_UV:O_UV + 1024], w_uv).then_inc(ukv_landed, 16)
            sp.dma_start(arena_o[0:NOPE, O_UKT:O_UKT + 2048], w_ukT).then_inc(ukv_landed, 16)
            sp.wait_ge(const_ready, 5)
            sp.dma_start(slot_table.rearrange("(p n) o -> p (n o)", p=P), empty[:, :]).then_inc(table_empty, 16)
            sp.wait_ge(kpe_done, 1)
            sp.dma_start(kpe_out, kpe[64:96, :]).then_inc(outs_stored, 16)
            sp.wait_ge(ckv_done, 1)
            sp.dma_start(ckv_out, kvz).then_inc(outs_stored, 16)
            sp.wait_ge(h_done, 5)
            sp.dma_start(conv_p_out, conv_tail[:, :, :]).then_inc(outs_stored, 16)
            sp.dma_start(conv_s_out, cdec[:, :, 1:CONV, :]).then_inc(outs_stored, 16)
            sp.dma_start(rec_p_out, rec_last[:, :]).then_inc(outs_stored, 16)
            sp.dma_start(rec_s_out, xc[:, :, SEQ:TOK]).then_inc(outs_stored, 16)
            sp.wait_ge(unit_done, N_UNITS)
            sp.wait_ge(ql_done, 1)
            sp.dma_start(arena_o[:, 0:O_LEN], w_out).then_inc(wo_landed, 16)
            sp.wait_ge(pv_done, NH // 2)
            sp.wait_ge(qq_done, 1)
            sp.dma_start(uv2, w_uv.rearrange("p (k n) -> p k n", k=KKV)).then_inc(uv2_landed, 16)
            for t in range(TT):
                sp.dma_start(x1[0:ROWS[t], t, :], x_tok[P * t:P * t + ROWS[t], :]).then_inc(xtok_landed, 16)
            sp.dma_start(lng, lns[0:2].partition_broadcast(P)).then_inc(ln1_landed, 16)
            sp.wait_ge(f_pe, 4)
            sp.dma_start(arena_s[:, S_WR:S_WR + 512], w_router).then_inc(wr_landed, 16)

            def expert(j, e):
                sp.dma_start(gu_w[j], w_gu[e].rearrange("o (k p) n -> p (o k) n", p=P)).then_inc(expert_landed[j], 16)
                sp.dma_start(dn_w[j], w_dn[e].rearrange("o (k p) n -> p (o k) n", p=P)).then_inc(expert_landed[j], 16)
            for j in range(3):
                expert(j, slice(j, j + 1))
            for n, t in enumerate([4, 0, 1, 2, 3]):
                sp.wait_ge(x1_done, n + 1)
                sp.dma_start(x1_rows[P * t:P * t + ROWS[t], :], x1[0:ROWS[t], t, :]).then_inc(x1_stored, 16)
            sp.wait_ge(o_done, 9)
            expert(3, slice(3, 4))
            sp.dma_start(lng, lns[2:4].partition_broadcast(P)).then_inc(ln2_landed, 16)
            sp.wait_ge(pos_ready, 1)
            n_rounds = sp.value_load(rounds[0:1, 0:1], min_val=1, max_val=MAXR)
            with sp.Fori(1, n_rounds * NGRP) as it:
                for j in range(GRP):
                    sp.wait_ge(dn_ps, (it - 1) * GRP + j + 1)
                    expert(j, bass.ds((it % NGRP) * GRP + j, 1))
            for j in range(GRP):
                sp.wait_ge(scattered[j], n_rounds * (NGRP * 16))
            for t in range(TT):
                b, n = t % 2, ROWS[t]
                if t >= 2:
                    sp.wait_ge(y_sum, t - 1)
                    landed(sp, y_stored[b], t // 2)
                sp.dma_start(y1[b][0:n, :], pair_rows[P * t:P * t + n, :]).then_inc(y_landed[b], 16)
                sp.dma_start(y2[b][0:n, :], pair_rows[HALF_ID + P * t:HALF_ID + P * t + n, :]).then_inc(y_landed[b], 16)
                if t >= 1:
                    sp.wait_ge(y_ready, t)
                    store_y(sp, t - 1)
            sp.wait_ge(y_ready, TT)
            store_y(sp, TT - 1)
            landed(sp, y_stored[0], 3)
            landed(sp, y_stored[1], 2)
            landed(sp, outs_stored, 6)

        @block.tensor
        def _(pe):
            mm = nc.tensor.matmul

            def unit(u, lhs, rhs, ks, rows=slice(0, P)):
                if u >= 4:
                    pe.wait_ge(evac[u % 4], u // 4)
                b = 2 * (u % 4)
                for k in range(ks):
                    if u == 0 and k % 2 == 0:
                        landed(pe, x_landed[k // 2])
                    for n in range(2):
                        last = mm(ps[rows, b + n, 0:HALF], lhs(k), rhs(k)[:, n * HALF:(n + 1) * HALF],
                                  start=(k == 0), stop=(k == ks - 1))
                last.then_inc(unit_done, 1)

            def project(u):
                c = CHUNK_OF[u]
                landed(pe, win_landed[LAND_OF[c]], LAND_OF.count(LAND_OF[c]))
                unit(u, lambda k: w_chunk[c][:, k, :], lambda k: xTv[:, k, :], KD)

            for u in range(U_RX, U_KPE):
                project(u)
            landed(pe, kpe_w_landed)
            unit(U_KPE, lambda k: w_kpev[:, k, :], lambda k: xTv[:, k, :], KD, slice(64, 128))
            for u in range(U_Q, U_Q + KQ):
                project(u)
            landed(pe, gates_landed)
            for g, u0 in enumerate((U_R, U_I)):
                for c in range(KR):
                    pe.wait_ge(conv_done, c + 1)
                    unit(u0 + c, lambda k: gw[:, g, c, :], lambda k: xc[:, c, :], 1)
            pe.wait_ge(ones_ready, 1)
            pe.wait_ge(squares, 2)
            unit(U_NQ, lambda k: ones[:, :], lambda k: sq0[:, k, :], KQ)
            unit(U_NKV, lambda k: ones[:, :], lambda k: sq0[:, KQ + k, :], KKV)
            for u in range(U_G, U_G + KR):
                project(u)
            pe.wait_ge(wuq_scaled, 1)
            for h in range(NH):
                unit(U_UQ + h, lambda k: uq[:, k, h, :], lambda k: qz[:, k, :], KQ)
            landed(pe, ukv_landed, 3)
            pe.wait_ge(ckv_done, 1)
            for n in range(4):
                u = U_UK + n
                pe.wait_ge(evac[u % 4], u // 4)
                for k in range(KKV):
                    last = mm(ps[:, 2 * (u % 4), :], uk[:, k, n * P:(n + 1) * P], kvz[:, k, 0:SEQ],
                              start=(k == 0), stop=(k == KKV - 1))
                last.then_inc(unit_done, 1)
            for n in range(4):
                u = U_V + n
                pe.wait_ge(evac[u % 4], u // 4)
                for k in range(KKV):
                    last = mm(ps[:, 2 * (u % 4), :], kvz[:, k, n * P:(n + 1) * P], uv[:, k, :],
                              start=(k == 0), stop=(k == KKV - 1))
                last.then_inc(unit_done, 1)
            for n in range(4):
                pe.wait_ge(evac[n], N_UNITS // 4)

            pe.wait_ge(qrope_done, NH)
            for hi in range(2):
                for g in range(4):
                    h = 4 * hi + g
                    last = mm(ps[32 * g:32 * g + 32, 6, hi * KVL:(hi + 1) * KVL], qh[0:NOPE, h, TOK - 32:TOK],
                              ukT[0:NOPE, h, :], start=True, stop=True)
            last.then_inc(ql_done, 1)
            pe.wait_ge(ql_evac, 1)
            pe.wait_ge(const_ready, 5)
            for n in range(4):
                last = nc.tensor.transpose(ps[:, 7, n * P:(n + 1) * P], qlt[:, n * P:(n + 1) * P], ident[:, :])
            last.then_inc(qlT_done, 1)

            pe.wait_ge(khrope_done, 1)

            def scores(h, i):
                n = 4 * h + i
                if n >= 3:
                    pe.wait_ge(exp_done, n - 2)
                b = n % 3
                mm(ps[:, b, 0:P * (i + 1)], qh[0:96, h, i * P:(i + 1) * P], kh[0:96, h, 0:P * (i + 1)],
                   start=True, stop=False)
                mm(ps[:, b, P * i:P * (i + 1)], identb[:, :], maskb[:, :], start=False, stop=True,
                   ).then_inc(s_done, 1)

            def turn(h, j):
                n = 4 * h + j
                pe.wait_ge(p_done, 4 * h + 4)
                if n >= 3:
                    m = n - 3
                    pe.wait_ge(pt_act if m % 4 < 2 else pt_dve, 2 * (m // 4) + m % 2 + 1)
                for i in range(j, 4):
                    last = nc.tensor.transpose(ps[:, 3 + n % 3, (i - j) * P:(i - j + 1) * P],
                                               Pb[h % 2][:, OFF[i] + j * P:OFF[i] + (j + 1) * P], ident[:, :])
                last.then_inc(t_done, 1)

            def values(hp):
                pe.wait_ge(pt_act, 4 * hp + 4)
                pe.wait_ge(pt_dve, 4 * hp + 4)
                if hp == 1:
                    pe.wait_ge(qq_done, 1)
                if hp >= 2:
                    pe.wait_ge(att_done, hp - 1)
                for j in range(4):
                    for e in range(2):
                        h = 2 * hp + e
                        last = mm(ps[64 * e:64 * e + 64, 6 + hp % 2, j * P:SEQ], v[:, j, h * VH:(h + 1) * VH],
                                  PTb[e][:, POFF[j]:POFF[j] + (4 - j) * P], start=(j == 0), stop=(j == 3))
                last.then_inc(pv_done, 1)

            for i in range(4):
                scores(0, i)
            for h in range(NH):
                for i in range(4):
                    if h + 1 < NH:
                        scores(h + 1, i)
                    turn(h, i)
                    if i == 0 and h % 2 == 0 and h > 0:
                        values(h // 2 - 1)
            values(NH // 2 - 1)

            pe.wait_ge(att_done, NH // 2)
            pe.wait_ge(exp_done, 4 * NH)
            pe.wait_ge(pt_act, 2 * NH)
            pe.wait_ge(pt_dve, 2 * NH)

            def turn_cache(s, b2, fetched):
                landed(pe, cache_landed[b2], 2 * fetched)
                for b in range(9):
                    pe.wait_ge(kt_evac[b % 3], 3 * s + b // 3)
                    for j in range(4):
                        i, kc = b // 2, b % 2
                        src = crope[b2][:, j, :] if b == 8 else cache[b2][:, 4 * i + j, kc * P:(kc + 1) * P]
                        last = nc.tensor.transpose(ps[:, b % 3, j * P:(j + 1) * P], src, ident[:, :])
                    last.then_inc(kt_done, 1)

            def cache_scores(s, b2):
                for n in range(3):
                    pe.wait_ge(kt_evac[n], 3 * s + 3)
                pe.wait_ge(qs_done, s + 1)
                if not (isinstance(s, int) and s < 2):
                    pe.wait_ge(dexp_done, s - 1)
                for kc in range(KKV):
                    for i in range(4):
                        mm(ps[32 * i:32 * i + 32, 3 + b2, :], qs[:, b2, 32 * kc:32 * kc + 32],
                           KT[:, kc, i * 512:(i + 1) * 512], start=(kc == 0), stop=False, skip_group_check=True)
                for j in range(4):
                    for i in range(4):
                        last = mm(ps[32 * i:32 * i + 32, 3 + b2, j * P:(j + 1) * P],
                                  qs[:, b2, 64 + 32 * j:96 + 32 * j], ropeT[:, i * P:(i + 1) * P],
                                  start=False, stop=(j == 3), skip_group_check=True)
                last.then_inc(sc_done, 1)

            def cache_values(s, b2):
                pe.wait_ge(dexp_done, s + 1)
                pe.wait_ge(dpt_evac, s)
                for j in range(4):
                    last = nc.tensor.transpose(ps[:, 5, j * P:(j + 1) * P], dP[:, j * P:(j + 1) * P], ident[:, :])
                last.then_inc(dpt_done, 1)
                pe.wait_ge(dpt_evac, s + 1)
                pe.wait_ge(op_evac, s)
                for j in range(4):
                    for i in range(4):
                        last = mm(ps[32 * i:32 * i + 32, 6, 0:KVL], dPT[:, j * P + 32 * i:j * P + 32 * i + 32],
                                  cache[b2][:, 4 * i + j, :], start=(j == 0), stop=(j == 3))
                last.then_inc(op_done, 1)

            turn_cache(0, 0, 1)
            cache_scores(0, 0)
            with pe.Fori(0, 3) as it:
                for d in (1, 2):
                    s = it * 2 + d
                    turn_cache(s, d % 2, it + d)
                    cache_values(s - 1, (d - 1) % 2)
                    cache_scores(s, d % 2)
            turn_cache(7, 1, 4)
            cache_values(6, 0)
            cache_scores(7, 1)
            cache_values(7, 1)

            pe.wait_ge(dexp_done, DEC)
            nc.tensor.transpose(ps[0:DEC, 0, 0:P], mx[:, :], ident[:, :])
            nc.tensor.transpose(ps[0:DEC, 0, P:2 * P], ls[:, :], ident[:, :])
            for kc in range(KKV):
                mm(ps[0:DEC, 1, 0:64], kvz[:, kc, SEQ:TOK], qq[:, :, 32 * kc:32 * kc + NH], start=(kc == 0), stop=False)
            mm(ps[0:DEC, 1, 0:64], kpn[:, :], qq[0:32, :, 64:64 + NH], start=False, stop=True).then_inc(f_pe, 1)
            pe.wait_ge(f_dve, 1)
            nc.tensor.transpose(ps[:, 2, 0:DEC], fin[:, 0:P], ident[0:DEC, 0:DEC])
            mm(ps[:, 2, 64:128], ones[0:DEC, :], fin[:, 384:448], start=True, stop=True).then_inc(f_pe, 1)
            pe.wait_ge(f_dve, 2)
            for g in range(4):
                last = mm(ps[32 * g:32 * g + 32, 3, :], sel[:, :], op[:, 2 * g:2 * g + 2, :].rearrange("p a b -> p (a b)"),
                          start=True, stop=True)
            last.then_inc(f_pe, 1)
            pe.wait_ge(f_act, 3)
            for n in range(4):
                last = nc.tensor.transpose(ps[:, 4, n * P:(n + 1) * P], osum[:, n * P:(n + 1) * P], ident[:, :])
            last.then_inc(f_pe, 1)
            landed(pe, uv2_landed)
            pe.wait_ge(f_dve, 3)
            for h in range(NH):
                for kc in range(KKV):
                    last = mm(ps[64 * (h % 2):64 * (h % 2) + 64, 5, 8 * (h // 2):8 * (h // 2) + 8],
                              uv2[:, kc, h * VH:(h + 1) * VH], oT[:, kc, h, :], start=(kc == 0), stop=(kc == KKV - 1))
            last.then_inc(f_pe, 1)

            pe.wait_ge(sq_done, 3)
            for k in range(KR):
                for g in range(4):
                    w, half = g // 2, g % 2
                    last = mm(ps[32 * g:32 * g + 32, 7, 0:WIN], ones[:, 0:32],
                              sq[:, KR * w + k, SHIFT * half:SHIFT * half + WIN], start=(k == 0), stop=(k == KR - 1))
            last.then_inc(d_pe, 1)
            pe.wait_ge(d_act, 1)
            nc.tensor.transpose(ps[:, 6, 0:P], ss[:, 0:P], ident[:, :])
            nc.tensor.transpose(ps[:, 6, P:2 * P], ss[:, P:2 * P], ident[:, :])
            nc.tensor.transpose(ps[0:DEC, 6, 2 * P:3 * P], ss[:, 2 * P:WIN], ident[:, :]).then_inc(d_pe, 1)

            pe.wait_ge(wo_scaled, 1)
            for k in range(KR):
                for g in range(4):
                    w, n = g // 2, g % 2
                    act_in = (attT if w == 0 else recT)[:, k, SEQ:TOK]
                    last = mm(ps[32 * g:32 * g + DEC, 0, :], act_in, wo[:, KR * w + k, n * 512:(n + 1) * 512],
                              start=(k == 0), stop=(k == KR - 1))
            last.then_inc(o_done, 1)

            def turn_x1(m):
                t = [4, 0, 1, 2, 3][m]
                pe.wait_ge(x1_done, m + 1)
                if m == 0:
                    pe.wait_ge(d_act, 2)
                if m > 0:
                    pe.wait_ge(x1T_act, m)
                    pe.wait_ge(x1T_dve, m)
                n = ROWS[t]
                for k in range(KD):
                    last = nc.tensor.transpose(ps[:, 6 + k // 4, (k % 4) * P:(k % 4) * P + n],
                                               x1[0:n, t, k * P:(k + 1) * P], ident[0:n, 0:n])
                last.then_inc(x1T_ps, 1)

            for t in range(4):
                for n in range(2):
                    m = 1 + 2 * t + n
                    b = 2 * (m % 3)
                    if m == 3:
                        pe.wait_ge(d_act, 3)
                    if m > 3:
                        pe.wait_ge(oA_done, m - 3)
                        pe.wait_ge(oR_done, m - 3)
                    for w in range(2):
                        for k in range(KR):
                            last = mm(ps[:, b + w, :], (attT if w == 0 else recT)[:, k, t * P:(t + 1) * P],
                                      wo[:, KR * w + k, n * 512:(n + 1) * 512], start=(k == 0), stop=(k == KR - 1))
                    last.then_inc(o_done, 1)
                if t == 1:
                    turn_x1(0)
                if t >= 2:
                    turn_x1(t - 1)
            turn_x1(3)
            turn_x1(4)

            landed(pe, wr_landed)
            pe.wait_ge(x1T_act, TT)
            pe.wait_ge(x1T_dve, TT)
            pe.wait_ge(oA_done, 8)
            pe.wait_ge(oR_done, 8)
            for k in range(KD):
                for half in range(2):
                    last = mm(ps[64 * half:64 * half + 64, 0, 0:WIN], wr[:, k, :],
                              x1T[:, k, SHIFT * half:SHIFT * half + WIN], start=(k == 0), stop=(k == KD - 1))
            last.then_inc(r_pe, 1)
            pe.wait_ge(r_act, 1)
            nc.tensor.transpose(ps[:, 1, 0:P], rt[:, 0:P], ident[:, :])
            nc.tensor.transpose(ps[:, 1, P:2 * P], rt[:, P:2 * P], ident[:, :])
            nc.tensor.transpose(ps[0:DEC, 1, 2 * P:3 * P], rt[:, 2 * P:WIN], ident[:, :]).then_inc(r_pe, 1)
            pe.wait_ge(r_dve, 1)
            for t in range(TT):
                for q in range(t + 1):
                    mm(ps[:, 2, t * NE:(t + 1) * NE], (trib if q == t else onesb)[:, :], ohb[:, q, :],
                       start=(q == 0), stop=(q == t))
            for q in range(TT):
                last = mm(ps[:, 2, TT * NE:(TT + 1) * NE], onesb[:, :], ohb[:, q, :], start=(q == 0), stop=(q == TT - 1))
            last.then_inc(r_pe, 1)

            pe.wait_ge(pos_ready, 1)
            n_rounds = pe.value_load(rounds[0:1, 0:1], min_val=1, max_val=MAXR)
            turn = [ctx.enter_context(pe.register(f"pe_turn{j}")) for j in range(GRP + 1)]
            tokens_in = ctx.enter_context(pe.register("pe_tokens_in"))
            with pe.Fori(0, n_rounds * NGRP) as it:
                for j in range(GRP + 1):
                    pe.reg_mov(turn[j], it * GRP + j)
                pe.reg_mov(tokens_in, it * 16 + 16)

                def turn_tokens(j):
                    pe.wait_ge(pos_ready, 1)
                    pe.wait_ge(gathered[j], tokens_in)
                    pe.wait_ge(xt_sb, turn[max(j - 1, 0)])
                    for k in range(KD):
                        last = nc.tensor.transpose(ps[:, j % 2, k * CAP:(k + 1) * CAP],
                                                   xg[j][0:CAP, k * P:(k + 1) * P], ident[0:CAP, 0:CAP])
                    last.then_inc(xt_ps, 1)
                turn_tokens(0)
                for j in range(GRP):
                    b = j % 2
                    before = turn[max(j - 1, 0)]
                    pe.wait_ge(xt_sb, turn[j + 1])
                    landed(pe, expert_landed[j], 2 * (it + 1))
                    pe.wait_ge(h_ready, before)
                    for k in range(KD):
                        for n in range(2):
                            last = mm(ps[64 * n:64 * n + 64, 2 + b, 0:DE], xgT[b][:, k, :],
                                      gu_w[j][:, k, n * DE:(n + 1) * DE], start=(k == 0), stop=(k == KD - 1))
                    last.then_inc(gu_ps, 1)
                    if j + 1 < GRP:
                        turn_tokens(j + 1)
                    pe.wait_ge(pos_ready, 1)
                    pe.wait_ge(h_ready, turn[j + 1])
                    pe.wait_ge(ht_sb, turn[j])
                    for f in range(2):
                        last = nc.tensor.transpose(ps[:, 4, f * CAP:(f + 1) * CAP], hx[b][0:CAP, f * P:(f + 1) * P],
                                                   ident[0:CAP, 0:CAP])
                    last.then_inc(ht_ps, 1)
                    pe.wait_ge(ht_sb, turn[j + 1])
                    pe.wait_ge(ya_done, before)
                    pe.wait_ge(yd_done, before)
                    for f in range(2):
                        for n in range(2):
                            last = mm(ps[64 * n:64 * n + 64, 5 + b, :], hT[b][:, f, :],
                                      dn_w[j][:, f, n * 512:(n + 1) * 512], start=(f == 0), stop=(f == 1))
                    last.then_inc(dn_ps, 1)

        @block.scalar
        def _(act):
            steps = [0]

            def step(ins):
                steps[0] += 1
                ins.then_inc(act_step, 1)

            def settle():
                act.wait_ge(act_step, steps[0])

            fn = nc.scalar.activation
            act.dma_start(vec[:, :], vecs).then_inc(params_landed, 16)
            act.dma_start(cdec[:, :, 0:CONV - 1, :], conv_st).then_inc(params_landed, 16)
            act.dma_start(rst[:, :, :], rec_st).then_inc(params_landed, 16)
            act.dma_start(cs[64:128, :], cs_tab).then_inc(cs_landed, 16)
            act.dma_start(pages[:, :], page_rep).then_inc(pages_landed, 16)
            act.dma_start(lane_sb[:, :], lane).then_inc(pages_landed, 16)
            act.dma_start(id_sb[:, :], ids).then_inc(ids_landed, 16)
            act.dma_start(eoff_sb[:, :], eoff.partition_broadcast(P)).then_inc(ids_landed, 16)
            act.dma_start(rbias[:, :], r_bias.partition_broadcast(P)).then_inc(ids_landed, 16)
            act.wait_ge(lam_ready, 1)
            fn(lam[:, 1, :], lam[:, 0, :], ACT.Exp).then_inc(sp_exp, 1)
            for c in range(KR):
                u = U_RX + c
                b = 2 * (u % 4)
                act.wait_ge(unit_done, u + 1)
                nc.scalar.copy(xp[:, c, 3:3 + HALF], ps[:, b, 0:HALF])
                nc.scalar.copy(xp[:, c, 3 + HALF:3 + SEQ], ps[:, b + 1, 0:SEQ - HALF])
                nc.scalar.copy(cdec[:, c, CONV - 1, :], ps[:, b + 1, SEQ - HALF:HALF]).then_inc(evac[u % 4], 1)
            for k in range(KKV):
                u = U_KV + k
                act.wait_ge(unit_done, u + 1)
                nc.scalar.copy(kvz[:, k, :].rearrange("p (a b) -> p a b", a=2), pair(u)).then_inc(evac[u % 4], 1)
            for k in range(KQ):
                u = U_Q + k
                act.wait_ge(unit_done, u + 1)
                nc.scalar.copy(qz[:, k, :].rearrange("p (a b) -> p a b", a=2), pair(u)).then_inc(evac[u % 4], 1)
            act.wait_ge(lam_ready, 2)
            for c in range(KR):
                u = U_R + c
                act.wait_ge(unit_done, u + 1)
                fn(tr[:, c, :].rearrange("p (a b) -> p a b", a=2), pair(u), ACT.Tanh, bias=bh[:, 0, c:c + 1],
                   scale=0.5).then_inc(evac[u % 4], 1)
            for c in range(KR):
                u = U_I + c
                act.wait_ge(unit_done, u + 1)
                if c == 3:
                    act.wait_ge(ix_done, 1)
                fn(tmp[:, c % 3, :].rearrange("p (a b) -> p a b", a=2), pair(u), ACT.Tanh, bias=bh[:, 1, c:c + 1],
                   scale=0.5).then_inc(evac[u % 4], 1)
            act.wait_ge(conv_done, KR)
            for c in range(KR):
                act.wait_ge(evac[(U_R + c) % 4], (U_R + c) // 4 + 1)
                fn(xp[:, c, :], tr[:, c, :], ACT.Exp, bias=nsp[:, 0, c:c + 1], scale=nsp[:, 0, c:c + 1]).then_inc(a_done, 1)
                act.wait_ge(a_done, c + 1)
                fn(tr[:, c, :], tr[:, c, :], ACT.Tanh, bias=nsp[:, 1, c:c + 1], scale=nsp[:, 1, c:c + 1]).then_inc(th_done, 1)
            for n, (u, dst, width) in enumerate(((U_NQ, rq, QL), (U_NKV, rkv, KVL))):
                act.wait_ge(unit_done, u + 1)
                if n == 0:
                    act.wait_ge(kpe_done, 1)
                fn(dst.rearrange("p (a b) -> p a b", a=2), pair(u), ACT.Sqrt, bias=eps[:, 0:1],
                   scale=1.0 / width).then_inc(evac[u % 4], 1)
            for c in range(KR):
                act.wait_ge(w_done, c + 1)
                fn(tr[:, c, :], tr[:, c, :], ACT.Sqrt, scale=0.25).then_inc(root_w, 1)
            for c in range(KR):
                u = U_G + c
                act.wait_ge(unit_done, u + 1)
                fn(recT[:, c, :].rearrange("p (a b) -> p a b", a=2), pair(u), ACT.Gelu_apprx_tanh).then_inc(evac[u % 4], 1)
            for n in range(4):
                u = U_UK + n
                act.wait_ge(unit_done, u + 1)
                nc.scalar.copy(kh[0:64, 2 * n, :], ps[0:64, 2 * (u % 4), :])
                nc.scalar.copy(kh[0:64, 2 * n + 1, :], ps[64:128, 2 * (u % 4), :]).then_inc(evac[u % 4], 1)
            act.wait_ge(ql_done, 1)
            nc.scalar.copy(qlt, ps[:, 6, :]).then_inc(ql_evac, 1)

            def prob(h, i):
                n = 4 * h + i
                act.wait_ge(nm_done, n + 1)
                if h >= 2:
                    act.wait_ge(t_done, 4 * (h - 1))
                if n >= 2:
                    act.wait_ge(p_done, n - 1)
                fn(Pb[h % 2][:, OFF[i]:OFF[i] + P * (i + 1)], ps[:, n % 3, 0:P * (i + 1)], ACT.Exp,
                   bias=stat[:, n % 2, 1:2], scale=SM, accum_out=stat[:, n % 2, 2:3]).then_inc(exp_done, 1)

            def turned(h, j):
                n = 4 * h + j
                act.wait_ge(t_done, n + 1)
                if h >= 2:
                    act.wait_ge(pv_done, h // 2)
                nc.scalar.copy(PTb[h % 2][:, POFF[j]:POFF[j] + (4 - j) * P], ps[:, 3 + n % 3, 0:(4 - j) * P]).then_inc(pt_act, 1)

            def head_out(hp):
                act.wait_ge(pv_done, hp + 1)
                nc.scalar.copy(attT[:, hp, 0:SEQ], ps[:, 6 + hp % 2, :]).then_inc(att_done, 1)

            for i in range(4):
                prob(0, i)
            for h in range(NH):
                for i in range(4):
                    if h + 1 < NH:
                        prob(h + 1, i)
                    if i < 2:
                        turned(h, i)
                    if i == 1 and h % 2 == 0 and h > 0:
                        head_out(h // 2 - 1)
            head_out(NH // 2 - 1)

            def cache_out(s):
                act.wait_ge(sc_done, s)
                for b in range(0, 9, 2):
                    act.wait_ge(kt_done, 9 * s + b + 1)
                    dst = ropeT if b == 8 else KT[:, 0, (b // 2) * 512:(b // 2 + 1) * 512]
                    nc.scalar.copy(dst, ps[:, b % 3, :]).then_inc(kt_evac[b % 3], 1)

            def cache_prob(s, s_col, b2):
                act.wait_ge(dmx_done, s + 1)
                act.wait_ge(dpt_done, s)
                fn(dP, ps[:, 3 + b2, :], ACT.Exp, bias=nmd[:, b2:b2 + 1], scale=SM, accum_out=ls[:, s_col]).then_inc(dexp_done, 1)

            def part_out(s, s_col):
                act.wait_ge(op_done, s + 1)
                nc.scalar.copy(op[:, s_col, :], ps[:, 6, 0:KVL]).then_inc(op_evac, 1)

            def col(s):
                return slice(s, s + 1) if isinstance(s, int) else bass.ds(s, 1)

            cache_out(0)
            cache_prob(0, col(0), 0)
            with act.Fori(0, 3) as it:
                for d in (1, 2):
                    s = it * 2 + d
                    cache_out(s)
                    part_out(s - 1, col(s - 1))
                    cache_prob(s, col(s), d % 2)
            cache_out(7)
            part_out(6, col(6))
            cache_prob(7, col(7), 1)
            part_out(7, col(7))
            act.wait_ge(f_pe, 1)
            nc.scalar.copy(fin[:, 0:256], ps[0:DEC, 0, 0:256]).then_inc(f_act, 1)
            fn(sq[:, KR:KD, :], recT, ACT.Square).then_inc(sq_done, 1)
            fn(sq[:, 0:KR, 0:SEQ], attT[:, :, 0:SEQ], ACT.Square).then_inc(sq_done, 1)
            act.wait_ge(diff_ready, 1)
            for n in range(2):
                a = fin[:, 448 + 0:456] if n else fin[:, 256:384].rearrange("p (i h) -> p i h", i=4)[:, :, 0:NH]
                last = fn(a, a, ACT.Exp, scale=SM)
            last.then_inc(f_act, 1)
            act.wait_ge(f_pe, 3)
            nc.scalar.copy(osum, ps[:, 3, :]).then_inc(f_act, 1)
            act.wait_ge(f_pe, 5)
            for hp in range(4):
                last = nc.scalar.copy(attT[:, hp, SEQ:TOK], ps[:, 5, 8 * hp:8 * hp + 8])
            last.then_inc(f_act, 1)
            act.wait_ge(f_act, 4)
            fn(sq[:, 0:KR, SEQ:TOK], attT[:, :, SEQ:TOK], ACT.Square).then_inc(sq_done, 1)

            act.wait_ge(d_pe, 1)
            nc.scalar.copy(ss, ps[:, 7, 0:WIN]).then_inc(d_act, 1)
            act.wait_ge(d_pe, 2)
            for tt in range(2):
                fn(rinv[:, :, :, tt], ps[:, 6, tt * P:(tt + 1) * P].rearrange("p (w h x) -> p w h x", w=2, h=2)[:, :, :, 0],
                   ACT.Sqrt, bias=eps[:, 0:1], scale=1.0 / REC)
            fn(rinv4[:, :], ps[0:DEC, 6, 2 * P:3 * P].rearrange("p (w h x) -> p w h x", w=2, h=2)[:, :, 1, 0],
               ACT.Sqrt, bias=eps[0:DEC, 0:1], scale=1.0 / REC).then_inc(d_act, 1)
            act.wait_ge(o_done, 1)
            for g in range(4):
                last = nc.scalar.copy(tb[g // 2][0:DEC, (g % 2) * 512:(g % 2 + 1) * 512], ps[32 * g:32 * g + DEC, 0, :])
            last.then_inc(d_act, 1)

            def ln_act(n, rows, root_sem, norm_sem, var_sem, x, out):
                act.wait_ge(var_sem, 2 * n + 1)
                fn(mv[0:rows, 2:3], mv[0:rows, 1:2], ACT.Sqrt, bias=eps[0:rows, 1:2]).then_inc(root_sem, 1)
                act.wait_ge(var_sem, 2 * n + 2)
                fn(out, x, ACT.Identity, bias=mv[0:rows, 3:4], scale=mv[0:rows, 2:3]).then_inc(norm_sem, 1)

            def x1T_out(m):
                t = [4, 0, 1, 2, 3][m]
                act.wait_ge(x1T_ps, m + 1)
                nc.scalar.copy(x1T[:, 0:4, P * t:P * t + ROWS[t]],
                               ps[:, 6, :].rearrange("p (k n) -> p k n", k=4)[:, :, 0:ROWS[t]]).then_inc(x1T_act, 1)

            ln_act(0, DEC, ln_root, ln_norm, ln_var, x1[0:DEC, 4, :], x1[0:DEC, 4, :])
            for t in range(4):
                for n in range(2):
                    m = 1 + 2 * t + n
                    act.wait_ge(o_done, m + 1)
                    act.wait_ge(d_dve, 1)
                    act.wait_ge(x1_sum, t if t else 1)
                    fn(tb[t % 2][:, n * 512:(n + 1) * 512], ps[:, 2 * (m % 3), :], ACT.Identity,
                       scale=rinv[:, 0, t // 2, t % 2:t % 2 + 1]).then_inc(oA_done, 1)
                ln_act(t + 1, P, ln_root, ln_norm, ln_var, x1[:, t, :], x1[:, t, :])
                if t == 1:
                    x1T_out(0)
                if t >= 2:
                    x1T_out(t - 1)
            x1T_out(3)
            x1T_out(4)
            act.wait_ge(r_pe, 1)
            nc.scalar.copy(rt, ps[:, 0, 0:WIN]).then_inc(r_act, 1)
            act.wait_ge(r_dve, 2)
            fn(rt_t[:, :, 0:NG], rt_t[:, :, 0:NG], ACT.Exp).then_inc(r_act, 1)
            act.wait_ge(r_dve, 3)
            fn(rs[:, 6:8, :], rs[:, 6:8, :], ACT.Exp).then_inc(r_act, 1)

            act.wait_ge(pos_ready, 1)
            n_rounds = act.value_load(rounds[0:1, 0:1], min_val=1, max_val=MAXR)
            with act.Fori(0, n_rounds * NGRP) as it:
                for j in range(GRP):
                    t = it * GRP + j
                    b = j % 2
                    act.wait_ge(gu_ps, t + 1)
                    act.wait_ge(h_ready, it * GRP + max(j - 1, 0))
                    fn(sg[b][0:CAP, :], ps[0:CAP, 2 + b, 0:DE], ACT.Silu).then_inc(silu_done, 1)
                    act.wait_ge(dn_ps, t + 1)
                    landed(act, scattered[j], it)
                    nc.scalar.copy(yb[j][0:CAP, 0:512], ps[0:CAP, 5 + b, :]).then_inc(ya_done, 1)

            for t in range(TT):
                b, n = t % 2, ROWS[t]
                landed(act, y_landed[b], 2 * (t // 2 + 1))
                fn(y1[b][0:n, :], y1[b][0:n, :], ACT.Identity, scale=rs[0:n, 10, t:t + 1]).then_inc(g1_done, 1)
                ln_act(t, n, root2, n2_done, v2_done, x1[0:n, t, :], x1[0:n, t, :])

        @block.vector
        def _(dve):
            steps = [0]

            def step(ins):
                steps[0] += 1
                ins.then_inc(dve_step, 1)

            def settle():
                dve.wait_ge(dve_step, steps[0])

            def link(ins):
                step(ins)
                settle()

            V = nc.vector
            tt, ts, stt = V.tensor_tensor, V.tensor_scalar, V.scalar_tensor_tensor
            V.memset(ones[:, :], 1.0).then_inc(ones_ready, 1)
            step(V.memset(eps[:, 0:1], RMS_EPS))
            step(V.memset(eps[:, 1:2], LN_EPS))
            step(V.memset(xp[:, :, 0:3], 0.0))
            landed(dve, params_landed, 3)
            lam_in = vec[:, V_LAM:V_LAM + KR]
            link(ts(lam[:, 0, :], lam_in, -1.0, None, ALU.mult))
            link(tt(lam[:, 2, :], lam[:, 0, :], lam_in, ALU.max))
            ts(lam[:, 0, :], lam[:, 2, :], -1.0, None, ALU.mult).then_inc(lam_ready, 1)
            dve.wait_ge(sp_exp, 1)
            link(ts(lam[:, 2, :], lam[:, 1, :], 2.0, None, ALU.add))
            link(V.reciprocal(lam[:, 2, :], lam[:, 2, :]))
            link(tt(lam[:, 2, :], lam[:, 1, :], lam[:, 2, :], ALU.mult))
            link(tt(lam[:, 3, :], lam[:, 2, :], lam[:, 2, :], ALU.mult))
            link(V.memset(lam[:, 4, :], 1.0 / 17))
            for n in range(15, 0, -2):
                link(tt(lam[:, 4, :], lam[:, 4, :], lam[:, 3, :], ALU.mult))
                link(ts(lam[:, 4, :], lam[:, 4, :], 1.0 / n, None, ALU.add))
            link(tt(lam[:, 4, :], lam[:, 4, :], lam[:, 2, :], ALU.mult))
            link(ts(lam[:, 5, :], lam_in, -1.0, 0.0, ALU.mult, ALU.max))
            link(stt(lam[:, 4, :], lam[:, 4, :], 2.0, lam[:, 5, :], ALU.mult, ALU.add))
            step(ts(nsp[:, 0, :], lam[:, 4, :], -4.0, None, ALU.mult))
            step(ts(nsp[:, 1, :], lam[:, 4, :], 4.0, None, ALU.mult))
            step(ts(bh[:, 0, :], vec[:, V_BR:V_BR + KR], 0.5, None, ALU.mult))
            ts(bh[:, 1, :], vec[:, V_BI:V_BI + KR], 0.5, None, ALU.mult).then_inc(lam_ready, 1)
            landed(dve, pages_landed, 2)
            link(ts(pages[:, :], pages[:, :], 8, None, ALU.mult))
            tt(pages[:, :], pages[:, :], lane_sb[:, 0:1].broadcast_to([P, DEC]), ALU.add).then_inc(cidx_ready, 1)
            settle()
            for c in range(KR):
                u = U_RX + c
                dve.wait_ge(evac[u % 4], u // 4 + 1)
                step(V.tensor_copy(conv_tail[:, c, :], xp[:, c, SEQ:SEQ + 3]))
                w = vec[:, V_CW + CONV * c:V_CW + CONV * (c + 1)]
                step(ts(xc[:, c, 0:SEQ], xp[:, c, 0:SEQ], w[:, 0:1], vec[:, V_CB + c:V_CB + c + 1], ALU.mult, ALU.add))
                step(ts(xc[:, c, SEQ:TOK], cdec[:, c, 0, :], w[:, 0:1], vec[:, V_CB + c:V_CB + c + 1], ALU.mult, ALU.add))
                for k in range(1, CONV):
                    settle()
                    step(stt(xc[:, c, 0:SEQ], xp[:, c, k:k + SEQ], w[:, k:k + 1], xc[:, c, 0:SEQ], ALU.mult, ALU.add))
                    last = stt(xc[:, c, SEQ:TOK], cdec[:, c, k, :], w[:, k:k + 1], xc[:, c, SEQ:TOK], ALU.mult, ALU.add)
                    if k + 1 < CONV:
                        step(last)
                last.then_inc(conv_done, 1)
            landed(dve, cs_landed)
            dve.wait_ge(unit_done, U_KPE + 1)
            two = lambda a: a.rearrange("p (a b) -> p a b", a=2)
            b = 2 * (U_KPE % 4)
            step(tt(two(rq[64:96, :]), ps[96:128, b:b + 2, 0:HALF], two(cs[96:128, :]), ALU.mult))
            tt(two(kpe[64:96, :]), ps[64:96, b:b + 2, 0:HALF], two(cs[64:96, :]), ALU.mult).then_inc(evac[U_KPE % 4], 1)
            settle()
            dve.wait_ge(evac[U_KPE % 4], U_KPE // 4 + 1)
            tt(kpe[64:96, :], kpe[64:96, :], rq[64:96, :], ALU.add).then_inc(kpe_done, 1)
            for c in range(KR):
                u = U_I + c
                dve.wait_ge(evac[u % 4], u // 4 + 1)
                stt(xc[:, c, :], tmp[:, c % 3, :], 1.0, xc[:, c, :], ALU.add, ALU.mult).then_inc(ix_done, 1)
            for c in range(KR):
                dve.wait_ge(th_done, c + 1)
                dve.wait_ge(a2_done, c + 1)
                stt(tr[:, c, :], tmp[:, c % 3, :], 1.0, tr[:, c, :], ALU.add, ALU.mult).then_inc(w_done, 1)
            dve.wait_ge(evac[U_NQ % 4], U_NQ // 4 + 1)
            link(V.reciprocal(rq, rq))
            tt(rq[64:128, :], rq[64:128, :], cs[64:128, :], ALU.mult).then_inc(rq_done, 1)
            dve.wait_ge(evac[U_NKV % 4], U_NKV // 4 + 1)
            link(V.reciprocal(rkv, rkv))
            step(stt(kvz[:, 0, :], kvz[:, 0, :], vec[:, V_KVG:V_KVG + 1], rkv, ALU.mult, ALU.mult))
            stt(kvz[:, 1, :], kvz[:, 1, :], vec[:, V_KVG + 1:V_KVG + 2], rkv, ALU.mult, ALU.mult).then_inc(ckv_done, 1)
            for c in range(KR):
                dve.wait_ge(root_w, c + 1)
                dve.wait_ge(ix_done, c + 1)
                link(tt(xc[:, c, :], tr[:, c, :], xc[:, c, :], ALU.mult))
                V.tensor_tensor_scan(xc[:, c, 0:SEQ], xp[:, c, 0:SEQ], xc[:, c, 0:SEQ], 0.0, ALU.mult,
                                     ALU.add).then_inc(h_done, 1)
            dve.wait_ge(h_done, KR)
            step(V.tensor_copy(rec_last[:, :], xc[:, :, SEQ - 1]))
            link(tt(rst[:, :, :], xp[:, :, SEQ:TOK], rst[:, :, :], ALU.mult))
            tt(xc[:, :, SEQ:TOK], xc[:, :, SEQ:TOK], rst[:, :, :], ALU.add).then_inc(h_done, 1)
            dve.wait_ge(rq_done, 1)
            for h in range(NH):
                u = U_UQ + h
                b = 2 * (u % 4)
                dve.wait_ge(unit_done, u + 1)
                if h >= 2:
                    dve.wait_ge(qrope_done, h - 1)
                step(tt(two(qh[0:64, h, :]), ps[0:64, b:b + 2, 0:HALF], two(rq[0:64, :]), ALU.mult))
                step(tt(two(tmp[64:96, h % 2, :]), ps[96:128, b:b + 2, 0:HALF], two(rq[96:128, :]), ALU.mult))
                tt(two(qh[64:96, h, :]), ps[64:96, b:b + 2, 0:HALF], two(rq[64:96, :]), ALU.mult).then_inc(evac[u % 4], 1)
            for n in range(4):
                u = U_V + n
                dve.wait_ge(unit_done, u + 1)
                V.tensor_copy(v[:, n, :], ps[:, 2 * (u % 4), :]).then_inc(evac[u % 4], 1)
            dve.wait_ge(rec_done, KR)
            landed(dve, outs_stored, 6)
            step(V.memset(qq[:, :, :], 0.0))
            dve.wait_ge(qrope_done, NH)
            settle()
            for j in range(4):
                step(V.tensor_copy(qq[32 * j:32 * j + 32, :, 64 + 32 * j:64 + 32 * j + NH],
                                   qh[64:96, :, SEQ:TOK].rearrange("p h s -> p s h")))
            step(V.tensor_copy(kpn[:, :], kpe[64:96, SEQ:TOK]))
            dve.wait_ge(qlT_done, 1)
            for hi in range(2):
                for kc in range(KKV):
                    n = 2 * hi + kc
                    last = V.tensor_copy(qq[:, :, 32 * kc + 4 * hi:32 * kc + 4 * hi + 4],
                                         ps[:, 7, n * P:(n + 1) * P].rearrange("p (g x) -> p x g", g=4)[:, 32 - DEC:32, :])
                    if n < 3:
                        step(last)
            last.then_inc(qq_done, 1)

            def row_max(h, i):
                n = 4 * h + i
                dve.wait_ge(s_done, n + 1)
                link(V.tensor_reduce(stat[:, n % 2, 0:1], ps[:, n % 3, 0:P * (i + 1)], AX_X, ALU.max))
                if n >= 2:
                    dve.wait_ge(exp_done, n - 1)
                ts(stat[:, n % 2, 1:2], stat[:, n % 2, 0:1], -SM, None, ALU.mult).then_inc(nm_done, 1)

            def normal(h, i):
                n = 4 * h + i
                dve.wait_ge(exp_done, n + 1)
                link(V.reciprocal(stat[:, n % 2, 3:4], stat[:, n % 2, 2:3]))
                pr = Pb[h % 2][:, OFF[i]:OFF[i] + P * (i + 1)]
                ts(pr, pr, stat[:, n % 2, 3:4], None, ALU.mult).then_inc(p_done, 1)

            def turned(h, j):
                n = 4 * h + j
                dve.wait_ge(t_done, n + 1)
                if h >= 2:
                    dve.wait_ge(pv_done, h // 2)
                V.tensor_copy(PTb[h % 2][:, POFF[j]:POFF[j] + (4 - j) * P], ps[:, 3 + n % 3, 0:(4 - j) * P]).then_inc(pt_dve, 1)

            row_max(0, 0)
            for i in range(1, 4):
                row_max(0, i)
                normal(0, i - 1)
            for h in range(NH):
                for i in range(4):
                    if h + 1 < NH:
                        row_max(h + 1, i)
                    if i == 0:
                        normal(h, 3)
                    elif h + 1 < NH:
                        normal(h + 1, i - 1)
                    if i >= 2:
                        turned(h, i)

            def col(s):
                return slice(s, s + 1) if isinstance(s, int) else bass.ds(s, 1)

            def cache_out(s, b2):
                if not (isinstance(s, int) and s < 2):
                    dve.wait_ge(sc_done, s - 1)
                V.tensor_copy(qs[:, b2, :], qq[:, col(s), :].rearrange("p o n -> p (o n)")).then_inc(qs_done, 1)
                dve.wait_ge(sc_done, s)
                for b in range(1, 9, 2):
                    dve.wait_ge(kt_done, 9 * s + b + 1)
                    V.tensor_copy(KT[:, 1, (b // 2) * 512:(b // 2 + 1) * 512], ps[:, b % 3, :]).then_inc(kt_evac[b % 3], 1)

            def cache_max(s, b2):
                dve.wait_ge(sc_done, s + 1)
                V.tensor_reduce(mx[:, col(s)], ps[:, 3 + b2, :], AX_X, ALU.max).then_inc(dmax_raw, 1)
                dve.wait_ge(dmax_raw, s + 1)
                ts(nmd[:, b2:b2 + 1], mx[:, col(s)], -SM, None, ALU.mult).then_inc(dmx_done, 1)

            def turned_prob(s):
                dve.wait_ge(dpt_done, s + 1)
                dve.wait_ge(op_done, s)
                V.tensor_copy(dPT, ps[:, 5, :]).then_inc(dpt_evac, 1)

            dve.wait_ge(qq_done, 1)
            cache_out(0, 0)
            cache_max(0, 0)
            with dve.Fori(0, 3) as it:
                for d in (1, 2):
                    s = it * 2 + d
                    cache_out(s, d % 2)
                    turned_prob(s - 1)
                    cache_max(s, d % 2)
            cache_out(7, 1)
            turned_prob(6)
            cache_max(7, 1)
            turned_prob(7)
            dve.wait_ge(const_ready, 5)
            step(V.tensor_reduce(sel[:, :], ident[:, :].rearrange("p (b m) -> p m b", b=4), AX_X, ALU.add))
            e8 = ident[0:DEC, 0:DEC].unsqueeze(2).broadcast_to([DEC, DEC, NH])
            snew, M, LL, wn = fin[:, 448:456], fin[:, 456:464], fin[:, 464:472], fin[:, 448:456]
            sd = fin[:, 384:448].rearrange("p (s h) -> p s h", s=DEC)
            parts = lambda at: fin[:, at:at + P].rearrange("p (i h) -> p i h", i=4)[:, :, 0:NH]
            dve.wait_ge(f_pe, 1)
            link(tt(sd, ps[0:DEC, 1, 0:64].rearrange("p (s h) -> p s h", s=DEC), e8, ALU.mult))
            link(V.tensor_reduce(snew, sd.rearrange("p s h -> p h s"), AX_X, ALU.add))
            dve.wait_ge(f_act, 1)
            link(V.tensor_reduce(M, parts(0).rearrange("p i h -> p h i"), AX_X, ALU.max))
            link(tt(M, M, snew, ALU.max))
            step(V.memset(fin[:, 256:384], 0.0))
            settle()
            step(tt(parts(256), parts(0), M.unsqueeze(1).broadcast_to([DEC, 4, NH]), ALU.subtract))
            tt(wn, snew, M, ALU.subtract).then_inc(diff_ready, 1)
            dve.wait_ge(f_act, 2)
            link(tt(parts(128), parts(128), parts(256), ALU.mult))
            link(V.tensor_reduce(LL, parts(128).rearrange("p i h -> p h i"), AX_X, ALU.add))
            link(tt(LL, LL, wn, ALU.add))
            link(V.reciprocal(LL, LL))
            step(V.memset(fin[:, 0:P], 0.0))
            link(tt(wn, wn, LL, ALU.mult))
            step(tt(parts(0), parts(256), LL.unsqueeze(1).broadcast_to([DEC, 4, NH]), ALU.mult))
            settle()
            tt(sd, e8, wn.unsqueeze(1).broadcast_to([DEC, DEC, NH]), ALU.mult).then_inc(f_dve, 1)
            dve.wait_ge(f_pe, 2)
            link(V.tensor_copy(wcol[:, :], ps[:, 2, 0:DEC]))
            for kc in range(KKV):
                step(tt(tn[:, kc, :, :], ps[:, 2, 64:128].rearrange("p (s h) -> p s h", s=DEC),
                        kvz[:, kc, SEQ:TOK].unsqueeze(2).broadcast_to([P, DEC, NH]), ALU.mult))
            dve.wait_ge(op_evac, DEC)
            for s in range(DEC):
                last = ts(op[:, s, :], op[:, s, :], wcol[:, s:s + 1], None, ALU.mult)
                if s < DEC - 1:
                    step(last)
            last.then_inc(f_dve, 1)
            dve.wait_ge(f_pe, 4)
            settle()
            for s1 in range(2):
                for kc in range(KKV):
                    n = 2 * s1 + kc
                    last = tt(oT[:, kc, :, s1:DEC:2].rearrange("p h g -> p g h"),
                              ps[:, 4, n * P:(n + 1) * P].rearrange("p (g x) -> p g x", g=4)[:, :, 0:NH],
                              tn[:, kc, s1:DEC:2, :], ALU.add)
                    if n < 3:
                        step(last)
            last.then_inc(f_dve, 1)

            dve.wait_ge(d_act, 2)
            step(V.reciprocal(rinv[:, :, :, :].rearrange("p a b c -> p (a b c)"), rinv[:, :, :, :].rearrange("p a b c -> p (a b c)")))
            V.reciprocal(rinv4[:, :], rinv4[:, :]).then_inc(d_dve, 1)

            def ln_dve(x, n, rows, root_sem, norm_sem, var_sem, g_sem, out):
                for q in range(2):
                    step(V.bn_stats(bn[0:rows, q, :], x[:, q * 512:(q + 1) * 512]))
                settle()
                V.bn_aggr(mv[0:rows, 0:2], bn[0:rows, :, :]).then_inc(var_sem, 1)
                dve.wait_ge(root_sem, n + 1)
                link(V.reciprocal(mv[0:rows, 2:3], mv[0:rows, 2:3]))
                stt(mv[0:rows, 3:4], mv[0:rows, 0:1], -1.0, mv[0:rows, 2:3], ALU.mult, ALU.mult).then_inc(var_sem, 1)
                dve.wait_ge(norm_sem, n + 1)
                tt(out, x, lng[0:rows, 0, :], ALU.mult).then_inc(g_sem, 1)

            dve.wait_ge(d_act, 3)
            dve.wait_ge(d_dve, 1)
            link(ts(tb[0][0:DEC, :], tb[0][0:DEC, :], rinv4[:, 0:1], None, ALU.mult))
            link(stt(tb[0][0:DEC, :], tb[1][0:DEC, :], rinv4[:, 1:2], tb[0][0:DEC, :], ALU.mult, ALU.add))
            dve.wait_ge(xa_done, 1)
            tt(x1[0:DEC, 4, :], x1[0:DEC, 4, :], tb[0][0:DEC, :], ALU.add).then_inc(x1_sum, 1)
            dve.wait_ge(x1_sum, 1)
            landed(dve, ln1_landed)
            ln_dve(x1[0:DEC, 4, :], 0, DEC, ln_root, ln_norm, ln_var, ln_g, x1[0:DEC, 4, :])

            def x1T_out(m):
                t = [4, 0, 1, 2, 3][m]
                dve.wait_ge(x1T_ps, m + 1)
                V.tensor_copy(x1T[:, 4:8, P * t:P * t + ROWS[t]],
                              ps[:, 7, :].rearrange("p (k n) -> p k n", k=4)[:, :, 0:ROWS[t]]).then_inc(x1T_dve, 1)

            for t in range(4):
                for n in range(2):
                    m = 1 + 2 * t + n
                    dve.wait_ge(oA_done, m)
                    cols = slice(n * 512, (n + 1) * 512)
                    stt(tb[t % 2][:, cols], ps[:, 2 * (m % 3) + 1, :], rinv[:, 1, t // 2, t % 2:t % 2 + 1],
                        tb[t % 2][:, cols], ALU.mult, ALU.add).then_inc(oR_done, 1)
                dve.wait_ge(oR_done, 2 * t + 2)
                tt(x1[:, t, :], x1[:, t, :], tb[t % 2], ALU.add).then_inc(x1_sum, 1)
                dve.wait_ge(x1_sum, t + 2)
                ln_dve(x1[:, t, :], t + 1, P, ln_root, ln_norm, ln_var, ln_g, x1[:, t, :])
                if t == 1:
                    x1T_out(0)
                if t >= 2:
                    x1T_out(t - 1)
            x1T_out(3)
            x1T_out(4)

            landed(dve, ids_landed, 3)
            link(V.memset(L[:, :, :], 0.0))
            step(V.memset(gpad[:, :, NG:8], -3e38))
            link(V.memset(valid[:, 0:4], 1.0))
            link(V.memset(valid[:, 4:5], 0.0))
            link(V.memset(valid[0:DEC, 4:5], 1.0))
            dve.wait_ge(r_pe, 2)
            for n in range(2):
                step(V.tensor_copy(L[:, 0:4, :].rearrange("p (h t) n -> p t h n", h=2)[:, n],
                                   ps[:, 1, n * P:(n + 1) * P].rearrange("p (h x) -> p h x", h=2)[:, :, 0:NG + NE]))
            link(V.tensor_copy(L[0:DEC, 4, :], ps[0:DEC, 1, 2 * P + 64:2 * P + 64 + NG + NE]))
            bc = lambda a, n: a.unsqueeze(1).broadcast_to([P, TT, n])
            per = lambda a, n: a.unsqueeze(2).broadcast_to([P, TT, n])
            link(tt(Lb, L, bc(rbias[:, :], NG + NE), ALU.add))
            link(V.tensor_copy(gpad[:, :, 0:NG], Lb[:, :, 0:NG]))
            for t in range(TT):
                step(V.max(top8[:, t, :], gpad[:, t, :]))
            settle()
            for t in range(TT):
                step(V.max_index(idx8[:, t, :], top8[:, t, :], gpad[:, t, :]))
            settle()
            link(V.tensor_copy(rs[:, 0, :], idx8[:, :, 0]))
            link(tt(ohg[:, :, :], bc(eoff_sb[:, 0:NG], NG), per(rs[:, 0, :], NG), ALU.is_equal))
            link(ts(rt_t[:, :, 0:NG], ohg[:, :, :], 1.0, 1e30, ALU.subtract, ALU.mult))
            for t in range(TT):
                step(tt(me[:, t, :].rearrange("p (g e) -> p g e", g=NG), Lb[:, t, NG:].rearrange("p (g e) -> p g e", g=NG),
                        rt_t[:, t, 0:NG].unsqueeze(2).broadcast_to([P, NG, EPG]), ALU.add))
            settle()
            for t in range(TT):
                step(V.max(top8[:, t, :], me[:, t, :]))
            settle()
            for t in range(TT):
                step(V.max_index(idx8[:, t, :], top8[:, t, :], me[:, t, :]))
            settle()
            step(V.tensor_copy(rs[:, 1, :], idx8[:, :, 0]))
            link(V.tensor_copy(rs[:, 2, :], idx8[:, :, 1]))
            step(tt(oh1, bc(eoff_sb[:, 0:NE], NE), per(rs[:, 1, :], NE), ALU.is_equal))
            link(tt(oh2, bc(eoff_sb[:, 0:NE], NE), per(rs[:, 2, :], NE), ALU.is_equal))
            link(tt(me, oh1, oh2, ALU.add))
            tt(ohb[:, :, :], me, per(valid[:, :], NE), ALU.mult).then_inc(r_dve, 1)
            dve.wait_ge(r_dve, 1)
            link(V.tensor_reduce(rs[:, 3, :], L[:, :, 0:NG], AX_X, ALU.max))
            tt(rt_t[:, :, 0:NG], L[:, :, 0:NG], per(rs[:, 3, :], NG), ALU.subtract).then_inc(r_dve, 1)
            link(tt(me, oh1, L[:, :, NG:], ALU.mult))
            link(V.tensor_reduce(rs[:, 4, :], me, AX_X, ALU.add))
            link(tt(me, oh2, L[:, :, NG:], ALU.mult))
            link(V.tensor_reduce(rs[:, 5, :], me, AX_X, ALU.add))
            link(tt(rs[:, 8, :], rs[:, 4, :], rs[:, 5, :], ALU.max))
            step(tt(rs[:, 6, :], rs[:, 4, :], rs[:, 8, :], ALU.subtract))
            tt(rs[:, 7, :], rs[:, 5, :], rs[:, 8, :], ALU.subtract).then_inc(r_dve, 1)
            dve.wait_ge(r_dve, 3)
            dve.wait_ge(r_act, 2)
            link(V.tensor_reduce(rs[:, 8, :], rt_t[:, :, 0:NG], AX_X, ALU.add))
            link(tt(rt_t[:, :, 0:NG], rt_t[:, :, 0:NG], ohg[:, :, :], ALU.mult))
            link(V.tensor_reduce(rs[:, 9, :], rt_t[:, :, 0:NG], AX_X, ALU.add))
            dve.wait_ge(r_act, 3)
            link(tt(rs[:, 12, :], rs[:, 6, :], rs[:, 7, :], ALU.add))
            link(tt(rs[:, 12, :], rs[:, 12, :], rs[:, 8, :], ALU.mult))
            link(V.reciprocal(rs[:, 12, :], rs[:, 12, :]))
            link(tt(rs[:, 12, :], rs[:, 12, :], rs[:, 9, :], ALU.mult))
            step(tt(rs[:, 10, :], rs[:, 12, :], rs[:, 6, :], ALU.mult))
            step(tt(rs[:, 11, :], rs[:, 12, :], rs[:, 7, :], ALU.mult))
            dve.wait_ge(r_pe, 3)
            step(V.tensor_copy(rt_t, ps[:, 2, 0:TT * NE].rearrange("p (t e) -> p t e", t=TT)))
            step(V.tensor_reduce(rs[:, 13, 0:1], ps[:, 2, TT * NE:(TT + 1) * NE], AX_X, ALU.max))
            for n, oh in enumerate((oh1, oh2)):
                settle()
                link(tt(me, oh, rt_t, ALU.mult))
                link(V.tensor_reduce(rs[:, 14, :], me, AX_X, ALU.add))
                link(V.tensor_copy(posi[:, n, :], rs[:, 14, :]))
                link(tt(me, oh, bc(eoff_sb[:, NE:2 * NE], NE), ALU.mult))
                link(V.tensor_reduce(rs[:, 15, :], me, AX_X, ALU.add))
                link(V.tensor_copy(posj[:, n, :], rs[:, 15, :]))
                link(stt(posj[:, n, :], posi[:, n, :], float(GRP), posj[:, n, :], ALU.mult, ALU.add))
                link(ts(posi[:, n, :], posi[:, n, :], 6, None, ALU.arith_shift_right))
                link(stt(posi[:, n, :], posi[:, n, :], float(NGRP * BLK - BLK), posj[:, n, :], ALU.mult, ALU.add))
            link(ts(rs[:, 13, 1:2], rs[:, 13, 0:1], float(CAP - 1), None, ALU.add))
            link(V.tensor_copy(rounds[:, 1:2], rs[:, 13, 1:2]))
            link(ts(rounds[:, 0:1], rounds[:, 1:2], 6, None, ALU.arith_shift_right))
            ts(rounds[:, 1:2], rounds[:, 0:1], float(NE), float(-GRP), ALU.mult, ALU.add).then_inc(pos_ready, 1)

            dve.wait_ge(pos_ready, 1)
            n_rounds = dve.value_load(rounds[0:1, 0:1], min_val=1, max_val=MAXR)
            with dve.Fori(0, n_rounds * NGRP) as it:
                def tokens_out(j):
                    t = it * GRP + j
                    dve.wait_ge(xt_ps, t + 1)
                    dve.wait_ge(gu_ps, it * GRP + max(j - 1, 0))
                    V.tensor_copy(xgT[j % 2], ps[:, j % 2, :].rearrange("p (k n) -> p k n", k=KD)).then_inc(xt_sb, 1)
                tokens_out(0)
                for j in range(GRP):
                    t = it * GRP + j
                    b = j % 2
                    if j + 1 < GRP:
                        tokens_out(j + 1)
                    dve.wait_ge(silu_done, t + 1)
                    dve.wait_ge(ht_ps, it * GRP + max(j - 1, 0))
                    tt(hx[b][0:CAP, :], sg[b][0:CAP, :], ps[64:64 + CAP, 2 + b, 0:DE], ALU.mult).then_inc(h_ready, 1)
                    dve.wait_ge(ht_ps, t + 1)
                    dve.wait_ge(dn_ps, it * GRP + max(j - 1, 0))
                    V.tensor_copy(hT[b], ps[:, 4, 0:2 * CAP].rearrange("p (f n) -> p f n", f=2)).then_inc(ht_sb, 1)
                    dve.wait_ge(dn_ps, t + 1)
                    landed(dve, scattered[j], it)
                    V.tensor_copy(yb[j][0:CAP, 512:D], ps[64:64 + CAP, 5 + b, :]).then_inc(yd_done, 1)

            landed(dve, ln2_landed)
            for t in range(TT):
                b, n = t % 2, ROWS[t]
                dve.wait_ge(g1_done, t + 1)
                link(stt(y2[b][0:n, :], y2[b][0:n, :], rs[0:n, 11, t:t + 1], y1[b][0:n, :], ALU.mult, ALU.add))
                stt(x1[0:n, t, :], x1[0:n, t, :], ALPHA, y2[b][0:n, :], ALU.mult, ALU.add).then_inc(y_sum, 1)
                dve.wait_ge(y_sum, t + 1)
                ln_dve(x1[0:n, t, :], t, n, root2, n2_done, v2_done, g2_done, y1[b][0:n, :])

        @block.gpsimd
        def _(pool):
            G = nc.gpsimd
            steps = [0]

            def step(ins):
                steps[0] += 1
                ins.then_inc(pool_step, 1)

            def settle():
                pool.wait_ge(pool_step, steps[0])

            step(G.memset(ident[:, :], 0.0))
            step(G.memset(identb[:, :], 0.0))
            step(G.memset(maskb[:, :], 0.0))
            step(G.memset(trib[:, :], 1.0))
            step(G.memset(onesb[:, :], 1.0))
            settle()
            for m in (ident, identb):
                G.affine_select(out=m[:, :], in_=m[:, :], compare_op=ALU.not_equal, fill=1.0, base=0,
                                pattern=[[-1, P]], channel_multiplier=1).then_inc(const_ready, 1)
            G.affine_select(out=maskb[:, :], in_=maskb[:, :], compare_op=ALU.is_ge, fill=NEG, base=0,
                            pattern=[[-1, P]], channel_multiplier=1).then_inc(const_ready, 1)
            G.affine_select(out=trib[:, :], in_=trib[:, :], compare_op=ALU.is_gt, fill=0.0, base=0,
                            pattern=[[1, P]], channel_multiplier=-1).then_inc(const_ready, 1)
            G.memset(empty[:, :], FREE_SLOT).then_inc(const_ready, 1)
            landed(pool, params_landed, 3)
            for k in range(KKV):
                u = U_KV + k
                pool.wait_ge(evac[u % 4], u // 4 + 1)
            G.tensor_tensor(sq0[:, KQ:KQ + KKV, :], kvz, kvz, ALU.mult).then_inc(squares, 1)
            for k in range(KQ):
                u = U_Q + k
                pool.wait_ge(evac[u % 4], u // 4 + 1)
            G.tensor_tensor(sq0[:, 0:KQ, :], qz, qz, ALU.mult).then_inc(squares, 1)
            pool.wait_ge(ix_done, KR)
            for c in range(KR):
                pool.wait_ge(a_done, c + 1)
                if c == 3:
                    pool.wait_ge(w_done, 1)
                G.tensor_tensor(tmp[:, c % 3, :], xp[:, c, :], xp[:, c, :], ALU.mult).then_inc(a2_done, 1)
            pool.wait_ge(unit_done, U_Q + KQ)
            pool.wait_ge(cidx_ready, 1)

            def fetch(s, b2):
                for rows, dst in ((kv_rows, arena_w[:, CB * b2:CB * b2 + 16 * KVL]),
                                  (rope_rows, arena_w[:, CB * b2 + 16 * KVL:CB * (b2 + 1)])):
                    G.indirect_dma_start(out=dst, out_offset=None, in_=rows,
                                         in_offset=bass.IndirectOffsetOnAxis(ap=pages[:, s:s + 1], axis=0)).then_inc(cache_landed[b2], 16)
            fetch(0, 0)
            fetch(1, 1)
            landed(pool, uq_landed)
            for k in range(KQ):
                last = G.tensor_scalar(uq[:, k, :, :], uq[:, k, :, :], vec[:, V_QG + k:V_QG + k + 1], 1.0, ALU.mult, ALU.mult)
                if k < KQ - 1:
                    step(last)
            last.then_inc(wuq_scaled, 1)
            pool.wait_ge(h_done, KR + 1)
            for c in range(KR):
                u = U_G + c
                pool.wait_ge(evac[u % 4], u // 4 + 1)
                G.tensor_tensor(recT[:, c, :], xc[:, c, :], recT[:, c, :], ALU.mult).then_inc(rec_done, 1)
            pool.wait_ge(unit_done, U_NKV + 1)
            pool.wait_ge(kpe_done, 1)
            pool.wait_ge(rec_done, KR)
            for b2 in range(2):
                landed(pool, cache_landed[b2], 2)
            for h in range(NH):
                last = G.tensor_copy(kh[64:96, h, :], kpe[64:96, 0:SEQ])
                if h < NH - 1:
                    step(last)
            last.then_inc(khrope_done, 1)
            for h in range(NH):
                u = U_UQ + h
                pool.wait_ge(evac[u % 4], u // 4 + 1)
                G.tensor_tensor(qh[64:96, h, :], qh[64:96, h, :], tmp[64:96, h % 2, :], ALU.add).then_inc(qrope_done, 1)
            landed(pool, wo_landed)
            pool.wait_ge(qrope_done, NH)
            for k in range(KD):
                g = V_AG + k
                last = G.tensor_scalar(wo[:, k, :], wo[:, k, :], vec[:, g:g + 1], 1.0, ALU.mult, ALU.mult)
                if k < KD - 1:
                    step(last)
            last.then_inc(wo_scaled, 1)
            for s in range(2, DEC):
                pool.wait_ge(op_done, s - 1)
                fetch(s, s % 2)
                if s == 3:
                    landed(pool, xtok_landed, TT)
                    step(G.tensor_scalar(x1[:, 0:4, :], x1[:, 0:4, :], ALPHA, 1.0, ALU.mult, ALU.mult))
                    G.tensor_scalar(x1[0:DEC, 4, :], x1[0:DEC, 4, :], ALPHA, 1.0, ALU.mult, ALU.mult).then_inc(xa_done, 1)

            def ln_pool(n, g_sem, done_sem, out, rows):
                pool.wait_ge(g_sem, n + 1)
                G.tensor_tensor(out, out, lng[0:rows, 1, :], ALU.add).then_inc(done_sem, 1)

            landed(pool, ln1_landed)
            for m, t in enumerate([4, 0, 1, 2, 3]):
                ln_pool(m, ln_g, x1_done, x1[0:ROWS[t], t, :], ROWS[t])
            pool.wait_ge(d_pe, 1)
            for j in range(GRP):
                step(G.memset(xg[j][0:CAP, 0:1024], 0.0))
            settle()

            landed(pool, table_empty)
            landed(pool, ids_landed, 3)
            pool.wait_ge(pos_ready, 1)
            for n in range(2):
                for t in range(TT):
                    rows = ROWS[t]
                    G.indirect_dma_start(out=slot_table, out_offset=bass.IndirectOffsetOnAxis(ap=posi[0:rows, n, t:t + 1], axis=0),
                                         in_=id_sb[0:rows, n * TT + t:n * TT + t + 1], in_offset=None).then_inc(scattered_ids, 16)
            landed(pool, scattered_ids, 2 * TT)
            landed(pool, x1_stored, TT)
            n_rounds = pool.value_load(rounds[0:1, 0:1], min_val=1, max_val=MAXR)
            before_last = pool.value_load(rounds[0:1, 1:2], min_val=NE - GRP, max_val=MAXR * NE - GRP)

            def load_slots(it):
                src = slot_table[it * BLK:(it + 1) * BLK, :] if isinstance(it, int) else slot_table[bass.ds(it * BLK, BLK), :]
                G.dma_start(raw4[:, :], src.rearrange("(s j) o -> s (j o)", j=GRP)).then_inc(raw_landed, 16)

            def gather(j):
                G.indirect_dma_start(out=xg[j][0:CAP, :], out_offset=None, in_=x1_rows,
                                     in_offset=bass.IndirectOffsetOnAxis(ap=gidx[:, j:j + 1], axis=0),
                                     bounds_check=TOK - 1, oob_is_err=False).then_inc(gathered[j], 16)

            def scatter(j):
                G.indirect_dma_start(out=pair_rows, out_offset=bass.IndirectOffsetOnAxis(ap=sidx[:, j:j + 1], axis=0),
                                     in_=yb[j][0:CAP, :], in_offset=None, bounds_check=2 * HALF_ID - 1,
                                     oob_is_err=False).then_inc(scattered[j], 16)

            def token_index(first, second):
                G.tensor_scalar(gidx[:, :], raw4[:, :], HALF_ID, -HALF_ID, ALU.is_ge, ALU.mult).then_inc(idx_half, 1)
                pool.wait_ge(pos_ready, 1)
                pool.wait_ge(idx_half, first)
                G.tensor_tensor(gidx[:, :], gidx[:, :], raw4[:, :], ALU.add).then_inc(idx_half, 1)
                pool.wait_ge(pos_ready, 1)
                pool.wait_ge(idx_half, second)

            load_slots(0)
            pool.wait_ge(raw_landed, 16)
            G.tensor_copy(sidx[:, :], raw4[:, :]).then_inc(idx_copied, 1)
            pool.wait_ge(idx_copied, 1)
            token_index(1, 2)
            load_slots(1)
            for j in range(GRP):
                gather(j)
            at = [ctx.enter_context(pool.register(f"turn{j}")) for j in range(GRP)]
            loads_now, copied = ctx.enter_context(pool.register("loads_now")), ctx.enter_context(pool.register("copied"))

            halves = [ctx.enter_context(pool.register(f"halves{n}")) for n in range(2)]

            def fixed():
                pool.wait_ge(pos_ready, 1)
            with pool.Fori(1, n_rounds * NGRP) as it:
                for j in range(GRP):
                    pool.reg_mov(at[j], (it - 1) * GRP + j + 1)
                pool.reg_mov(loads_now, it * 16 + 16)
                pool.reg_mov(copied, it + 1)
                for n in range(2):
                    pool.reg_mov(halves[n], it * 2 + n + 1)
                landings = pool.snap(it * 16)
                fixed()
                pool.wait_ge(raw_landed, loads_now)
                for j in range(GRP):
                    pool.wait_ge(gathered[j], landings)
                token_index(*halves)
                for j in range(GRP):
                    fixed()
                    pool.wait_ge(xt_ps, at[j])
                    gather(j)
                    fixed()
                    pool.wait_ge(ya_done, at[j])
                    pool.wait_ge(yd_done, at[j])
                    scatter(j)
                fixed()
                for j in range(GRP):
                    pool.wait_ge(scattered[j], landings)
                G.tensor_copy(sidx[:, :], raw4[:, :]).then_inc(idx_copied, 1)
                fixed()
                pool.wait_ge(idx_copied, copied)
                load_slots(it + 1)
            for j in range(GRP):
                pool.reg_mov(at[j], before_last + j + 1)
            for j in range(GRP):
                fixed()
                pool.wait_ge(ya_done, at[j])
                pool.wait_ge(yd_done, at[j])
                scatter(j)
            landed(pool, raw_landed, n_rounds * NGRP + 1)
            landed(pool, ln2_landed)
            for t in range(TT):
                ln_pool(t, g2_done, y_ready, y1[t % 2][0:ROWS[t], :], ROWS[t])


def _lay_out(i):
    f = np.float32
    c = np.ascontiguousarray
    x_tok = np.concatenate([i["x_prompt"].reshape(SEQ, D), i["x_sample"].reshape(DEC, D)], 0)

    def chunks(w, n):
        return w.reshape(n, P, -1).transpose(1, 0, 2)

    w_in = i["w_in"]
    a = QL + KVL
    order = [a + ROPE + P * n for n in range(4)] + [QL, QL + P] + [P * n for n in range(3)] + \
            [a + ROPE + REC + P * n for n in range(4)]
    w_in13 = np.stack([chunks(w_in[:, o:o + P], KD).reshape(P, -1) for o in order])
    hr = ROPE // 2
    kp = w_in[:, a:a + ROPE]
    w_kpe = chunks(np.concatenate([kp, kp[:, hr:], kp[:, :hr]], 1), KD).reshape(P, -1)
    uq = i["w_uq"]
    uq = np.concatenate([uq, uq[:, :, NOPE + hr:], uq[:, :, NOPE:NOPE + hr]], 2)
    w_uq = chunks(uq.reshape(QL, NH * P), KQ).reshape(P, -1)
    w_uk = chunks(i["w_uk"].reshape(KVL, -1), KKV).reshape(P, -1)
    w_uv = chunks(i["w_uv"].reshape(KVL, -1), KKV).reshape(P, -1)
    w_ukT = i["w_uk"].transpose(2, 1, 0).reshape(NOPE, -1)
    cols = lambda v: v.reshape(-1, P).T
    vecs = np.concatenate([cols(i["q_norm_g"]), cols(i["kv_norm_g"]),
                           i["conv_w"].reshape(CONV, KR, P).transpose(2, 1, 0).reshape(P, -1), cols(i["conv_b"]),
                           cols(i["b_rg"]), cols(i["b_ig"]), cols(i["lru_lambda"]), cols(i["att_out_g"]),
                           cols(i["rec_out_g"])], 1)
    gates = np.zeros((P, 2, KR, P), f)
    for g, w in enumerate((i["w_rg"], i["w_ig"])):
        for n in range(2 * KR):
            h = 64 * (n % 2)
            gates[h:h + 64, g, n // 2, h:h + 64] = w[n]
    inv = (10000.0 ** (-(np.arange(hr, dtype=np.float64) * 2.0 / ROPE))).astype(f)
    pos = np.concatenate([np.arange(SEQ), np.full(DEC, PAST)]).astype(f)
    ang = (pos[:, None] * inv[None, :]).astype(f).astype(np.float64)
    co, si = np.cos(ang).astype(f).T, np.sin(ang).astype(f).T
    w_router = np.zeros((D, 64), f)
    w_router[:, :NG] = i["w_group"]
    w_router[:, NG:NG + NE] = i["w_expert"]
    e = np.arange(NE)
    tok = np.arange(P)[:, None] + P * np.arange(TT)[None, :]
    return {
        "xT": x_tok.T.reshape(KD, P, TOK).transpose(1, 0, 2), "x_tok": x_tok,
        "kv_cache": i["cache_kv_latent"], "rope_cache": i["cache_k_rope"],
        "conv_st": i["state_conv"].reshape(DEC, CONV - 1, KR, P).transpose(3, 2, 1, 0),
        "rec_st": i["state_rec"].reshape(DEC, KR, P).transpose(2, 1, 0),
        "page_rep": np.repeat(i["page_table"].T, P // N_PAGES, axis=0).astype(np.int32),
        "lane": (np.arange(P) % 8).astype(np.int32)[:, None],
        "w_in": w_in13, "w_kpe": w_kpe, "w_uq": w_uq, "w_uk": w_uk, "w_uv": w_uv, "w_ukT": w_ukT, "vecs": vecs,
        "gates": gates.reshape(P, -1), "cs_tab": np.concatenate([co, co, -si, si], 0),
        "w_out": chunks(i["w_out"], KD).reshape(P, -1), "w_router": chunks(w_router, KD).reshape(P, -1),
        "r_bias": np.concatenate([i["b_group"], i["b_expert"]]),
        "lns": np.stack([i["ln1_g"], i["ln1_b"], i["ln2_g"], i["ln2_b"]]),
        "ids": np.concatenate([tok, tok + HALF_ID], 1).astype(np.int32),
        "eoff": np.concatenate([e, (e // GRP) * BLK + e % GRP]).astype(f),
        "w_gu": i["w_gate_up"], "w_dn": i["w_down"],
    }, c


_OUTS = {"y": (TOK, D), "ckv": (P, KKV, TOK), "kpe": (ROPE, TOK), "conv_p": (P, KR, CONV - 1), "rec_p": (P, KR),
         "conv_s": (P, KR, CONV - 1, DEC), "rec_s": (P, KR, DEC)}


def kernel(**inputs):
    import concourse.bacc as _bacc
    from concourse.bass_utils import run_bass_kernel_spmd as _run

    laid, c = _lay_out({k: np.asarray(v) for k, v in inputs.items()})
    nc = _bacc.Bacc("TRN2", target_bir_lowering=False, num_devices=1)
    arrays, args = {}, []
    for name, a in laid.items():
        a = c(a)
        arrays["in_" + name] = a
        args.append(nc.dram_tensor("in_" + name, a.shape, mybir.dt.from_np(a.dtype), kind="ExternalInput").ap())
    for name, shape in _OUTS.items():
        args.append(nc.dram_tensor("out_" + name, shape, F32, kind="ExternalOutput").ap())
    hymba_step(nc, *args)
    r = _run(nc, [arrays], core_ids=[0]).results[0]
    o = {k: np.asarray(r["out_" + k]) for k in _OUTS}
    ckv = o["ckv"].transpose(2, 1, 0).reshape(TOK, KVL)
    kpe = o["kpe"].T
    y = o["y"]
    conv_s = o["conv_s"].transpose(3, 2, 1, 0).reshape(DEC, CONV - 1, REC)
    return (c(y[:SEQ]).reshape(1, SEQ, D), c(y[SEQ:]).reshape(DEC, 1, D),
            c(ckv[:SEQ]).reshape(1, SEQ, KVL), c(kpe[:SEQ]).reshape(1, SEQ, ROPE),
            c(o["conv_p"].transpose(2, 1, 0)).reshape(1, CONV - 1, REC), c(o["rec_p"].T).reshape(1, REC),
            c(ckv[SEQ:]).reshape(DEC, 1, KVL), c(kpe[SEQ:]).reshape(DEC, 1, ROPE),
            c(conv_s), c(o["rec_s"].transpose(2, 1, 0)).reshape(DEC, REC))
```

```python
from contextlib import ExitStack

import numpy as np

import concourse.bass as bass
from concourse import mybir

ACT = mybir.ActivationFunctionType
ALU = mybir.AluOpType
AX_X = mybir.AxisListType.X
F32 = mybir.dt.float32
BF16 = mybir.dt.bfloat16
I32 = mybir.dt.int32
U32 = mybir.dt.uint32

P = 128
D = 1024
KD = D // P
SEQ = 512
DEC = 8
TOK = SEQ + DEC
HALF = TOK // 2
PAST, PAGE = 2048, 128
N_PAGES = PAST // PAGE
NPOOL = DEC * N_PAGES * 5 // 4
NH, NOPE, ROPE, VH = 8, 64, 32, 64
QL, KVL, REC = 384, 256, 512
KQ, KKV, KR = QL // P, KVL // P, REC // P
CONV = 4
NG, EPG, NE, DE = 4, 8, 32, 256
SM = float((NOPE + ROPE) ** -0.5)
ALPHA = float(2.0 ** 0.25)
LN_EPS, RMS_EPS = 1e-5, 1e-6
NEG = -1e30
TT = 5
ROWS = [P, P, P, P, DEC]
SHIFT = SEQ // 2
WIN = TOK - SHIFT

CAP = 64
GRP = 4
NPAIR = GRP // 2
NGRP = NE // GRP
MAXR = -(-TOK // CAP)
BLK = CAP * GRP
NTAB = (MAXR * NGRP + 2) * BLK
FREE_SLOT = 8191
HALF_ID = 1024

V_QG, V_KVG, V_CW, V_CB, V_BR, V_BI, V_LAM, V_AG, V_RG = 0, 3, 5, 21, 25, 29, 33, 37, 41
NV = 45

U_RX, U_KV, U_KPE, U_Q, U_R, U_I, U_NQ, U_NKV, U_G, U_UQ, U_UK, U_V = 0, 4, 6, 7, 10, 14, 18, 19, 20, 24, 32, 36
N_UNITS = 40
CHUNK_OF = {**{U_RX + c: c for c in range(4)}, U_KV: 4, U_KV + 1: 5, U_Q: 6, U_Q + 1: 7, U_Q + 2: 8,
            **{U_G + c: 9 + c for c in range(4)}}
N_CHUNKS = 13
LAND_OF = [0, 1, 2, 3, 4, 5, 6, 6, 6, 7, 7, 7, 7]

W_X = N_CHUNKS * D + KD * 64
W_SLOT = KD * 2 * DE + 2 * D
W_LEN = 3 * W_SLOT
CB = 16 * (KVL + ROPE)
W_OP = 2 * CB
W_PT = W_OP + DEC * KVL
W_KT = W_PT + 2 * 1280
O_UQ, O_UK, O_UV, O_UKT, O_GATE = 0, 3072, 4096, 5120, 7168
O_LEN = KD * D
S_QH, S_KH, S_V, S_ATT, S_REC, S_XC, S_XP, S_TMP = 0, 4160, 8256, 10304, 12384, 14464, 16544, 18624
S_QZ, S_KVZ, S_RQ, S_RKV, S_KPE = 20184, 21744, 22784, 23304, 23824
S_LEN = 24344
S_SQ0 = S_KH
S_P = [S_QZ, S_XP]
S_RT8, S_DP, S_DPT = S_XP + 1280, S_RKV, S_RKV + 512
S_QQ, S_QS = S_XC, S_XC + 8 * 192
S_X1, S_UV2, S_SQ = 0, 9280, 5120
S_RT = 9280
S_X1T = S_XC
S_WR = S_TMP
S_LN = 19392
S_T = S_KVZ
S_XG, S_YB, S_E = 5120, S_ATT, S_XC

OFF = [0, 128, 384, 768]
POFF = [0, 512, 896, 1152]

TURNS = ["p", 0, 1, "h0", 2, 3, "h1", 4, 5, "h2", 6, 7, 8, "h3"]


def turn_no(s, what):
    return len(TURNS) * s + TURNS.index(what) - 1


def hymba_step(nc, xT, x_tok, kv_cache, rope_cache, conv_st, rec_st, page_rep, lane, w_in, w_kpe, w_uq, w_uk,
               w_uv, w_ukT, vecs, gates, cs_tab, w_out, w_router, r_bias, lns, ids, eoff, w_gu, w_dn,
               y_out, ckv_out, kpe_out, conv_p_out, rec_p_out, conv_s_out, rec_s_out):
    x1_rows = nc.dram_tensor("x1_rows", (TOK, D), F32, kind="Internal").ap()
    pair_rows = nc.dram_tensor("pair_rows", (2 * HALF_ID, D), F32, kind="Internal").ap()
    slot_table = nc.dram_tensor("slot_table", (NTAB, 1), I32, kind="Internal").ap()
    kv_rows = kv_cache.rearrange("n (c j) e -> (n c) (j e)", c=8)
    rope_rows = rope_cache.rearrange("n (c j) e -> (n c) (j e)", c=8)

    with ExitStack() as ctx:
        def sb(name, shape, dt=F32):
            return ctx.enter_context(nc.sbuf_tensor(name, shape, dt))

        def sem(name):
            return ctx.enter_context(nc.semaphore(name))

        ps = ctx.enter_context(nc.psum_tensor("ps", [P, 8, 512], F32))
        arena_w = sb("arena_w", [P, W_LEN])
        arena_o = sb("arena_o", [P, O_LEN])
        arena_s = sb("arena_s", [P, S_LEN])

        def part(arena, at, *dims):
            n = int(np.prod(dims))
            v = arena[:, at:at + n]
            if len(dims) == 2:
                v = v.rearrange("p (a b) -> p a b", a=dims[0])
            if len(dims) == 3:
                v = v.rearrange("p (a b c) -> p a b c", a=dims[0], b=dims[1])
            return v

        ident = sb("ident", [P, P])
        identb = sb("identb", [P, P], BF16)
        maskb = sb("maskb", [P, P], BF16)
        trib = sb("trib", [P, P], BF16)
        onesb = sb("onesb", [P, P], BF16)
        ones = sb("ones", [P, P])
        cs = sb("cs", [P, TOK])
        vec = sb("vec", [P, NV])
        lam = sb("lam", [P, 8, KR])
        nsp = sb("nsp", [P, 2, KR])
        bh = sb("bh", [P, 2, KR])
        eps = sb("eps", [P, 2])
        cdec = sb("cdec", [P, KR, CONV, DEC])
        conv_tail = sb("conv_tail", [P, KR, CONV - 1])
        rec_last = sb("rec_last", [P, KR])
        rst = sb("rst", [P, KR, DEC])
        rbias = sb("rbias", [P, NG + NE])
        stat = sb("stat", [P, 2, 4])
        mx = sb("mx", [P, DEC])
        ls = sb("ls", [P, DEC])
        nmd = sb("nmd", [P, 2])
        pages = sb("pages", [P, DEC], I32)
        lane_sb = sb("lane_sb", [P, 1], I32)
        kpn = sb("kpn", [ROPE, DEC])
        sel = sb("sel", [P, 32])
        wcol = sb("wcol", [P, DEC])
        rinv = sb("rinv", [P, 2, 2, 2])
        rinv4 = sb("rinv4", [DEC, 2])
        bn = sb("bn", [P, 2, 6])
        mv = sb("mv", [P, 2, 4])
        gpad = sb("gpad", [P, TT, 8])
        top8 = sb("top8", [P, TT, 8])
        idx8 = sb("idx8", [P, TT, 8], U32)
        rs = sb("rs", [P, 16, TT])
        ohb = sb("ohb", [P, TT, NE], BF16)
        ohg = sb("ohg", [P, TT, NG])
        id_sb = sb("id_sb", [P, 2 * TT], I32)
        eoff_sb = sb("eoff_sb", [P, 2 * NE])
        valid = sb("valid", [P, TT])
        posi = sb("posi", [P, 2, TT], I32)
        posj = sb("posj", [P, 2, TT], I32)
        rounds = sb("rounds", [P, 2], I32)
        raw = sb("raw", [P, 2, NPAIR], I32)
        gidx = sb("gidx", [P, NPAIR], I32)
        sidx = sb("sidx", [P, NPAIR], I32)
        empty = sb("empty", [P, NTAB // P], I32)

        xTv = part(arena_w, W_X, KD, TOK)
        w_chunk = [part(arena_w, c * D, KD, P) for c in range(N_CHUNKS)]
        w_kpev = part(arena_w, N_CHUNKS * D, KD, 64)
        uq, uk, uv = part(arena_o, O_UQ, KQ, NH, P), part(arena_o, O_UK, KKV, 512), part(arena_o, O_UV, KKV, 512)
        ukT = part(arena_o, O_UKT, NH, KVL)
        gw = part(arena_o, O_GATE, 2, KR, P)
        wo = part(arena_o, 0, KD, D)
        qh, kh, v = part(arena_s, S_QH, NH, TOK), part(arena_s, S_KH, NH, SEQ), part(arena_s, S_V, 4, 512)
        attT, recT = part(arena_s, S_ATT, KR, TOK), part(arena_s, S_REC, KR, TOK)
        tr, xc, xp = attT, part(arena_s, S_XC, KR, TOK), part(arena_s, S_XP, KR, TOK)
        tmp = part(arena_s, S_TMP, 3, TOK)
        qz, kvz = part(arena_s, S_QZ, KQ, TOK), part(arena_s, S_KVZ, KKV, TOK)
        rq, rkv, kpe = part(arena_s, S_RQ, TOK), part(arena_s, S_RKV, TOK), part(arena_s, S_KPE, TOK)
        sq0 = part(arena_s, S_SQ0, KQ + KKV, TOK)
        Pb = [part(arena_s, S_P[b], 1280) for b in range(2)]
        PTb = [part(arena_w, W_PT + 1280 * b, 1280) for b in range(2)]
        buf = [arena_w[:, 0:CB], arena_w[:, CB:2 * CB], arena_o[:, 0:CB]]
        cache = [part(b, 0, 16, KVL) for b in buf]
        crope = [part(b, 16 * KVL, 4, P) for b in buf]
        KT, ropeT = part(arena_w, W_KT, KKV, PAST), part(arena_s, S_RT8, 512)
        dP, dPT = part(arena_s, S_DP, 512), part(arena_s, S_DPT, 512)
        op = part(arena_w, W_OP, DEC, KVL)
        qq, qs = part(arena_s, S_QQ, DEC, 192), part(arena_s, S_QS, 2, 192)
        qlt = part(arena_s, S_TMP, 512)
        fin = arena_s[0:DEC, S_RQ:S_RQ + 512]
        osum, tn, oT = part(arena_s, S_TMP, 512), part(arena_s, S_TMP + 512, KKV, DEC, NH), part(arena_s, S_TMP + 640, KKV, NH, DEC)
        uv2 = part(arena_s, S_UV2, KKV, 512)
        x1, sq = part(arena_s, S_X1, TT, D), part(arena_s, S_SQ, KD, TOK)
        L, Lb = part(arena_s, S_RT, TT, NG + NE), part(arena_s, S_RT + 180, TT, NG + NE)
        me, oh1, oh2, rt_t = (part(arena_s, S_RT + 360 + 160 * n, TT, NE) for n in range(4))
        x1T = part(arena_s, S_X1T, KD, TOK)
        wr = part(arena_s, S_WR, KD, 64)
        lng = part(arena_s, S_LN, 2, D)
        lng2 = part(arena_o, W_SLOT, 2, D)
        tb = [part(arena_s, S_T + D * b, D) for b in range(2)]
        ss, rt = part(arena_s, S_T, WIN), part(arena_s, S_T, WIN)
        slot = [arena_w[:, W_SLOT * n:W_SLOT * (n + 1)] for n in range(3)] + [arena_o[:, 0:W_SLOT]]
        gu_w = [s[:, 0:KD * 2 * DE].rearrange("p (k n) -> p k n", k=KD) for s in slot]
        dn_w = [s[:, KD * 2 * DE:W_SLOT].rearrange("p (k n) -> p k n", k=2) for s in slot]
        xg = [part(arena_s, S_XG + D * b, D) for b in range(NPAIR)]
        yb = [part(arena_s, S_YB + D * b, D) for b in range(NPAIR)]
        xgT = part(arena_s, S_E, KD, P)
        sg, hx, hT = part(arena_s, S_E + 1024, DE), part(arena_s, S_E + 1024 + DE, DE), part(arena_s, S_E + 1024 + 2 * DE, 2, P)
        y1, y2 = ([part(arena_w, 2 * D * t + D * n, D) for t in range(TT)] for n in range(2))
        mixer = part(arena_s, S_E + 2048, 2 * TT, P)

        def pair(u, cols=HALF):
            b = 2 * (u % 4)
            return ps[:, b:b + 2, 0:cols]

        x_landed = [sem(f"x_landed{n}") for n in range(4)]
        win_landed = [sem(f"win_landed{n}") for n in range(8)]
        kpe_w_landed, gates_landed, uq_landed = sem("kpe_w_landed"), sem("gates_landed"), sem("uq_landed")
        ukv_landed, params_landed, cs_landed = sem("ukv_landed"), sem("params_landed"), sem("cs_landed")
        pages_landed, ids_landed = sem("pages_landed"), sem("ids_landed")
        wo_landed, uv2_landed, xtok_landed = sem("wo_landed"), sem("uv2_landed"), sem("xtok_landed")
        ln1_landed, ln2_landed = sem("ln1_landed"), sem("ln2_landed")
        cache_landed = [sem(f"cache_landed{b}") for b in range(3)]
        gu_landed = [sem(f"gu_landed{q}") for q in range(NPAIR)]
        dn_landed = [sem(f"dn_landed{q}") for q in range(NPAIR)]
        table_empty, scattered_ids = sem("table_empty"), sem("scattered_ids")
        raw_landed = sem("raw_landed")
        gathered = [sem(f"gathered{q}") for q in range(NPAIR)]
        scattered = [sem(f"scattered{q}") for q in range(NPAIR)]
        x1_stored = sem("x1_stored")
        y_landed = [sem(f"y_landed{t}") for t in range(TT)]
        y_stored = sem("y_stored")
        outs_stored = sem("outs_stored")
        dve_step, act_step, pool_step = sem("dve_step"), sem("act_step"), sem("pool_step")
        const_ready, ones_ready = sem("const_ready"), sem("ones_ready")
        unit_done = sem("unit_done")
        evac = [sem(f"evac{n}") for n in range(4)]
        conv_done, kpe_done, squares, wuq_scaled = sem("conv_done"), sem("kpe_done"), sem("squares"), sem("wuq_scaled")
        rms_root, ckv_done, rq_done = sem("rms_root"), sem("ckv_done"), sem("rq_done")
        gate_in, a_done, th_done, a2_done, w_done, root_w = (sem(n) for n in (
            "gate_in", "a_done", "th_done", "a2_done", "w_done", "root_w"))
        ix_done, h_done, rec_done = sem("ix_done"), sem("h_done"), sem("rec_done")
        lam_ready, eps_ready, sp_exp = sem("lam_ready"), sem("eps_ready"), sem("sp_exp")
        swap_done, qrope_done, khrope_done = sem("swap_done"), sem("qrope_done"), sem("khrope_done")
        s_done, nm_done, exp_done, p_done, t_done = (sem(n) for n in ("s_done", "nm_done", "exp_done", "p_done", "t_done"))
        out_act, out_dve, pv_done, att_done = sem("out_act"), sem("out_dve"), sem("pv_done"), sem("att_done")
        ql_done, ql_evac, qlT_done, qq_done = sem("ql_done"), sem("ql_evac"), sem("qlT_done"), sem("qq_done")
        qs_done, sc_done, dmx_done, dexp_done = (sem(n) for n in ("qs_done", "sc_done", "dmx_done", "dexp_done"))
        op_done, op_evac = sem("op_done"), sem("op_evac")
        cidx_ready, dmax_raw, diff_ready = sem("cidx_ready"), sem("dmax_raw"), sem("diff_ready")
        wr_landed, idx_half, idx_copied = sem("wr_landed"), sem("idx_half"), sem("idx_copied")
        f_pe, f_act, f_dve = sem("f_pe"), sem("f_act"), sem("f_dve")
        sq_done, wo_scaled, xa_done = sem("sq_done"), sem("wo_scaled"), sem("xa_done")
        d_pe, d_act, d_dve = sem("d_pe"), sem("d_act"), sem("d_dve")
        o_done, oA_done, oR_done, x1_sum, ln_norm, ln_g, x1_done = (sem(n) for n in (
            "o_done", "oA_done", "oR_done", "x1_sum", "ln_norm", "ln_g", "x1_done"))
        ln_var, ln_root = sem("ln_var"), sem("ln_root")
        x1T_ps, x1T_act, x1T_dve = sem("x1T_ps"), sem("x1T_act"), sem("x1T_dve")
        r_pe, r_act, r_dve, pos_ready = sem("r_pe"), sem("r_act"), sem("r_dve"), sem("pos_ready")
        xg_zero = sem("xg_zero")
        xt_ps, xt_sb, gu_ps, silu_done, h_ready, ht_ps, ht_sb, dn_ps, ya_done, yd_done = (sem(n) for n in (
            "xt_ps", "xt_sb", "gu_ps", "silu_done", "h_ready", "ht_ps", "ht_sb", "dn_ps", "ya_done", "yd_done"))
        mixer_in = sem("mixer_in")
        mixer_ready, y_mixed, y_sum, v2_done, root2, n2_done, g2_done, y_ready = (sem(n) for n in (
            "mixer_ready", "y_mixed", "y_sum", "v2_done", "root2", "n2_done", "g2_done", "y_ready"))

        block = ctx.enter_context(nc.Block())

        def landed(eng, s, n=1):
            eng.wait_ge(s, 16 * n)

        def out_of_psum(eng, n):
            eng.wait_ge(out_dve if n % 2 else out_act, n // 2 + 1)

        @block.sync
        def _(sp):
            def chunk(c):
                sp.dma_start(arena_w[:, c * D:(c + 1) * D], w_in[c]).then_inc(win_landed[LAND_OF[c]], 16)
            sp.dma_start(xTv[:, 0:2, :], xT[:, 0:2, :]).then_inc(x_landed[0], 16)
            chunk(0)
            for n in range(1, 4):
                sp.dma_start(xTv[:, 2 * n:2 * n + 2, :], xT[:, 2 * n:2 * n + 2, :]).then_inc(x_landed[n], 16)
            for c in range(1, 6):
                chunk(c)
            sp.dma_start(arena_w[:, N_CHUNKS * D:W_X], w_kpe).then_inc(kpe_w_landed, 16)
            sp.dma_start(arena_o[:, O_GATE:O_GATE + 1024], gates).then_inc(gates_landed, 16)
            for c in range(6, N_CHUNKS):
                chunk(c)
            sp.dma_start(arena_o[:, O_UQ:O_UQ + 3072], w_uq).then_inc(uq_landed, 16)
            sp.dma_start(arena_o[:, O_UK:O_UK + 1024], w_uk).then_inc(ukv_landed, 16)
            sp.dma_start(arena_o[:, O_UV:O_UV + 1024], w_uv).then_inc(ukv_landed, 16)
            sp.dma_start(arena_o[0:NOPE, O_UKT:O_UKT + 2048], w_ukT).then_inc(ukv_landed, 16)
            sp.wait_ge(const_ready, 5)
            sp.dma_start(slot_table.rearrange("(p n) o -> p (n o)", p=P), empty[:, :]).then_inc(table_empty, 16)
            sp.wait_ge(kpe_done, 1)
            sp.dma_start(kpe_out, kpe[64:96, :]).then_inc(outs_stored, 16)
            sp.wait_ge(ckv_done, 1)
            sp.dma_start(ckv_out, kvz).then_inc(outs_stored, 16)
            sp.wait_ge(h_done, 5)
            sp.dma_start(conv_p_out, conv_tail[:, :, :]).then_inc(outs_stored, 16)
            sp.dma_start(conv_s_out, cdec[:, :, 1:CONV, :]).then_inc(outs_stored, 16)
            sp.dma_start(rec_p_out, rec_last[:, :]).then_inc(outs_stored, 16)
            sp.dma_start(rec_s_out, xc[:, :, SEQ:TOK]).then_inc(outs_stored, 16)
            sp.wait_ge(op_done, 6)
            sp.dma_start(arena_o[:, 0:O_LEN], w_out).then_inc(wo_landed, 16)
            sp.wait_ge(s_done, 4 * NH)
            for t in range(TT):
                sp.dma_start(x1[0:ROWS[t], t, :], x_tok[P * t:P * t + ROWS[t], :]).then_inc(xtok_landed, 16)
            sp.wait_ge(pv_done, NH // 2)
            sp.dma_start(uv2, w_uv.rearrange("p (k n) -> p k n", k=KKV)).then_inc(uv2_landed, 16)
            sp.dma_start(lng, lns[0:2].partition_broadcast(P)).then_inc(ln1_landed, 16)
            sp.wait_ge(f_pe, 4)
            sp.dma_start(arena_s[:, S_WR:S_WR + 512], w_router).then_inc(wr_landed, 16)

            def gate_up(j, e):
                sp.dma_start(gu_w[j], w_gu[e].rearrange("o (k p) n -> p (o k) n", p=P)).then_inc(gu_landed[j // 2], 16)

            def down(j, e):
                sp.dma_start(dn_w[j], w_dn[e].rearrange("o (k p) n -> p (o k) n", p=P)).then_inc(dn_landed[j // 2], 16)
            for j in (0, 1):
                gate_up(j, slice(j, j + 1))
            for j in (0, 1):
                down(j, slice(j, j + 1))
            gate_up(2, slice(2, 3))
            down(2, slice(2, 3))
            for n, t in enumerate([4, 0, 1, 2, 3]):
                sp.wait_ge(x1_done, n + 1)
                sp.dma_start(x1_rows[P * t:P * t + ROWS[t], :], x1[0:ROWS[t], t, :]).then_inc(x1_stored, 16)
            sp.wait_ge(o_done, 9)
            gate_up(3, slice(3, 4))
            down(3, slice(3, 4))
            sp.dma_start(lng2, lns[2:4].partition_broadcast(P)).then_inc(ln2_landed, 16)
            sp.wait_ge(pos_ready, 1)
            n_rounds = sp.value_load(rounds[0:1, 0:1], min_val=1, max_val=MAXR)
            with sp.Fori(1, n_rounds * NGRP) as it:
                for q in range(NPAIR):
                    sp.wait_ge(gu_ps, (it - 1) * NPAIR + q + 1)
                    for j in (2 * q, 2 * q + 1):
                        gate_up(j, bass.ds((it % NGRP) * GRP + j, 1))
                    sp.wait_ge(dn_ps, (it - 1) * NPAIR + q + 1)
                    for j in (2 * q, 2 * q + 1):
                        down(j, bass.ds((it % NGRP) * GRP + j, 1))
            for q in range(NPAIR):
                sp.wait_ge(scattered[q], n_rounds * (NGRP * 16))
            for t in range(TT):
                n = ROWS[t]
                sp.dma_start(y1[t][0:n, :], pair_rows[P * t:P * t + n, :]).then_inc(y_landed[t], 16)
                sp.dma_start(y2[t][0:n, :], pair_rows[HALF_ID + P * t:HALF_ID + P * t + n, :]).then_inc(y_landed[t], 16)
            for t in range(TT):
                sp.wait_ge(y_ready, t + 1)
                sp.dma_start(y_out[P * t:P * t + ROWS[t], :], y1[t][0:ROWS[t], :]).then_inc(y_stored, 16)
            landed(sp, y_stored, TT)
            landed(sp, outs_stored, 6)

        def turned(eng, copy, done, s, what):
            n = turn_no(s, what)
            eng.wait_ge(t_done, n + 1)
            cols = 512
            if what == "p":
                dst = dPT
                if s >= 2:
                    eng.wait_ge(op_done, s - 1)
            elif isinstance(what, int):
                dst = ropeT if what == 8 else KT[:, what % 2, (what // 2) * 512:(what // 2 + 1) * 512]
                if s >= 1:
                    eng.wait_ge(sc_done, s)
            else:
                j = int(what[1])
                cols = (4 - j) * P
                dst = PTb[s % 2][:, POFF[j]:POFF[j] + cols]
                if s >= 2:
                    eng.wait_ge(pv_done, s // 2)
            copy(dst, ps[:, 2 + n % 3, 0:cols]).then_inc(done, 1)

        @block.tensor
        def _(pe):
            mm = nc.tensor.matmul

            def unit(u, lhs, rhs, ks, rows=slice(0, P)):
                if u >= 4:
                    pe.wait_ge(evac[u % 4], u // 4)
                b = 2 * (u % 4)
                for k in range(ks):
                    if u == 0 and k % 2 == 0:
                        landed(pe, x_landed[k // 2])
                    for n in range(2):
                        last = mm(ps[rows, b + n, 0:HALF], lhs(k), rhs(k)[:, n * HALF:(n + 1) * HALF],
                                  start=(k == 0), stop=(k == ks - 1))
                last.then_inc(unit_done, 1)

            def project(u):
                c = CHUNK_OF[u]
                landed(pe, win_landed[LAND_OF[c]], LAND_OF.count(LAND_OF[c]))
                unit(u, lambda k: w_chunk[c][:, k, :], lambda k: xTv[:, k, :], KD)

            for u in range(U_RX, U_KPE):
                project(u)
            landed(pe, kpe_w_landed)
            unit(U_KPE, lambda k: w_kpev[:, k, :], lambda k: xTv[:, k, :], KD, slice(64, 128))
            for u in range(U_Q, U_Q + KQ):
                project(u)
            landed(pe, gates_landed)
            for g, u0 in enumerate((U_R, U_I)):
                for c in range(KR):
                    pe.wait_ge(conv_done, c + 1)
                    unit(u0 + c, lambda k: gw[:, g, c, :], lambda k: xc[:, c, :], 1)
            pe.wait_ge(ones_ready, 1)
            pe.wait_ge(squares, 2)
            unit(U_NQ, lambda k: ones[:, :], lambda k: sq0[:, k, :], KQ)
            unit(U_NKV, lambda k: ones[:, :], lambda k: sq0[:, KQ + k, :], KKV)
            for u in range(U_G, U_G + KR):
                project(u)
            pe.wait_ge(wuq_scaled, 1)
            for h in range(NH):
                unit(U_UQ + h, lambda k: uq[:, k, h, :], lambda k: qz[:, k, :], KQ)
            landed(pe, ukv_landed, 3)
            pe.wait_ge(ckv_done, 1)
            for n in range(4):
                u = U_UK + n
                pe.wait_ge(evac[u % 4], u // 4)
                for k in range(KKV):
                    last = mm(ps[:, 2 * (u % 4), :], uk[:, k, n * P:(n + 1) * P], kvz[:, k, 0:SEQ],
                              start=(k == 0), stop=(k == KKV - 1))
                last.then_inc(unit_done, 1)
            for n in range(4):
                u = U_V + n
                pe.wait_ge(evac[u % 4], u // 4)
                for k in range(KKV):
                    last = mm(ps[:, 2 * (u % 4), :], kvz[:, k, n * P:(n + 1) * P], uv[:, k, :],
                              start=(k == 0), stop=(k == KKV - 1))
                last.then_inc(unit_done, 1)
            for n in range(4):
                pe.wait_ge(evac[n], N_UNITS // 4)

            pe.wait_ge(qrope_done, NH)
            for hi in range(2):
                for g in range(4):
                    h = 4 * hi + g
                    last = mm(ps[32 * g:32 * g + 32, 6, hi * KVL:(hi + 1) * KVL], qh[0:NOPE, h, TOK - 32:TOK],
                              ukT[0:NOPE, h, :], start=True, stop=True)
            last.then_inc(ql_done, 1)

            pe.wait_ge(khrope_done, 1)
            pe.wait_ge(const_ready, 5)

            def scores(h, i):
                n = 4 * h + i
                if n >= 2:
                    pe.wait_ge(exp_done, n - 1)
                b = n % 2
                mm(ps[:, b, 0:P * (i + 1)], qh[0:96, h, i * P:(i + 1) * P], kh[0:96, h, 0:P * (i + 1)],
                   start=True, stop=False)
                mm(ps[:, b, P * i:P * (i + 1)], identb[:, :], maskb[:, :], start=False, stop=True,
                   ).then_inc(s_done, 1)

            def turn(n, blocks):
                if n >= 3:
                    out_of_psum(pe, n - 3)
                for m, src in enumerate(blocks):
                    last = nc.tensor.transpose(ps[:, 2 + n % 3, m * P:(m + 1) * P], src, ident[:, :])
                last.then_inc(t_done, 1)

            def turn_head(h, j):
                pe.wait_ge(p_done, 4 * h + 4)
                turn(turn_no(h, f"h{j}"), [Pb[h % 2][:, OFF[i] + j * P:OFF[i] + (j + 1) * P] for i in range(j, 4)])

            def turn_cache(s, b):
                landed(pe, cache_landed[s % 3], 2 * (s // 3 + 1))
                i, kc = b // 2, b % 2
                turn(turn_no(s, b), [crope[s % 3][:, j, :] if b == 8 else cache[s % 3][:, 4 * i + j, kc * P:(kc + 1) * P]
                                     for j in range(4)])

            def turn_cache_probs(s):
                pe.wait_ge(dexp_done, s + 1)
                turn(turn_no(s + 1, "p"), [dP[:, j * P:(j + 1) * P] for j in range(4)])

            def values(hp):
                out_of_psum(pe, turn_no(2 * hp + 1, "h1"))
                out_of_psum(pe, turn_no(2 * hp + 1, "h3"))
                if hp >= 1:
                    pe.wait_ge(att_done, hp)
                for j in range(4):
                    for e in range(2):
                        h = 2 * hp + e
                        last = mm(ps[64 * e:64 * e + 64, 5, j * P:SEQ], v[:, j, h * VH:(h + 1) * VH],
                                  PTb[e][:, POFF[j]:POFF[j] + (4 - j) * P], start=(j == 0), stop=(j == 3))
                last.then_inc(pv_done, 1)

            def cache_scores(s):
                out_of_psum(pe, turn_no(s, 7))
                out_of_psum(pe, turn_no(s, 8))
                pe.wait_ge(qs_done, s + 1)
                if s >= 1:
                    pe.wait_ge(dexp_done, s)
                q = qs[:, s % 2, :]
                for kc in range(KKV):
                    for i in range(4):
                        mm(ps[32 * i:32 * i + 32, 6, :], q[:, 32 * kc:32 * kc + 32],
                           KT[:, kc, i * 512:(i + 1) * 512], start=(kc == 0), stop=False, skip_group_check=True)
                for j in range(4):
                    for i in range(4):
                        last = mm(ps[32 * i:32 * i + 32, 6, j * P:(j + 1) * P], q[:, 64 + 32 * j:96 + 32 * j],
                                  ropeT[:, i * P:(i + 1) * P], start=False, stop=(j == 3), skip_group_check=True)
                last.then_inc(sc_done, 1)

            def cache_values(s):
                out_of_psum(pe, turn_no(s + 1, "p"))
                if s >= 1:
                    pe.wait_ge(op_evac, s)
                for j in range(4):
                    for i in range(4):
                        last = mm(ps[32 * i:32 * i + 32, 7, 0:KVL], dPT[:, j * P + 32 * i:j * P + 32 * i + 32],
                                  cache[s % 3][:, 4 * i + j, :], start=(j == 0), stop=(j == 3))
                last.then_inc(op_done, 1)

            scores(0, 0)
            scores(0, 1)
            pe.wait_ge(ql_evac, 1)
            for n in range(4):
                last = nc.tensor.transpose(ps[:, 7, n * P:(n + 1) * P], qlt[:, n * P:(n + 1) * P], ident[:, :])
            last.then_inc(qlT_done, 1)
            scores(0, 2)
            scores(0, 3)
            for s in range(NH):
                more = s + 1 < NH
                if more:
                    scores(s + 1, 0)
                if s >= 2 and s % 2 == 0:
                    values(s // 2 - 1)
                if s >= 1:
                    turn_cache_probs(s - 1)
                turn_cache(s, 0)
                turn_cache(s, 1)
                turn_head(s, 0)
                if more:
                    scores(s + 1, 1)
                turn_cache(s, 2)
                turn_cache(s, 3)
                turn_head(s, 1)
                if s >= 1:
                    cache_values(s - 1)
                if more:
                    scores(s + 1, 2)
                turn_cache(s, 4)
                turn_cache(s, 5)
                turn_head(s, 2)
                if more:
                    scores(s + 1, 3)
                turn_cache(s, 6)
                turn_cache(s, 7)
                turn_cache(s, 8)
                turn_head(s, 3)
                cache_scores(s)
            values(NH // 2 - 1)
            turn_cache_probs(DEC - 1)
            cache_values(DEC - 1)

            pe.wait_ge(dexp_done, DEC)
            nc.tensor.transpose(ps[0:DEC, 0, 0:P], mx[:, :], ident[:, :])
            nc.tensor.transpose(ps[0:DEC, 0, P:2 * P], ls[:, :], ident[:, :])
            for kc in range(KKV):
                mm(ps[0:DEC, 1, 0:64], kvz[:, kc, SEQ:TOK], qq[:, :, 32 * kc:32 * kc + NH], start=(kc == 0), stop=False)
            mm(ps[0:DEC, 1, 0:64], kpn[:, :], qq[0:32, :, 64:64 + NH], start=False, stop=True).then_inc(f_pe, 1)
            pe.wait_ge(f_dve, 1)
            nc.tensor.transpose(ps[:, 2, 0:DEC], fin[:, 0:P], ident[0:DEC, 0:DEC])
            mm(ps[:, 2, 64:128], ones[0:DEC, :], fin[:, 384:448], start=True, stop=True).then_inc(f_pe, 1)
            pe.wait_ge(f_dve, 2)
            for g in range(4):
                last = mm(ps[32 * g:32 * g + 32, 3, :], sel[:, :], op[:, 2 * g:2 * g + 2, :].rearrange("p a b -> p (a b)"),
                          start=True, stop=True)
            last.then_inc(f_pe, 1)
            pe.wait_ge(f_act, 3)
            for n in range(4):
                last = nc.tensor.transpose(ps[:, 4, n * P:(n + 1) * P], osum[:, n * P:(n + 1) * P], ident[:, :])
            last.then_inc(f_pe, 1)
            landed(pe, uv2_landed)
            pe.wait_ge(f_dve, 3)
            for h in range(NH):
                for kc in range(KKV):
                    last = mm(ps[64 * (h % 2):64 * (h % 2) + 64, 5, 8 * (h // 2):8 * (h // 2) + 8],
                              uv2[:, kc, h * VH:(h + 1) * VH], oT[:, kc, h, :], start=(kc == 0), stop=(kc == KKV - 1))
            last.then_inc(f_pe, 1)

            pe.wait_ge(sq_done, 3)
            for k in range(KR):
                for g in range(4):
                    w, half = g // 2, g % 2
                    last = mm(ps[32 * g:32 * g + 32, 7, 0:WIN], ones[:, 0:32],
                              sq[:, KR * w + k, SHIFT * half:SHIFT * half + WIN], start=(k == 0), stop=(k == KR - 1))
            last.then_inc(d_pe, 1)
            pe.wait_ge(d_act, 1)
            nc.tensor.transpose(ps[:, 6, 0:P], ss[:, 0:P], ident[:, :])
            nc.tensor.transpose(ps[:, 6, P:2 * P], ss[:, P:2 * P], ident[:, :])
            nc.tensor.transpose(ps[0:DEC, 6, 2 * P:3 * P], ss[:, 2 * P:WIN], ident[:, :]).then_inc(d_pe, 1)

            pe.wait_ge(wo_scaled, 1)
            for k in range(KR):
                for g in range(4):
                    w, n = g // 2, g % 2
                    act_in = (attT if w == 0 else recT)[:, k, SEQ:TOK]
                    last = mm(ps[32 * g:32 * g + DEC, 0, :], act_in, wo[:, KR * w + k, n * 512:(n + 1) * 512],
                              start=(k == 0), stop=(k == KR - 1))
            last.then_inc(o_done, 1)

            def turn_x1(m):
                t = [4, 0, 1, 2, 3][m]
                pe.wait_ge(x1_done, m + 1)
                if m == 0:
                    pe.wait_ge(d_act, 2)
                if m > 0:
                    pe.wait_ge(x1T_act, m)
                    pe.wait_ge(x1T_dve, m)
                n = ROWS[t]
                for k in range(KD):
                    last = nc.tensor.transpose(ps[:, 6 + k // 4, (k % 4) * P:(k % 4) * P + n],
                                               x1[0:n, t, k * P:(k + 1) * P], ident[0:n, 0:n])
                last.then_inc(x1T_ps, 1)

            for t in range(4):
                for n in range(2):
                    m = 1 + 2 * t + n
                    b = 2 * (m % 3)
                    if m == 3:
                        pe.wait_ge(d_act, 3)
                    if m > 3:
                        pe.wait_ge(oA_done, m - 3)
                        pe.wait_ge(oR_done, m - 3)
                    for w in range(2):
                        for k in range(KR):
                            last = mm(ps[:, b + w, :], (attT if w == 0 else recT)[:, k, t * P:(t + 1) * P],
                                      wo[:, KR * w + k, n * 512:(n + 1) * 512], start=(k == 0), stop=(k == KR - 1))
                    last.then_inc(o_done, 1)
                if t == 1:
                    turn_x1(0)
                if t >= 2:
                    turn_x1(t - 1)
            turn_x1(3)
            turn_x1(4)

            landed(pe, wr_landed)
            pe.wait_ge(x1T_act, TT)
            pe.wait_ge(x1T_dve, TT)
            pe.wait_ge(oA_done, 8)
            pe.wait_ge(oR_done, 8)
            for k in range(KD):
                for half in range(2):
                    last = mm(ps[64 * half:64 * half + 64, 0, 0:WIN], wr[:, k, :],
                              x1T[:, k, SHIFT * half:SHIFT * half + WIN], start=(k == 0), stop=(k == KD - 1))
            last.then_inc(r_pe, 1)
            pe.wait_ge(r_act, 1)
            nc.tensor.transpose(ps[:, 1, 0:P], rt[:, 0:P], ident[:, :])
            nc.tensor.transpose(ps[:, 1, P:2 * P], rt[:, P:2 * P], ident[:, :])
            nc.tensor.transpose(ps[0:DEC, 1, 2 * P:3 * P], rt[:, 2 * P:WIN], ident[:, :]).then_inc(r_pe, 1)
            pe.wait_ge(r_dve, 1)
            for t in range(TT):
                for q in range(t + 1):
                    mm(ps[:, 2, t * NE:(t + 1) * NE], (trib if q == t else onesb)[:, :], ohb[:, q, :],
                       start=(q == 0), stop=(q == t))
            for q in range(TT):
                last = mm(ps[:, 2, TT * NE:(TT + 1) * NE], onesb[:, :], ohb[:, q, :], start=(q == 0), stop=(q == TT - 1))
            last.then_inc(r_pe, 1)

            pe.wait_ge(pos_ready, 1)
            n_rounds = pe.value_load(rounds[0:1, 0:1], min_val=1, max_val=MAXR)
            turn = [ctx.enter_context(pe.register(f"pe_turn{n}")) for n in range(NPAIR + 1)]
            tokens_in = [ctx.enter_context(pe.register(f"pe_tokens{n}")) for n in range(2)]

            def turn_tokens(q, landings, before):
                pe.wait_ge(pos_ready, 1)
                pe.wait_ge(gathered[q], landings)
                pe.wait_ge(xt_sb, before)
                for k in range(KD):
                    last = nc.tensor.transpose(ps[:, k // 4, (k % 4) * P:(k % 4 + 1) * P],
                                               xg[q][:, k * P:(k + 1) * P], ident[:, :])
                last.then_inc(xt_ps, 1)
            turn_tokens(0, 16, 0)
            with pe.Fori(0, n_rounds * NGRP) as it:
                for n in range(NPAIR + 1):
                    pe.reg_mov(turn[n], it * NPAIR + n)
                for n in range(2):
                    pe.reg_mov(tokens_in[n], it * 16 + 16 * (n + 1))
                for q in range(NPAIR):
                    pe.wait_ge(xt_sb, turn[q + 1])
                    pe.wait_ge(gu_landed[q], it * 32 + 32)
                    for k in range(KD):
                        for e in range(2):
                            last = mm(ps[64 * e:64 * e + 64, 2 + q, :], xgT[:, k, CAP * e:CAP * (e + 1)],
                                      gu_w[2 * q + e][:, k, :], start=(k == 0), stop=(k == KD - 1))
                    last.then_inc(gu_ps, 1)
                    turn_tokens((q + 1) % NPAIR, tokens_in[(q + 1) // NPAIR], turn[q + 1])
                    pe.wait_ge(pos_ready, 1)
                    pe.wait_ge(h_ready, turn[q + 1])
                    for f in range(2):
                        last = nc.tensor.transpose(ps[:, 4, f * P:(f + 1) * P], hx[:, f * P:(f + 1) * P], ident[:, :])
                    last.then_inc(ht_ps, 1)
                    pe.wait_ge(ht_sb, turn[q + 1])
                    pe.wait_ge(dn_landed[q], it * 32 + 32)
                    pe.wait_ge(ya_done, turn[q])
                    pe.wait_ge(yd_done, turn[q])
                    for n in range(2):
                        for f in range(2):
                            for e in range(2):
                                last = mm(ps[64 * e:64 * e + 64, 5 + n, :], hT[:, f, CAP * e:CAP * (e + 1)],
                                          dn_w[2 * q + e][:, f, n * 512:(n + 1) * 512], start=(f == 0), stop=(f == 1))
                    last.then_inc(dn_ps, 1)

            pe.wait_ge(mixer_ready, 1)
            pe.wait_ge(xt_sb, n_rounds * (NGRP * NPAIR) + 1)
            pe.wait_ge(ya_done, n_rounds * (NGRP * NPAIR))
            pe.wait_ge(yd_done, n_rounds * (NGRP * NPAIR))
            for t in range(TT):
                n = ROWS[t]
                landed(pe, y_landed[t], 2)
                if t >= 2:
                    pe.wait_ge(y_sum, t - 1)
                for h in range(2):
                    for w, y in enumerate((y1, y2)):
                        last = mm(ps[0:n, 2 * (t % 2) + h, :], mixer[0:n, w * TT + t, 0:n], y[t][0:n, h * 512:(h + 1) * 512],
                                  start=(w == 0), stop=(w == 1))
                last.then_inc(y_mixed, 1)

        @block.scalar
        def _(act):
            steps = [0]

            def step(ins):
                steps[0] += 1
                ins.then_inc(act_step, 1)

            def settle():
                act.wait_ge(act_step, steps[0])

            fn = nc.scalar.activation
            act.dma_start(vec[:, :], vecs).then_inc(params_landed, 16)
            act.dma_start(cdec[:, :, 0:CONV - 1, :], conv_st).then_inc(params_landed, 16)
            act.dma_start(rst[:, :, :], rec_st).then_inc(params_landed, 16)
            act.dma_start(cs[64:128, :], cs_tab).then_inc(cs_landed, 16)
            act.dma_start(pages[:, :], page_rep).then_inc(pages_landed, 16)
            act.dma_start(lane_sb[:, :], lane).then_inc(pages_landed, 16)
            act.dma_start(id_sb[:, :], ids).then_inc(ids_landed, 16)
            act.dma_start(eoff_sb[:, :], eoff.partition_broadcast(P)).then_inc(ids_landed, 16)
            act.dma_start(rbias[:, :], r_bias.partition_broadcast(P)).then_inc(ids_landed, 16)
            act.wait_ge(lam_ready, 1)
            fn(lam[:, 1, :], lam[:, 0, :], ACT.Exp).then_inc(sp_exp, 1)
            for c in range(KR):
                u = U_RX + c
                b = 2 * (u % 4)
                act.wait_ge(unit_done, u + 1)
                nc.scalar.copy(xp[:, c, 3:3 + HALF], ps[:, b, 0:HALF])
                nc.scalar.copy(xp[:, c, 3 + HALF:3 + SEQ], ps[:, b + 1, 0:SEQ - HALF])
                nc.scalar.copy(cdec[:, c, CONV - 1, :], ps[:, b + 1, SEQ - HALF:HALF]).then_inc(evac[u % 4], 1)
            for k in range(KKV):
                u = U_KV + k
                act.wait_ge(unit_done, u + 1)
                nc.scalar.copy(kvz[:, k, :].rearrange("p (a b) -> p a b", a=2), pair(u)).then_inc(evac[u % 4], 1)
            for k in range(KQ):
                u = U_Q + k
                act.wait_ge(unit_done, u + 1)
                nc.scalar.copy(qz[:, k, :].rearrange("p (a b) -> p a b", a=2), pair(u)).then_inc(evac[u % 4], 1)
            act.wait_ge(lam_ready, 2)
            for c in range(KR):
                u = U_R + c
                act.wait_ge(unit_done, u + 1)
                fn(tr[:, c, :].rearrange("p (a b) -> p a b", a=2), pair(u), ACT.Tanh, bias=bh[:, 0, c:c + 1],
                   scale=0.5).then_inc(evac[u % 4], 1)
            for c in range(KR):
                u = U_I + c
                act.wait_ge(unit_done, u + 1)
                if c == 3:
                    act.wait_ge(ix_done, 1)
                fn(tmp[:, c % 3, :].rearrange("p (a b) -> p a b", a=2), pair(u), ACT.Tanh, bias=bh[:, 1, c:c + 1],
                   scale=0.5).then_inc(evac[u % 4], 1)
            act.wait_ge(conv_done, KR)
            for c in range(KR):
                act.wait_ge(evac[(U_R + c) % 4], (U_R + c) // 4 + 1)
                fn(xp[:, c, :], tr[:, c, :], ACT.Exp, bias=nsp[:, 0, c:c + 1], scale=nsp[:, 0, c:c + 1]).then_inc(a_done, 1)
                act.wait_ge(a_done, c + 1)
                fn(tr[:, c, :], tr[:, c, :], ACT.Tanh, bias=nsp[:, 1, c:c + 1], scale=nsp[:, 1, c:c + 1]).then_inc(th_done, 1)
            for n, (u, dst, width) in enumerate(((U_NQ, rq, QL), (U_NKV, rkv, KVL))):
                act.wait_ge(unit_done, u + 1)
                if n == 0:
                    act.wait_ge(kpe_done, 1)
                fn(dst.rearrange("p (a b) -> p a b", a=2), pair(u), ACT.Sqrt, bias=eps[:, 0:1],
                   scale=1.0 / width).then_inc(evac[u % 4], 1)
            for c in range(KR):
                act.wait_ge(w_done, c + 1)
                fn(tr[:, c, :], tr[:, c, :], ACT.Sqrt, scale=0.25).then_inc(root_w, 1)
            for c in range(KR):
                u = U_G + c
                act.wait_ge(unit_done, u + 1)
                fn(recT[:, c, :].rearrange("p (a b) -> p a b", a=2), pair(u), ACT.Gelu_apprx_tanh).then_inc(evac[u % 4], 1)
            for n in range(4):
                u = U_UK + n
                act.wait_ge(unit_done, u + 1)
                nc.scalar.copy(kh[0:64, 2 * n, :], ps[0:64, 2 * (u % 4), :])
                nc.scalar.copy(kh[0:64, 2 * n + 1, :], ps[64:128, 2 * (u % 4), :]).then_inc(evac[u % 4], 1)
            act.wait_ge(ql_done, 1)
            nc.scalar.copy(qlt, ps[:, 6, :]).then_inc(ql_evac, 1)

            def prob(h, i):
                n = 4 * h + i
                act.wait_ge(nm_done, n + 1)
                if h == 1:
                    act.wait_ge(h_done, KR + 1)
                if h >= 2:
                    act.wait_ge(t_done, turn_no(h - 2, "h3") + 1)
                if n >= 2:
                    act.wait_ge(p_done, n - 1)
                fn(Pb[h % 2][:, OFF[i]:OFF[i] + P * (i + 1)], ps[:, n % 2, 0:P * (i + 1)], ACT.Exp,
                   bias=stat[:, n % 2, 1:2], scale=SM, accum_out=stat[:, n % 2, 2:3]).then_inc(exp_done, 1)

            def head_out(hp):
                act.wait_ge(pv_done, hp + 1)
                nc.scalar.copy(attT[:, hp, 0:SEQ], ps[:, 5, :]).then_inc(att_done, 1)

            def cache_prob(s):
                act.wait_ge(dmx_done, s + 1)
                if s >= 1:
                    act.wait_ge(t_done, turn_no(s, "p") + 1)
                fn(dP, ps[:, 6, :], ACT.Exp, bias=nmd[:, 0:1], scale=SM, accum_out=ls[:, s:s + 1]).then_inc(dexp_done, 1)

            def part_out(s):
                act.wait_ge(op_done, s + 1)
                nc.scalar.copy(op[:, s, :], ps[:, 7, 0:KVL]).then_inc(op_evac, 1)

            for i in range(4):
                prob(0, i)
            for s in range(NH):
                out = lambda what: turned(act, nc.scalar.copy, out_act, s, what)
                more = s + 1 < NH
                if more:
                    prob(s + 1, 0)
                out(0)
                if s >= 2 and s % 2 == 0:
                    head_out(s // 2 - 1)
                out("h0")
                if more:
                    prob(s + 1, 1)
                out(3)
                if more:
                    prob(s + 1, 2)
                if s >= 1:
                    part_out(s - 1)
                out(4)
                out("h2")
                if more:
                    prob(s + 1, 3)
                out(7)
                out("h3")
                cache_prob(s)
            head_out(NH // 2 - 1)
            part_out(DEC - 1)
            act.wait_ge(f_pe, 1)
            nc.scalar.copy(fin[:, 0:256], ps[0:DEC, 0, 0:256]).then_inc(f_act, 1)
            fn(sq[:, KR:KD, :], recT, ACT.Square).then_inc(sq_done, 1)
            act.wait_ge(att_done, NH // 2)
            fn(sq[:, 0:KR, 0:SEQ], attT[:, :, 0:SEQ], ACT.Square).then_inc(sq_done, 1)
            act.wait_ge(diff_ready, 1)
            for n in range(2):
                a = fin[:, 448 + 0:456] if n else fin[:, 256:384].rearrange("p (i h) -> p i h", i=4)[:, :, 0:NH]
                last = fn(a, a, ACT.Exp, scale=SM)
            last.then_inc(f_act, 1)
            act.wait_ge(f_pe, 3)
            nc.scalar.copy(osum, ps[:, 3, :]).then_inc(f_act, 1)
            act.wait_ge(f_pe, 5)
            for hp in range(4):
                last = nc.scalar.copy(attT[:, hp, SEQ:TOK], ps[:, 5, 8 * hp:8 * hp + 8])
            last.then_inc(f_act, 1)
            act.wait_ge(f_act, 4)
            fn(sq[:, 0:KR, SEQ:TOK], attT[:, :, SEQ:TOK], ACT.Square).then_inc(sq_done, 1)

            act.wait_ge(d_pe, 1)
            nc.scalar.copy(ss, ps[:, 7, 0:WIN]).then_inc(d_act, 1)
            act.wait_ge(d_pe, 2)
            for tt in range(2):
                fn(rinv[:, :, :, tt], ps[:, 6, tt * P:(tt + 1) * P].rearrange("p (w h x) -> p w h x", w=2, h=2)[:, :, :, 0],
                   ACT.Sqrt, bias=eps[:, 0:1], scale=1.0 / REC)
            fn(rinv4[:, :], ps[0:DEC, 6, 2 * P:3 * P].rearrange("p (w h x) -> p w h x", w=2, h=2)[:, :, 1, 0],
               ACT.Sqrt, bias=eps[0:DEC, 0:1], scale=1.0 / REC).then_inc(d_act, 1)
            act.wait_ge(o_done, 1)
            for g in range(4):
                last = nc.scalar.copy(tb[g // 2][0:DEC, (g % 2) * 512:(g % 2 + 1) * 512], ps[32 * g:32 * g + DEC, 0, :])
            last.then_inc(d_act, 1)

            def ln_act(n, rows, root_sem, norm_sem, var_sem, x, out):
                act.wait_ge(var_sem, 2 * n + 1)
                fn(mv[0:rows, n % 2, 2:3], mv[0:rows, n % 2, 1:2], ACT.Sqrt, bias=eps[0:rows, 1:2]).then_inc(root_sem, 1)
                act.wait_ge(var_sem, 2 * n + 2)
                fn(out, x, ACT.Identity, bias=mv[0:rows, n % 2, 3:4], scale=mv[0:rows, n % 2, 2:3]).then_inc(norm_sem, 1)

            def x1T_out(m):
                t = [4, 0, 1, 2, 3][m]
                act.wait_ge(x1T_ps, m + 1)
                nc.scalar.copy(x1T[:, 0:4, P * t:P * t + ROWS[t]],
                               ps[:, 6, :].rearrange("p (k n) -> p k n", k=4)[:, :, 0:ROWS[t]]).then_inc(x1T_act, 1)

            ln_act(0, DEC, ln_root, ln_norm, ln_var, x1[0:DEC, 4, :], x1[0:DEC, 4, :])
            for t in range(4):
                for n in range(2):
                    m = 1 + 2 * t + n
                    act.wait_ge(o_done, m + 1)
                    act.wait_ge(d_dve, 1)
                    act.wait_ge(x1_sum, t if t else 1)
                    fn(tb[t % 2][:, n * 512:(n + 1) * 512], ps[:, 2 * (m % 3), :], ACT.Identity,
                       scale=rinv[:, 0, t // 2, t % 2:t % 2 + 1]).then_inc(oA_done, 1)
                ln_act(t + 1, P, ln_root, ln_norm, ln_var, x1[:, t, :], x1[:, t, :])
                if t == 1:
                    x1T_out(0)
                if t >= 2:
                    x1T_out(t - 1)
            x1T_out(3)
            x1T_out(4)
            act.wait_ge(r_pe, 1)
            nc.scalar.copy(rt, ps[:, 0, 0:WIN]).then_inc(r_act, 1)
            act.wait_ge(r_dve, 2)
            fn(rt_t[:, :, 0:NG], rt_t[:, :, 0:NG], ACT.Exp).then_inc(r_act, 1)
            act.wait_ge(r_dve, 3)
            fn(rs[:, 6:8, :], rs[:, 6:8, :], ACT.Exp).then_inc(r_act, 1)

            landed(act, x1_stored, TT)
            act.wait_ge(r_pe, 1)
            for t in range(TT):
                last = nc.scalar.mul(x1[0:ROWS[t], t, :], x1[0:ROWS[t], t, :], ALPHA)
            last.then_inc(mixer_in, 1)

            act.wait_ge(pos_ready, 1)
            n_rounds = act.value_load(rounds[0:1, 0:1], min_val=1, max_val=MAXR)
            with act.Fori(0, n_rounds * NGRP) as it:
                for q in range(NPAIR):
                    t = it * NPAIR + q
                    act.wait_ge(gu_ps, t + 1)
                    fn(sg, ps[:, 2 + q, 0:DE], ACT.Silu).then_inc(silu_done, 1)
                    act.wait_ge(ht_ps, t + 1)
                    nc.scalar.copy(hT, ps[:, 4, 0:2 * P].rearrange("p (f n) -> p f n", f=2)).then_inc(ht_sb, 1)
                    act.wait_ge(dn_ps, t + 1)
                    act.wait_ge(scattered[q], it * 16)
                    nc.scalar.copy(yb[q][:, 0:512], ps[:, 5, :]).then_inc(ya_done, 1)

            for t in range(TT):
                n = ROWS[t]
                if t >= 2:
                    act.wait_ge(g2_done, t - 1)
                b = 4 + 2 * (t % 2)
                ln_act(t, n, root2, n2_done, v2_done, x1[0:n, t, :].rearrange("p (a b) -> p a b", a=2), ps[0:n, b:b + 2, :])

        @block.vector
        def _(dve):
            steps = [0]

            def step(ins):
                steps[0] += 1
                ins.then_inc(dve_step, 1)

            def settle():
                dve.wait_ge(dve_step, steps[0])

            def link(ins):
                step(ins)
                settle()

            V = nc.vector
            tt, ts, stt = V.tensor_tensor, V.tensor_scalar, V.scalar_tensor_tensor
            V.memset(ones[:, :], 1.0).then_inc(ones_ready, 1)
            step(V.memset(eps[:, 0:1], RMS_EPS))
            step(V.memset(eps[:, 1:2], LN_EPS))
            step(V.memset(xp[:, :, 0:3], 0.0))
            landed(dve, params_landed, 3)
            lam_in = vec[:, V_LAM:V_LAM + KR]
            link(ts(lam[:, 0, :], lam_in, -1.0, None, ALU.mult))
            link(tt(lam[:, 2, :], lam[:, 0, :], lam_in, ALU.max))
            ts(lam[:, 0, :], lam[:, 2, :], -1.0, None, ALU.mult).then_inc(lam_ready, 1)
            dve.wait_ge(sp_exp, 1)
            link(ts(lam[:, 2, :], lam[:, 1, :], 2.0, None, ALU.add))
            link(V.reciprocal(lam[:, 2, :], lam[:, 2, :]))
            link(tt(lam[:, 2, :], lam[:, 1, :], lam[:, 2, :], ALU.mult))
            link(tt(lam[:, 3, :], lam[:, 2, :], lam[:, 2, :], ALU.mult))
            link(V.memset(lam[:, 4, :], 1.0 / 17))
            for n in range(15, 0, -2):
                link(tt(lam[:, 4, :], lam[:, 4, :], lam[:, 3, :], ALU.mult))
                link(ts(lam[:, 4, :], lam[:, 4, :], 1.0 / n, None, ALU.add))
            link(tt(lam[:, 4, :], lam[:, 4, :], lam[:, 2, :], ALU.mult))
            link(ts(lam[:, 5, :], lam_in, -1.0, 0.0, ALU.mult, ALU.max))
            link(stt(lam[:, 4, :], lam[:, 4, :], 2.0, lam[:, 5, :], ALU.mult, ALU.add))
            step(ts(nsp[:, 0, :], lam[:, 4, :], -4.0, None, ALU.mult))
            step(ts(nsp[:, 1, :], lam[:, 4, :], 4.0, None, ALU.mult))
            step(ts(bh[:, 0, :], vec[:, V_BR:V_BR + KR], 0.5, None, ALU.mult))
            ts(bh[:, 1, :], vec[:, V_BI:V_BI + KR], 0.5, None, ALU.mult).then_inc(lam_ready, 1)
            landed(dve, pages_landed, 2)
            link(ts(pages[:, :], pages[:, :], 8, None, ALU.mult))
            tt(pages[:, :], pages[:, :], lane_sb[:, 0:1].broadcast_to([P, DEC]), ALU.add).then_inc(cidx_ready, 1)
            settle()
            for c in range(KR):
                u = U_RX + c
                dve.wait_ge(evac[u % 4], u // 4 + 1)
                step(V.tensor_copy(conv_tail[:, c, :], xp[:, c, SEQ:SEQ + 3]))
                w = vec[:, V_CW + CONV * c:V_CW + CONV * (c + 1)]
                step(ts(xc[:, c, 0:SEQ], xp[:, c, 0:SEQ], w[:, 0:1], vec[:, V_CB + c:V_CB + c + 1], ALU.mult, ALU.add))
                step(ts(xc[:, c, SEQ:TOK], cdec[:, c, 0, :], w[:, 0:1], vec[:, V_CB + c:V_CB + c + 1], ALU.mult, ALU.add))
                for k in range(1, CONV):
                    settle()
                    step(stt(xc[:, c, 0:SEQ], xp[:, c, k:k + SEQ], w[:, k:k + 1], xc[:, c, 0:SEQ], ALU.mult, ALU.add))
                    last = stt(xc[:, c, SEQ:TOK], cdec[:, c, k, :], w[:, k:k + 1], xc[:, c, SEQ:TOK], ALU.mult, ALU.add)
                    if k + 1 < CONV:
                        step(last)
                last.then_inc(conv_done, 1)
            landed(dve, cs_landed)
            dve.wait_ge(unit_done, U_KPE + 1)
            two = lambda a: a.rearrange("p (a b) -> p a b", a=2)
            b = 2 * (U_KPE % 4)
            step(tt(two(rq[64:96, :]), ps[96:128, b:b + 2, 0:HALF], two(cs[96:128, :]), ALU.mult))
            tt(two(kpe[64:96, :]), ps[64:96, b:b + 2, 0:HALF], two(cs[64:96, :]), ALU.mult).then_inc(evac[U_KPE % 4], 1)
            settle()
            dve.wait_ge(evac[U_KPE % 4], U_KPE // 4 + 1)
            tt(kpe[64:96, :], kpe[64:96, :], rq[64:96, :], ALU.add).then_inc(kpe_done, 1)
            for c in range(KR):
                u = U_I + c
                dve.wait_ge(evac[u % 4], u // 4 + 1)
                stt(xc[:, c, :], tmp[:, c % 3, :], 1.0, xc[:, c, :], ALU.add, ALU.mult).then_inc(ix_done, 1)
            for c in range(KR):
                dve.wait_ge(th_done, c + 1)
                dve.wait_ge(a2_done, c + 1)
                stt(tr[:, c, :], tmp[:, c % 3, :], 1.0, tr[:, c, :], ALU.add, ALU.mult).then_inc(w_done, 1)
            dve.wait_ge(evac[U_NQ % 4], U_NQ // 4 + 1)
            link(V.reciprocal(rq, rq))
            tt(rq[64:128, :], rq[64:128, :], cs[64:128, :], ALU.mult).then_inc(rq_done, 1)
            dve.wait_ge(evac[U_NKV % 4], U_NKV // 4 + 1)
            link(V.reciprocal(rkv, rkv))
            step(stt(kvz[:, 0, :], kvz[:, 0, :], vec[:, V_KVG:V_KVG + 1], rkv, ALU.mult, ALU.mult))
            stt(kvz[:, 1, :], kvz[:, 1, :], vec[:, V_KVG + 1:V_KVG + 2], rkv, ALU.mult, ALU.mult).then_inc(ckv_done, 1)
            for c in range(KR):
                dve.wait_ge(root_w, c + 1)
                dve.wait_ge(ix_done, c + 1)
                link(tt(xc[:, c, :], tr[:, c, :], xc[:, c, :], ALU.mult))
                V.tensor_tensor_scan(xc[:, c, 0:SEQ], xp[:, c, 0:SEQ], xc[:, c, 0:SEQ], 0.0, ALU.mult,
                                     ALU.add).then_inc(h_done, 1)
            dve.wait_ge(h_done, KR)
            step(V.tensor_copy(rec_last[:, :], xc[:, :, SEQ - 1]))
            link(tt(rst[:, :, :], xp[:, :, SEQ:TOK], rst[:, :, :], ALU.mult))
            tt(xc[:, :, SEQ:TOK], xc[:, :, SEQ:TOK], rst[:, :, :], ALU.add).then_inc(h_done, 1)
            dve.wait_ge(rq_done, 1)
            for h in range(NH):
                u = U_UQ + h
                b = 2 * (u % 4)
                dve.wait_ge(unit_done, u + 1)
                if h >= 2:
                    dve.wait_ge(qrope_done, h - 1)
                step(tt(two(qh[0:64, h, :]), ps[0:64, b:b + 2, 0:HALF], two(rq[0:64, :]), ALU.mult))
                step(tt(two(tmp[64:96, h % 2, :]), ps[96:128, b:b + 2, 0:HALF], two(rq[96:128, :]), ALU.mult))
                tt(two(qh[64:96, h, :]), ps[64:96, b:b + 2, 0:HALF], two(rq[64:96, :]), ALU.mult).then_inc(evac[u % 4], 1)
            for n in range(4):
                u = U_V + n
                dve.wait_ge(unit_done, u + 1)
                V.tensor_copy(v[:, n, :], ps[:, 2 * (u % 4), :]).then_inc(evac[u % 4], 1)
            def absorbed_queries():
                dve.wait_ge(rec_done, KR)
                landed(dve, outs_stored, 6)
                step(V.memset(qq[:, :, :], 0.0))
                dve.wait_ge(qrope_done, NH)
                settle()
                for j in range(4):
                    step(V.tensor_copy(qq[32 * j:32 * j + 32, :, 64 + 32 * j:64 + 32 * j + NH],
                                       qh[64:96, :, SEQ:TOK].rearrange("p h s -> p s h")))
                step(V.tensor_copy(kpn[:, :], kpe[64:96, SEQ:TOK]))
                dve.wait_ge(qlT_done, 1)
                for hi in range(2):
                    for kc in range(KKV):
                        n = 2 * hi + kc
                        last = V.tensor_copy(qq[:, :, 32 * kc + 4 * hi:32 * kc + 4 * hi + 4],
                                             ps[:, 7, n * P:(n + 1) * P].rearrange("p (g x) -> p x g", g=4)[:, 32 - DEC:32, :])
                        if n < 3:
                            step(last)
                last.then_inc(qq_done, 1)

            def row_max(h, i):
                n = 4 * h + i
                dve.wait_ge(s_done, n + 1)
                link(V.tensor_reduce(stat[:, n % 2, 0:1], ps[:, n % 2, 0:P * (i + 1)], AX_X, ALU.max))
                if n >= 2:
                    dve.wait_ge(exp_done, n - 1)
                ts(stat[:, n % 2, 1:2], stat[:, n % 2, 0:1], -SM, None, ALU.mult).then_inc(nm_done, 1)

            def normal(h, i):
                n = 4 * h + i
                dve.wait_ge(exp_done, n + 1)
                link(V.reciprocal(stat[:, n % 2, 3:4], stat[:, n % 2, 2:3]))
                pr = Pb[h % 2][:, OFF[i]:OFF[i] + P * (i + 1)]
                ts(pr, pr, stat[:, n % 2, 3:4], None, ALU.mult).then_inc(p_done, 1)

            def queries_of(s):
                if s >= 2:
                    dve.wait_ge(sc_done, s - 1)
                V.tensor_copy(qs[:, s % 2, :], qq[:, s, :]).then_inc(qs_done, 1)

            def cache_max(s):
                dve.wait_ge(sc_done, s + 1)
                V.tensor_reduce(mx[:, s:s + 1], ps[:, 6, :], AX_X, ALU.max).then_inc(dmax_raw, 1)
                dve.wait_ge(dmax_raw, s + 1)
                if s >= 1:
                    dve.wait_ge(dexp_done, s)
                ts(nmd[:, 0:1], mx[:, s:s + 1], -SM, None, ALU.mult).then_inc(dmx_done, 1)

            row_max(0, 0)
            for i in range(1, 4):
                row_max(0, i)
                normal(0, i - 1)
            normal(0, 3)
            absorbed_queries()
            dve.wait_ge(qq_done, 1)
            for s in range(NH):
                out = lambda what: turned(dve, V.tensor_copy, out_dve, s, what)
                more = s + 1 < NH
                queries_of(s)
                if more:
                    row_max(s + 1, 0)
                if s >= 1:
                    out("p")
                out(1)
                if more:
                    row_max(s + 1, 1)
                    normal(s + 1, 0)
                out(2)
                out("h1")
                if more:
                    row_max(s + 1, 2)
                    normal(s + 1, 1)
                out(5)
                if more:
                    row_max(s + 1, 3)
                    normal(s + 1, 2)
                out(6)
                out(8)
                if more:
                    normal(s + 1, 3)
                cache_max(s)
            turned(dve, V.tensor_copy, out_dve, DEC, "p")
            dve.wait_ge(const_ready, 5)
            step(V.tensor_reduce(sel[:, :], ident[:, :].rearrange("p (b m) -> p m b", b=4), AX_X, ALU.add))
            e8 = ident[0:DEC, 0:DEC].unsqueeze(2).broadcast_to([DEC, DEC, NH])
            snew, M, LL, wn = fin[:, 448:456], fin[:, 456:464], fin[:, 464:472], fin[:, 448:456]
            sd = fin[:, 384:448].rearrange("p (s h) -> p s h", s=DEC)
            parts = lambda at: fin[:, at:at + P].rearrange("p (i h) -> p i h", i=4)[:, :, 0:NH]
            dve.wait_ge(f_pe, 1)
            link(tt(sd, ps[0:DEC, 1, 0:64].rearrange("p (s h) -> p s h", s=DEC), e8, ALU.mult))
            link(V.tensor_reduce(snew, sd.rearrange("p s h -> p h s"), AX_X, ALU.add))
            dve.wait_ge(f_act, 1)
            link(V.tensor_reduce(M, parts(0).rearrange("p i h -> p h i"), AX_X, ALU.max))
            link(tt(M, M, snew, ALU.max))
            step(V.memset(fin[:, 256:384], 0.0))
            settle()
            step(tt(parts(256), parts(0), M.unsqueeze(1).broadcast_to([DEC, 4, NH]), ALU.subtract))
            tt(wn, snew, M, ALU.subtract).then_inc(diff_ready, 1)
            dve.wait_ge(f_act, 2)
            link(tt(parts(128), parts(128), parts(256), ALU.mult))
            link(V.tensor_reduce(LL, parts(128).rearrange("p i h -> p h i"), AX_X, ALU.add))
            link(tt(LL, LL, wn, ALU.add))
            link(V.reciprocal(LL, LL))
            step(V.memset(fin[:, 0:P], 0.0))
            link(tt(wn, wn, LL, ALU.mult))
            step(tt(parts(0), parts(256), LL.unsqueeze(1).broadcast_to([DEC, 4, NH]), ALU.mult))
            settle()
            tt(sd, e8, wn.unsqueeze(1).broadcast_to([DEC, DEC, NH]), ALU.mult).then_inc(f_dve, 1)
            dve.wait_ge(f_pe, 2)
            link(V.tensor_copy(wcol[:, :], ps[:, 2, 0:DEC]))
            for kc in range(KKV):
                step(tt(tn[:, kc, :, :], ps[:, 2, 64:128].rearrange("p (s h) -> p s h", s=DEC),
                        kvz[:, kc, SEQ:TOK].unsqueeze(2).broadcast_to([P, DEC, NH]), ALU.mult))
            dve.wait_ge(op_evac, DEC)
            for s in range(DEC):
                last = ts(op[:, s, :], op[:, s, :], wcol[:, s:s + 1], None, ALU.mult)
                if s < DEC - 1:
                    step(last)
            last.then_inc(f_dve, 1)
            dve.wait_ge(f_pe, 4)
            settle()
            for s1 in range(2):
                for kc in range(KKV):
                    n = 2 * s1 + kc
                    last = tt(oT[:, kc, :, s1:DEC:2].rearrange("p h g -> p g h"),
                              ps[:, 4, n * P:(n + 1) * P].rearrange("p (g x) -> p g x", g=4)[:, :, 0:NH],
                              tn[:, kc, s1:DEC:2, :], ALU.add)
                    if n < 3:
                        step(last)
            last.then_inc(f_dve, 1)

            dve.wait_ge(d_act, 2)
            step(V.reciprocal(rinv[:, :, :, :].rearrange("p a b c -> p (a b c)"), rinv[:, :, :, :].rearrange("p a b c -> p (a b c)")))
            V.reciprocal(rinv4[:, :], rinv4[:, :]).then_inc(d_dve, 1)

            def ln_stats(x, n, rows, root_sem, var_sem):
                for q in range(2):
                    step(V.bn_stats(bn[0:rows, q, :], x[:, q * 512:(q + 1) * 512]))
                settle()
                V.bn_aggr(mv[0:rows, n % 2, 0:2], bn[0:rows, :, :]).then_inc(var_sem, 1)
                dve.wait_ge(root_sem, n + 1)
                link(V.reciprocal(mv[0:rows, n % 2, 2:3], mv[0:rows, n % 2, 2:3]))
                stt(mv[0:rows, n % 2, 3:4], mv[0:rows, n % 2, 0:1], -1.0, mv[0:rows, n % 2, 2:3], ALU.mult,
                    ALU.mult).then_inc(var_sem, 1)

            def ln_dve(x, n, rows):
                ln_stats(x, n, rows, ln_root, ln_var)
                dve.wait_ge(ln_norm, n + 1)
                link(tt(x, x, lng[0:rows, 0, :], ALU.mult))
                tt(x, x, lng[0:rows, 1, :], ALU.add).then_inc(x1_done, 1)

            dve.wait_ge(d_act, 3)
            dve.wait_ge(d_dve, 1)
            link(ts(tb[0][0:DEC, :], tb[0][0:DEC, :], rinv4[:, 0:1], None, ALU.mult))
            link(stt(tb[0][0:DEC, :], tb[1][0:DEC, :], rinv4[:, 1:2], tb[0][0:DEC, :], ALU.mult, ALU.add))
            dve.wait_ge(xa_done, 1)
            tt(x1[0:DEC, 4, :], x1[0:DEC, 4, :], tb[0][0:DEC, :], ALU.add).then_inc(x1_sum, 1)
            dve.wait_ge(x1_sum, 1)
            landed(dve, ln1_landed)
            ln_dve(x1[0:DEC, 4, :], 0, DEC)

            def x1T_out(m):
                t = [4, 0, 1, 2, 3][m]
                dve.wait_ge(x1T_ps, m + 1)
                V.tensor_copy(x1T[:, 4:8, P * t:P * t + ROWS[t]],
                              ps[:, 7, :].rearrange("p (k n) -> p k n", k=4)[:, :, 0:ROWS[t]]).then_inc(x1T_dve, 1)

            for t in range(4):
                for n in range(2):
                    m = 1 + 2 * t + n
                    dve.wait_ge(oA_done, m)
                    cols = slice(n * 512, (n + 1) * 512)
                    stt(tb[t % 2][:, cols], ps[:, 2 * (m % 3) + 1, :], rinv[:, 1, t // 2, t % 2:t % 2 + 1],
                        tb[t % 2][:, cols], ALU.mult, ALU.add).then_inc(oR_done, 1)
                dve.wait_ge(oR_done, 2 * t + 2)
                tt(x1[:, t, :], x1[:, t, :], tb[t % 2], ALU.add).then_inc(x1_sum, 1)
                dve.wait_ge(x1_sum, t + 2)
                ln_dve(x1[:, t, :], t + 1, P)
                if t == 1:
                    x1T_out(0)
                if t >= 2:
                    x1T_out(t - 1)
            x1T_out(3)
            x1T_out(4)

            landed(dve, ids_landed, 3)
            link(V.memset(L[:, :, :], 0.0))
            step(V.memset(gpad[:, :, NG:8], -3e38))
            link(V.memset(valid[:, 0:4], 1.0))
            link(V.memset(valid[:, 4:5], 0.0))
            link(V.memset(valid[0:DEC, 4:5], 1.0))
            dve.wait_ge(r_pe, 2)
            for n in range(2):
                step(V.tensor_copy(L[:, 0:4, :].rearrange("p (h t) n -> p t h n", h=2)[:, n],
                                   ps[:, 1, n * P:(n + 1) * P].rearrange("p (h x) -> p h x", h=2)[:, :, 0:NG + NE]))
            link(V.tensor_copy(L[0:DEC, 4, :], ps[0:DEC, 1, 2 * P + 64:2 * P + 64 + NG + NE]))
            bc = lambda a, n: a.unsqueeze(1).broadcast_to([P, TT, n])
            per = lambda a, n: a.unsqueeze(2).broadcast_to([P, TT, n])
            link(tt(Lb, L, bc(rbias[:, :], NG + NE), ALU.add))
            link(V.tensor_copy(gpad[:, :, 0:NG], Lb[:, :, 0:NG]))
            for t in range(TT):
                step(V.max(top8[:, t, :], gpad[:, t, :]))
            settle()
            for t in range(TT):
                step(V.max_index(idx8[:, t, :], top8[:, t, :], gpad[:, t, :]))
            settle()
            link(V.tensor_copy(rs[:, 0, :], idx8[:, :, 0]))
            link(tt(ohg[:, :, :], bc(eoff_sb[:, 0:NG], NG), per(rs[:, 0, :], NG), ALU.is_equal))
            link(ts(rt_t[:, :, 0:NG], ohg[:, :, :], 1.0, 1e30, ALU.subtract, ALU.mult))
            for t in range(TT):
                step(tt(me[:, t, :].rearrange("p (g e) -> p g e", g=NG), Lb[:, t, NG:].rearrange("p (g e) -> p g e", g=NG),
                        rt_t[:, t, 0:NG].unsqueeze(2).broadcast_to([P, NG, EPG]), ALU.add))
            settle()
            for t in range(TT):
                step(V.max(top8[:, t, :], me[:, t, :]))
            settle()
            for t in range(TT):
                step(V.max_index(idx8[:, t, :], top8[:, t, :], me[:, t, :]))
            settle()
            step(V.tensor_copy(rs[:, 1, :], idx8[:, :, 0]))
            link(V.tensor_copy(rs[:, 2, :], idx8[:, :, 1]))
            step(tt(oh1, bc(eoff_sb[:, 0:NE], NE), per(rs[:, 1, :], NE), ALU.is_equal))
            link(tt(oh2, bc(eoff_sb[:, 0:NE], NE), per(rs[:, 2, :], NE), ALU.is_equal))
            link(tt(me, oh1, oh2, ALU.add))
            tt(ohb[:, :, :], me, per(valid[:, :], NE), ALU.mult).then_inc(r_dve, 1)
            dve.wait_ge(r_dve, 1)
            both = part(arena_s, S_RT + 520, 2, TT, NE)
            prod = part(arena_s, S_ATT, 2, TT, NE)
            bc2 = lambda a: a.unsqueeze(1).broadcast_to([P, 2, TT, NE])
            link(tt(prod, both, bc2(bc(eoff_sb[:, NE:2 * NE], NE)), ALU.mult))
            link(V.tensor_reduce(rs[:, 14:16, :], prod, AX_X, ALU.add))
            step(V.tensor_copy(posj[:, :, :], rs[:, 14:16, :]))
            dve.wait_ge(r_pe, 3)
            step(V.tensor_reduce(rs[:, 13, 0:1], ps[:, 2, TT * NE:(TT + 1) * NE], AX_X, ALU.max))
            link(tt(prod, both, bc2(ps[:, 2, 0:TT * NE].rearrange("p (t e) -> p t e", t=TT)), ALU.mult))
            link(V.tensor_reduce(rs[:, 14:16, :], prod, AX_X, ALU.add))
            link(V.tensor_copy(posi[:, :, :], rs[:, 14:16, :]))
            link(stt(posj[:, :, :], posi[:, :, :], float(NPAIR), posj[:, :, :], ALU.mult, ALU.add))
            link(ts(posi[:, :, :], posi[:, :, :], 6, None, ALU.arith_shift_right))
            link(stt(posi[:, :, :], posi[:, :, :], float(NGRP * BLK - CAP * NPAIR), posj[:, :, :], ALU.mult, ALU.add))
            link(ts(rs[:, 13, 1:2], rs[:, 13, 0:1], float(CAP - 1), None, ALU.add))
            link(V.tensor_copy(rounds[:, 1:2], rs[:, 13, 1:2]))
            ts(rounds[:, 0:1], rounds[:, 1:2], 6, None, ALU.arith_shift_right).then_inc(pos_ready, 1)
            link(V.tensor_reduce(rs[:, 3, :], L[:, :, 0:NG], AX_X, ALU.max))
            tt(rt_t[:, :, 0:NG], L[:, :, 0:NG], per(rs[:, 3, :], NG), ALU.subtract).then_inc(r_dve, 1)
            link(tt(me, oh1, L[:, :, NG:], ALU.mult))
            link(V.tensor_reduce(rs[:, 4, :], me, AX_X, ALU.add))
            link(tt(me, oh2, L[:, :, NG:], ALU.mult))
            link(V.tensor_reduce(rs[:, 5, :], me, AX_X, ALU.add))
            link(tt(rs[:, 8, :], rs[:, 4, :], rs[:, 5, :], ALU.max))
            step(tt(rs[:, 6, :], rs[:, 4, :], rs[:, 8, :], ALU.subtract))
            tt(rs[:, 7, :], rs[:, 5, :], rs[:, 8, :], ALU.subtract).then_inc(r_dve, 1)
            dve.wait_ge(r_dve, 3)
            dve.wait_ge(r_act, 2)
            link(V.tensor_reduce(rs[:, 8, :], rt_t[:, :, 0:NG], AX_X, ALU.add))
            link(tt(rt_t[:, :, 0:NG], rt_t[:, :, 0:NG], ohg[:, :, :], ALU.mult))
            link(V.tensor_reduce(rs[:, 9, :], rt_t[:, :, 0:NG], AX_X, ALU.add))
            dve.wait_ge(r_act, 3)
            link(tt(rs[:, 12, :], rs[:, 6, :], rs[:, 7, :], ALU.add))
            link(tt(rs[:, 12, :], rs[:, 12, :], rs[:, 8, :], ALU.mult))
            link(V.reciprocal(rs[:, 12, :], rs[:, 12, :]))
            link(tt(rs[:, 12, :], rs[:, 12, :], rs[:, 9, :], ALU.mult))
            step(tt(rs[:, 10, :], rs[:, 12, :], rs[:, 6, :], ALU.mult))
            link(tt(rs[:, 11, :], rs[:, 12, :], rs[:, 7, :], ALU.mult))

            dve.wait_ge(pos_ready, 1)
            n_rounds = dve.value_load(rounds[0:1, 0:1], min_val=1, max_val=MAXR)
            for n in range(2):
                for t in range(TT):
                    last = ts(mixer[:, n * TT + t, :], ident[:, :], rs[:, 10 + n, t:t + 1], None, ALU.mult)
                    if n * TT + t < 2 * TT - 1:
                        step(last)
            last.then_inc(mixer_ready, 1)

            def tokens_out(t):
                dve.wait_ge(xt_ps, t + 1)
                dve.wait_ge(gu_ps, t)
                V.tensor_copy(xgT.rearrange("p (a b) n -> p a b n", a=2),
                              ps[:, 0:2, :].rearrange("p a (b n) -> p a b n", b=4)).then_inc(xt_sb, 1)
            tokens_out(0)
            with dve.Fori(0, n_rounds * NGRP) as it:
                for q in range(NPAIR):
                    t = it * NPAIR + q
                    dve.wait_ge(silu_done, t + 1)
                    tt(hx, sg, ps[:, 2 + q, DE:2 * DE], ALU.mult).then_inc(h_ready, 1)
                    tokens_out(t + 1)
                    dve.wait_ge(dn_ps, t + 1)
                    dve.wait_ge(scattered[q], it * 16)
                    V.tensor_copy(yb[q][:, 512:D], ps[:, 6, :]).then_inc(yd_done, 1)

            landed(dve, ln2_landed)
            dve.wait_ge(mixer_in, 1)

            def total(t):
                n, b = ROWS[t], 2 * (t % 2)
                x = x1[0:n, t, :].rearrange("p (a b) -> p a b", a=2)
                dve.wait_ge(y_mixed, t + 1)
                tt(x, ps[0:n, b:b + 2, :], x, ALU.add).then_inc(y_sum, 1)
                dve.wait_ge(y_sum, t + 1)

            def gain(t):
                n, b = ROWS[t], 4 + 2 * (t % 2)
                dve.wait_ge(n2_done, t + 1)
                tt(y1[t][0:n, :].rearrange("p (a b) -> p a b", a=2), ps[0:n, b:b + 2, :],
                   lng2[0:n, 0, :].rearrange("p (a b) -> p a b", a=2), ALU.mult).then_inc(g2_done, 1)

            for t in range(TT):
                total(t)
                ln_stats(x1[0:ROWS[t], t, :], t, ROWS[t], root2, v2_done)
                if t > 0:
                    gain(t - 1)
            gain(TT - 1)

        @block.gpsimd
        def _(pool):
            G = nc.gpsimd
            steps = [0]

            def step(ins):
                steps[0] += 1
                ins.then_inc(pool_step, 1)

            def settle():
                pool.wait_ge(pool_step, steps[0])

            step(G.memset(ident[:, :], 0.0))
            step(G.memset(identb[:, :], 0.0))
            step(G.memset(maskb[:, :], 0.0))
            step(G.memset(trib[:, :], 1.0))
            step(G.memset(onesb[:, :], 1.0))
            settle()
            for m in (ident, identb):
                G.affine_select(out=m[:, :], in_=m[:, :], compare_op=ALU.not_equal, fill=1.0, base=0,
                                pattern=[[-1, P]], channel_multiplier=1).then_inc(const_ready, 1)
            G.affine_select(out=maskb[:, :], in_=maskb[:, :], compare_op=ALU.is_ge, fill=NEG, base=0,
                            pattern=[[-1, P]], channel_multiplier=1).then_inc(const_ready, 1)
            G.affine_select(out=trib[:, :], in_=trib[:, :], compare_op=ALU.is_gt, fill=0.0, base=0,
                            pattern=[[1, P]], channel_multiplier=-1).then_inc(const_ready, 1)
            G.memset(empty[:, :], FREE_SLOT).then_inc(const_ready, 1)
            landed(pool, params_landed, 3)
            for k in range(KKV):
                u = U_KV + k
                pool.wait_ge(evac[u % 4], u // 4 + 1)
            G.tensor_tensor(sq0[:, KQ:KQ + KKV, :], kvz, kvz, ALU.mult).then_inc(squares, 1)
            for k in range(KQ):
                u = U_Q + k
                pool.wait_ge(evac[u % 4], u // 4 + 1)
            G.tensor_tensor(sq0[:, 0:KQ, :], qz, qz, ALU.mult).then_inc(squares, 1)
            pool.wait_ge(ix_done, KR)
            for c in range(KR):
                pool.wait_ge(a_done, c + 1)
                if c == 3:
                    pool.wait_ge(w_done, 1)
                G.tensor_tensor(tmp[:, c % 3, :], xp[:, c, :], xp[:, c, :], ALU.mult).then_inc(a2_done, 1)
            pool.wait_ge(unit_done, U_Q + KQ)
            pool.wait_ge(cidx_ready, 1)

            def fetch(s):
                for rows, dst in ((kv_rows, buf[s % 3][:, 0:16 * KVL]), (rope_rows, buf[s % 3][:, 16 * KVL:CB])):
                    G.indirect_dma_start(out=dst, out_offset=None, in_=rows,
                                         in_offset=bass.IndirectOffsetOnAxis(ap=pages[:, s:s + 1], axis=0)).then_inc(cache_landed[s % 3], 16)
            fetch(0)
            fetch(1)
            landed(pool, uq_landed)
            for k in range(KQ):
                last = G.tensor_scalar(uq[:, k, :, :], uq[:, k, :, :], vec[:, V_QG + k:V_QG + k + 1], 1.0, ALU.mult, ALU.mult)
                if k < KQ - 1:
                    step(last)
            last.then_inc(wuq_scaled, 1)
            pool.wait_ge(h_done, KR + 1)
            for c in range(KR):
                u = U_G + c
                pool.wait_ge(evac[u % 4], u // 4 + 1)
                G.tensor_tensor(recT[:, c, :], xc[:, c, :], recT[:, c, :], ALU.mult).then_inc(rec_done, 1)
            pool.wait_ge(unit_done, U_NKV + 1)
            pool.wait_ge(kpe_done, 1)
            pool.wait_ge(rec_done, KR)
            for b2 in range(2):
                landed(pool, cache_landed[b2], 2)
            for h in range(NH):
                last = G.tensor_copy(kh[64:96, h, :], kpe[64:96, 0:SEQ])
                if h < NH - 1:
                    step(last)
            last.then_inc(khrope_done, 1)
            for h in range(NH):
                u = U_UQ + h
                pool.wait_ge(evac[u % 4], u // 4 + 1)
                G.tensor_tensor(qh[64:96, h, :], qh[64:96, h, :], tmp[64:96, h % 2, :], ALU.add).then_inc(qrope_done, 1)
            pool.wait_ge(qrope_done, NH)
            pool.wait_ge(unit_done, N_UNITS)
            fetch(2)
            for s in range(3, DEC):
                pool.wait_ge(op_done, s - 2)
                fetch(s)
            landed(pool, wo_landed)
            for k in range(KD):
                g = V_AG + k
                last = G.tensor_scalar(wo[:, k, :], wo[:, k, :], vec[:, g:g + 1], 1.0, ALU.mult, ALU.mult)
                if k < KD - 1:
                    step(last)
            last.then_inc(wo_scaled, 1)
            landed(pool, xtok_landed, TT)
            step(G.tensor_scalar(x1[:, 0:4, :], x1[:, 0:4, :], ALPHA, 1.0, ALU.mult, ALU.mult))
            G.tensor_scalar(x1[0:DEC, 4, :], x1[0:DEC, 4, :], ALPHA, 1.0, ALU.mult, ALU.mult).then_inc(xa_done, 1)

            pool.wait_ge(d_pe, 1)
            for j in range(NPAIR):
                step(G.memset(xg[j], 0.0))
            settle()

            landed(pool, table_empty)
            landed(pool, ids_landed, 3)
            pool.wait_ge(pos_ready, 1)
            for n in range(2):
                for t in range(TT):
                    rows = ROWS[t]
                    G.indirect_dma_start(out=slot_table, out_offset=bass.IndirectOffsetOnAxis(ap=posi[0:rows, n, t:t + 1], axis=0),
                                         in_=id_sb[0:rows, n * TT + t:n * TT + t + 1], in_offset=None).then_inc(scattered_ids, 16)
            landed(pool, scattered_ids, 2 * TT)
            landed(pool, x1_stored, TT)
            n_rounds = pool.value_load(rounds[0:1, 0:1], min_val=1, max_val=MAXR)

            def load_slots(g, b):
                src = slot_table[g * BLK:(g + 1) * BLK, :] if isinstance(g, int) else slot_table[bass.ds(g * BLK, BLK), :]
                G.dma_start(raw[:, b, :], src.rearrange("(s j) o -> s (j o)", j=NPAIR)).then_inc(raw_landed, 16)

            def gather(q):
                G.indirect_dma_start(out=xg[q], out_offset=None, in_=x1_rows,
                                     in_offset=bass.IndirectOffsetOnAxis(ap=gidx[:, q:q + 1], axis=0),
                                     bounds_check=TOK - 1, oob_is_err=False).then_inc(gathered[q], 16)

            def scatter(q):
                G.indirect_dma_start(out=pair_rows, out_offset=bass.IndirectOffsetOnAxis(ap=sidx[:, q:q + 1], axis=0),
                                     in_=yb[q], in_offset=None, bounds_check=2 * HALF_ID - 1,
                                     oob_is_err=False).then_inc(scattered[q], 16)

            def fixed():
                pool.wait_ge(pos_ready, 1)

            def token_index(b, first, second):
                G.tensor_scalar(gidx[:, :], raw[:, b, :], HALF_ID, -HALF_ID, ALU.is_ge, ALU.mult).then_inc(idx_half, 1)
                fixed()
                pool.wait_ge(idx_half, first)
                G.tensor_tensor(gidx[:, :], gidx[:, :], raw[:, b, :], ALU.add).then_inc(idx_half, 1)
                fixed()
                pool.wait_ge(idx_half, second)

            load_slots(0, 0)
            landed(pool, raw_landed)
            token_index(0, 1, 2)
            for q in range(NPAIR):
                gather(q)
            load_slots(1, 1)
            turn = [ctx.enter_context(pool.register(f"pool_turn{n}")) for n in range(NPAIR)]
            loads_in, sofar, copied = (ctx.enter_context(pool.register(n)) for n in ("loads_in", "sofar", "copied"))
            tokens_in = ctx.enter_context(pool.register("tokens_in"))
            halves = [ctx.enter_context(pool.register(f"halves{n}")) for n in range(2)]
            with pool.Fori(0, n_rounds * (NGRP // 2)) as it:
                for b in range(2):
                    g = it * 2 + b
                    for q in range(NPAIR):
                        pool.reg_mov(turn[q], g * NPAIR + q + 1)
                    pool.reg_mov(loads_in, g * 16 + 32)
                    pool.reg_mov(tokens_in, g * 16 + 16)
                    pool.reg_mov(sofar, g * 16)
                    pool.reg_mov(copied, g + 1)
                    for n in range(2):
                        pool.reg_mov(halves[n], g * 2 + 3 + n)
                    fixed()
                    pool.wait_ge(raw_landed, loads_in)
                    for q in range(NPAIR):
                        pool.wait_ge(gathered[q], tokens_in)
                    token_index(1 - b, *halves)
                    for q in range(NPAIR):
                        fixed()
                        pool.wait_ge(xt_ps, turn[q])
                        gather(q)
                    fixed()
                    for q in range(NPAIR):
                        pool.wait_ge(scattered[q], sofar)
                    G.tensor_copy(sidx[:, :], raw[:, b, :]).then_inc(idx_copied, 1)
                    fixed()
                    pool.wait_ge(idx_copied, copied)
                    load_slots(g + 2, b)
                    for q in range(NPAIR):
                        fixed()
                        pool.wait_ge(ya_done, turn[q])
                        pool.wait_ge(yd_done, turn[q])
                        scatter(q)
            landed(pool, raw_landed, n_rounds * NGRP + 2)
            for q in range(NPAIR):
                landed(pool, gathered[q], n_rounds * NGRP + 1)
            landed(pool, ln2_landed)
            for t in range(TT):
                n = ROWS[t]
                pool.wait_ge(g2_done, t + 1)
                G.tensor_tensor(y1[t][0:n, :], y1[t][0:n, :], lng2[0:n, 1, :], ALU.add).then_inc(y_ready, 1)


def _lay_out(i):
    f = np.float32
    c = np.ascontiguousarray
    x_tok = np.concatenate([i["x_prompt"].reshape(SEQ, D), i["x_sample"].reshape(DEC, D)], 0)

    def chunks(w, n):
        return w.reshape(n, P, -1).transpose(1, 0, 2)

    w_in = i["w_in"]
    a = QL + KVL
    order = [a + ROPE + P * n for n in range(4)] + [QL, QL + P] + [P * n for n in range(3)] + \
            [a + ROPE + REC + P * n for n in range(4)]
    w_in13 = np.stack([chunks(w_in[:, o:o + P], KD).reshape(P, -1) for o in order])
    hr = ROPE // 2
    kp = w_in[:, a:a + ROPE]
    w_kpe = chunks(np.concatenate([kp, kp[:, hr:], kp[:, :hr]], 1), KD).reshape(P, -1)
    uq = i["w_uq"]
    uq = np.concatenate([uq, uq[:, :, NOPE + hr:], uq[:, :, NOPE:NOPE + hr]], 2)
    w_uq = chunks(uq.reshape(QL, NH * P), KQ).reshape(P, -1)
    w_uk = chunks(i["w_uk"].reshape(KVL, -1), KKV).reshape(P, -1)
    w_uv = chunks(i["w_uv"].reshape(KVL, -1), KKV).reshape(P, -1)
    w_ukT = i["w_uk"].transpose(2, 1, 0).reshape(NOPE, -1)
    cols = lambda v: v.reshape(-1, P).T
    vecs = np.concatenate([cols(i["q_norm_g"]), cols(i["kv_norm_g"]),
                           i["conv_w"].reshape(CONV, KR, P).transpose(2, 1, 0).reshape(P, -1), cols(i["conv_b"]),
                           cols(i["b_rg"]), cols(i["b_ig"]), cols(i["lru_lambda"]), cols(i["att_out_g"]),
                           cols(i["rec_out_g"])], 1)
    gates = np.zeros((P, 2, KR, P), f)
    for g, w in enumerate((i["w_rg"], i["w_ig"])):
        for n in range(2 * KR):
            h = 64 * (n % 2)
            gates[h:h + 64, g, n // 2, h:h + 64] = w[n]
    inv = (10000.0 ** (-(np.arange(hr, dtype=np.float64) * 2.0 / ROPE))).astype(f)
    pos = np.concatenate([np.arange(SEQ), np.full(DEC, PAST)]).astype(f)
    ang = (pos[:, None] * inv[None, :]).astype(f).astype(np.float64)
    co, si = np.cos(ang).astype(f).T, np.sin(ang).astype(f).T
    w_router = np.zeros((D, 64), f)
    w_router[:, :NG] = i["w_group"]
    w_router[:, NG:NG + NE] = i["w_expert"]
    e = np.arange(NE)
    tok = np.arange(P)[:, None] + P * np.arange(TT)[None, :]
    return {
        "xT": x_tok.T.reshape(KD, P, TOK).transpose(1, 0, 2), "x_tok": x_tok,
        "kv_cache": i["cache_kv_latent"], "rope_cache": i["cache_k_rope"],
        "conv_st": i["state_conv"].reshape(DEC, CONV - 1, KR, P).transpose(3, 2, 1, 0),
        "rec_st": i["state_rec"].reshape(DEC, KR, P).transpose(2, 1, 0),
        "page_rep": np.repeat(i["page_table"].T, P // N_PAGES, axis=0).astype(np.int32),
        "lane": (np.arange(P) % 8).astype(np.int32)[:, None],
        "w_in": w_in13, "w_kpe": w_kpe, "w_uq": w_uq, "w_uk": w_uk, "w_uv": w_uv, "w_ukT": w_ukT, "vecs": vecs,
        "gates": gates.reshape(P, -1), "cs_tab": np.concatenate([co, co, -si, si], 0),
        "w_out": chunks(i["w_out"], KD).reshape(P, -1), "w_router": chunks(w_router, KD).reshape(P, -1),
        "r_bias": np.concatenate([i["b_group"], i["b_expert"]]),
        "lns": np.stack([i["ln1_g"], i["ln1_b"], i["ln2_g"], i["ln2_b"]]),
        "ids": np.concatenate([tok, tok + HALF_ID], 1).astype(np.int32),
        "eoff": np.concatenate([e, (e // GRP) * BLK + (e % 2) * CAP * NPAIR + (e % GRP) // 2]).astype(f),
        "w_gu": i["w_gate_up"], "w_dn": i["w_down"],
    }, c


_OUTS = {"y": (TOK, D), "ckv": (P, KKV, TOK), "kpe": (ROPE, TOK), "conv_p": (P, KR, CONV - 1), "rec_p": (P, KR),
         "conv_s": (P, KR, CONV - 1, DEC), "rec_s": (P, KR, DEC)}


def kernel(**inputs):
    import concourse.bacc as _bacc
    from concourse.bass_utils import run_bass_kernel_spmd as _run

    laid, c = _lay_out({k: np.asarray(v) for k, v in inputs.items()})
    nc = _bacc.Bacc("TRN2", target_bir_lowering=False, num_devices=1)
    arrays, args = {}, []
    for name, a in laid.items():
        a = c(a)
        arrays["in_" + name] = a
        args.append(nc.dram_tensor("in_" + name, a.shape, mybir.dt.from_np(a.dtype), kind="ExternalInput").ap())
    for name, shape in _OUTS.items():
        args.append(nc.dram_tensor("out_" + name, shape, F32, kind="ExternalOutput").ap())
    hymba_step(nc, *args)
    r = _run(nc, [arrays], core_ids=[0]).results[0]
    o = {k: np.asarray(r["out_" + k]) for k in _OUTS}
    ckv = o["ckv"].transpose(2, 1, 0).reshape(TOK, KVL)
    kpe = o["kpe"].T
    y = o["y"]
    conv_s = o["conv_s"].transpose(3, 2, 1, 0).reshape(DEC, CONV - 1, REC)
    return (c(y[:SEQ]).reshape(1, SEQ, D), c(y[SEQ:]).reshape(DEC, 1, D),
            c(ckv[:SEQ]).reshape(1, SEQ, KVL), c(kpe[:SEQ]).reshape(1, SEQ, ROPE),
            c(o["conv_p"].transpose(2, 1, 0)).reshape(1, CONV - 1, REC), c(o["rec_p"].T).reshape(1, REC),
            c(ckv[SEQ:]).reshape(DEC, 1, KVL), c(kpe[SEQ:]).reshape(DEC, 1, ROPE),
            c(conv_s), c(o["rec_s"].transpose(2, 1, 0)).reshape(DEC, REC))
```

```python
from contextlib import ExitStack

import numpy as np

import concourse.bass as bass
from concourse import mybir

ACT = mybir.ActivationFunctionType
ALU = mybir.AluOpType
AX_X = mybir.AxisListType.X
F32 = mybir.dt.float32
BF16 = mybir.dt.bfloat16
I32 = mybir.dt.int32
U32 = mybir.dt.uint32

P = 128
D = 1024
KD = D // P
SEQ = 512
DEC = 8
TOK = SEQ + DEC
HALF = TOK // 2
PAST, PAGE = 2048, 128
N_PAGES = PAST // PAGE
NH, NOPE, ROPE, VH = 8, 64, 32, 64
QL, KVL, REC = 384, 256, 512
KQ, KKV, KR = QL // P, KVL // P, REC // P
CONV = 4
NG, EPG, NE, DE = 4, 8, 32, 256
SM = float((NOPE + ROPE) ** -0.5)
ALPHA = float(2.0 ** 0.25)
LN_EPS, RMS_EPS = 1e-5, 1e-6
NEG = -1e30
TT = 5
ROWS = [P, P, P, P, DEC]
ORDER = [0, 1, 4, 2, 3]
LAST_ORDER = [4, 0, 1, 2, 3]
POOL_TILES, DVE_TILES = [0, 2], [4, 1, 3]
SHIFT = SEQ // 2
WIN = TOK - SHIFT

CAP = 64
GRP = 4
NPAIR = GRP // 2
NGRP = NE // GRP
MAXR = -(-TOK // CAP)
BLK = CAP * GRP
RBLK = NGRP * BLK
NTAB = (MAXR + 1) * RBLK
FREE_SLOT = 8191
HALF_ID = 1024

V_QG, V_KVG, V_CW, V_CB, V_BR, V_BI, V_LAM, V_AG, V_RG = 0, 3, 5, 21, 25, 29, 33, 37, 41
NV = 45

U_RX, U_KV, U_KPE, U_Q, U_R, U_I, U_NQ, U_NKV, U_G, U_UQ, U_UK, U_V = 0, 4, 6, 7, 10, 14, 18, 19, 20, 24, 32, 36
N_UNITS = 40
CHUNK_OF = {**{U_RX + c: c for c in range(4)}, U_KV: 4, U_KV + 1: 5, U_Q: 6, U_Q + 1: 7, U_Q + 2: 8,
            **{U_G + c: 9 + c for c in range(4)}}
N_CHUNKS = 13
LAND_OF = [0, 1, 2, 3, 4, 5, 6, 6, 6, 7, 7, 7, 7]

W_X = N_CHUNKS * D + KD * 64
W_SLOT = KD * 2 * DE + 2 * D
W_LEN = 3 * W_SLOT
CB = 16 * (KVL + ROPE)
W_OP = 2 * CB
W_PT = W_OP + DEC * KVL
W_KT = W_PT + 2 * 1280
O_UQ, O_UK, O_UV, O_UKT, O_GATE = 0, 3072, 4096, 5120, 7168
O_LEN = KD * D
WO_LATE = 5
S_QH, S_KH, S_V, S_ATT, S_REC, S_XC, S_XP, S_TMP = 0, 4160, 8256, 10304, 12384, 14464, 16544, 18624
S_QZ, S_KVZ, S_RQ, S_RKV, S_KPE = 20184, 21744, 22784, 23304, 23824
S_LEN = 24344
S_SQ0 = S_KH
S_P = [S_QZ, S_XP]
S_RT8, S_DP, S_DPT = S_XP + 1280, S_RKV, S_RKV + 512
S_QQ, S_QS = S_XC, S_XC + 8 * 192
S_X1, S_UV2, S_SQ = 0, 9280, 5120
S_RT = 9280
S_X1T = S_XC
S_WR = S_TMP
S_LN = 19392
S_T = S_KVZ
S_XG, S_YB = 5120, 7168
S_SLOT = S_ATT
S_E = S_SLOT + 2 * W_SLOT

OFF = [0, 128, 384, 768]
POFF = [0, 512, 896, 1152]

TURNS = ["p", 0, 2, "h0", 4, 6, "h1", 1, 3, 5, 7, 8, "h2", "h3"]


def turn_no(s, what):
    return len(TURNS) * s + TURNS.index(what) - 1


def hymba_step(nc, xT, x_tok, kv_cache, rope_cache, conv_st, rec_st, page_rep, lane, w_in, w_kpe, w_uq, w_uk,
               w_uv, w_ukT, vecs, gates, cs_tab, w_out, w_router, r_bias, lns, ids, count, w_gu, w_dn,
               y_out, ckv_out, kpe_out, conv_p_out, rec_p_out, conv_s_out, rec_s_out):
    x1_rows = nc.dram_tensor("x1_rows", (TOK, D), F32, kind="Internal").ap()
    pair_rows = nc.dram_tensor("pair_rows", (2 * HALF_ID, D), F32, kind="Internal").ap()
    slot_table = nc.dram_tensor("slot_table", (NTAB, 1), I32, kind="Internal").ap()
    kv_rows = kv_cache.rearrange("n (c j) e -> (n c) (j e)", c=8)
    rope_rows = rope_cache.rearrange("n (c j) e -> (n c) (j e)", c=8)

    with ExitStack() as ctx:
        def sb(name, shape, dt=F32):
            return ctx.enter_context(nc.sbuf_tensor(name, shape, dt))

        def sem(name):
            return ctx.enter_context(nc.semaphore(name))

        ps = ctx.enter_context(nc.psum_tensor("ps", [P, 8, 512], F32))
        arena_w = sb("arena_w", [P, W_LEN])
        arena_o = sb("arena_o", [P, O_LEN])
        arena_s = sb("arena_s", [P, S_LEN])

        def part(arena, at, *dims):
            n = int(np.prod(dims))
            v = arena[:, at:at + n]
            if len(dims) == 2:
                v = v.rearrange("p (a b) -> p a b", a=dims[0])
            if len(dims) == 3:
                v = v.rearrange("p (a b c) -> p a b c", a=dims[0], b=dims[1])
            return v

        ident = sb("ident", [P, P])
        identb = sb("identb", [P, P], BF16)
        maskb = sb("maskb", [P, P], BF16)
        trib = sb("trib", [P, P], BF16)
        onesb = sb("onesb", [P, P], BF16)
        ones = sb("ones", [P, P])
        cs = sb("cs", [P, TOK])
        vec = sb("vec", [P, NV])
        lam = sb("lam", [P, 8, KR])
        nsp = sb("nsp", [P, 2, KR])
        bh = sb("bh", [P, 2, KR])
        eps = sb("eps", [P, 2])
        cdec = sb("cdec", [P, KR, CONV, DEC])
        conv_tail = sb("conv_tail", [P, KR, CONV - 1])
        rec_last = sb("rec_last", [P, KR])
        rst = sb("rst", [P, KR, DEC])
        rbias = sb("rbias", [P, NG + NE])
        stat = sb("stat", [P, 2, 4])
        mx = sb("mx", [P, DEC])
        ls = sb("ls", [P, DEC])
        nmd = sb("nmd", [P, 2])
        pages = sb("pages", [P, DEC], I32)
        lane_sb = sb("lane_sb", [P, 1], I32)
        kpn = sb("kpn", [ROPE, DEC])
        sel = sb("sel", [P, 32])
        wcol = sb("wcol", [P, DEC])
        rinv = sb("rinv", [P, 2, 2, 2])
        rinv4 = sb("rinv4", [DEC, 2])
        bn = sb("bn", [P, 2, 6])
        mv = sb("mv", [P, 2, 4])
        gpad = sb("gpad", [P, TT, 8])
        top8 = sb("top8", [P, TT, 8])
        idx8 = sb("idx8", [P, TT, 8], U32)
        rs = sb("rs", [P, 16, TT])
        ohb = sb("ohb", [P, TT, NE], BF16)
        ohg = sb("ohg", [P, TT, NG])
        id_sb = sb("id_sb", [P, 2 * TT, 2])
        count_sb = sb("count_sb", [P, CAP])
        valid = sb("valid", [P, TT])
        rounds = sb("rounds", [P, 2], I32)
        raw = sb("raw", [P, 2, NPAIR], I32)
        gidx = sb("gidx", [P, NPAIR], I32)
        sidx = sb("sidx", [P, NPAIR], I32)
        table = sb("table", [P, 3, NE // 2])
        table_i = sb("table_i", [P, NE // 2], I32)

        xTv = part(arena_w, W_X, KD, TOK)
        w_chunk = [part(arena_w, c * D, KD, P) for c in range(N_CHUNKS)]
        w_kpev = part(arena_w, N_CHUNKS * D, KD, 64)
        uq, uk, uv = part(arena_o, O_UQ, KQ, NH, P), part(arena_o, O_UK, KKV, 512), part(arena_o, O_UV, KKV, 512)
        ukT = part(arena_o, O_UKT, NH, KVL)
        gw = part(arena_o, O_GATE, 2, KR, P)
        wo = part(arena_o, 0, KD, D)
        qh, kh, v = part(arena_s, S_QH, NH, TOK), part(arena_s, S_KH, NH, SEQ), part(arena_s, S_V, 4, 512)
        attT, recT = part(arena_s, S_ATT, KR, TOK), part(arena_s, S_REC, KR, TOK)
        tr, xc, xp = attT, part(arena_s, S_XC, KR, TOK), part(arena_s, S_XP, KR, TOK)
        tmp = part(arena_s, S_TMP, 3, TOK)
        qz, kvz = part(arena_s, S_QZ, KQ, TOK), part(arena_s, S_KVZ, KKV, TOK)
        rq, rkv, kpe = part(arena_s, S_RQ, TOK), part(arena_s, S_RKV, TOK), part(arena_s, S_KPE, TOK)
        sq0 = part(arena_s, S_SQ0, KQ + KKV, TOK)
        Pb = [part(arena_s, S_P[b], 1280) for b in range(2)]
        PTb = [part(arena_w, W_PT + 1280 * b, 1280) for b in range(2)]
        buf = [arena_w[:, 0:CB], arena_w[:, CB:2 * CB], arena_o[:, 0:CB]]
        cache = [part(b, 0, 16, KVL) for b in buf]
        crope = [part(b, 16 * KVL, 4, P) for b in buf]
        KT, ropeT = part(arena_w, W_KT, KKV, PAST), part(arena_s, S_RT8, 512)
        dP, dPT = part(arena_s, S_DP, 512), part(arena_s, S_DPT, 512)
        op = part(arena_w, W_OP, DEC, KVL)
        qq, qs = part(arena_s, S_QQ, DEC, 192), part(arena_s, S_QS, 2, 192)
        qlt = part(arena_s, S_TMP, 512)
        fin = arena_s[0:DEC, S_RQ:S_RQ + 512]
        osum, tn, oT = part(arena_s, S_TMP, 512), part(arena_s, S_TMP + 512, KKV, DEC, NH), part(arena_s, S_TMP + 640, KKV, NH, DEC)
        uv2 = part(arena_s, S_UV2, KKV, 512)
        x1, sq = part(arena_s, S_X1, TT, D), part(arena_s, S_SQ, KD, TOK)
        L, Lb = part(arena_s, S_RT, TT, NG + NE), part(arena_s, S_RT + 180, TT, NG + NE)
        me, oh1, oh2, rt_t = (part(arena_s, S_RT + 360 + 160 * n, TT, NE) for n in range(4))
        x1T = part(arena_s, S_X1T, KD, TOK)
        wr = part(arena_s, S_WR, KD, 64)
        lng = part(arena_s, S_LN, 2, D)
        pair_parts = part(arena_s, S_RT + 180, 320).bitcast(BF16).rearrange("p (a b c d) -> p a b c d", a=2 * TT, b=2, c=2)
        slot_mark = part(arena_s, S_YB + 2 * D - 320, 320).bitcast(BF16).rearrange("p (a b) -> p a b", a=2 * TT)
        lng2 = part(arena_o, W_SLOT, 2, D)
        tb = [part(arena_s, S_T + D * b, D) for b in range(2)]
        ss, rt = part(arena_s, S_DP, SHIFT), part(arena_s, S_E, WIN)
        slot = [arena_w[:, W_SLOT * n:W_SLOT * (n + 1)] for n in range(3)] + [arena_o[:, 0:W_SLOT]] + \
            [arena_s[:, S_SLOT + W_SLOT * n:S_SLOT + W_SLOT * (n + 1)] for n in range(2)]
        gu_w = [s[:, 0:KD * 2 * DE].rearrange("p (k n) -> p k n", k=KD) for s in slot]
        dn_w = [s[:, KD * 2 * DE:W_SLOT].rearrange("p (k n) -> p k n", k=2) for s in slot]
        xg = [part(arena_s, S_XG + D * b, D) for b in range(NPAIR)]
        yb = [part(arena_s, S_YB + D * b, D) for b in range(NPAIR)]
        xgT = part(arena_s, S_E, KD, P)
        sg, hx, hT = part(arena_s, S_E + 1024, DE), part(arena_s, S_E + 1024 + DE, DE), part(cs, 0, 2, P)
        y1, y2 = ([part(arena_w, 2 * D * t + D * n, D) for t in range(TT)] for n in range(2))
        mixer = part(arena_s, S_SLOT, 2 * 4, P)

        def pair(u, cols=HALF):
            b = 2 * (u % 4)
            return ps[:, b:b + 2, 0:cols]

        x_landed = [sem(f"x_landed{n}") for n in range(4)]
        win_landed = [sem(f"win_landed{n}") for n in range(8)]
        kpe_w_landed, gates_landed, uq_landed = sem("kpe_w_landed"), sem("gates_landed"), sem("uq_landed")
        ukv_landed, params_landed, cs_landed = sem("ukv_landed"), sem("params_landed"), sem("cs_landed")
        pages_landed, ids_landed = sem("pages_landed"), sem("ids_landed")
        wo_landed = [sem(f"wo_landed{n}") for n in range(2)]
        uv2_landed, xtok_landed = sem("uv2_landed"), sem("xtok_landed")
        ln1_landed, ln2_landed = sem("ln1_landed"), sem("ln2_landed")
        cache_landed = [sem(f"cache_landed{b}") for b in range(3)]
        gu_landed = [sem(f"gu_landed{q}") for q in range(3)]
        dn_landed = [sem(f"dn_landed{q}") for q in range(3)]
        slots_ready, slots_ps, table_ready, table_stored = (sem(n) for n in (
            "slots_ready", "slots_ps", "table_ready", "table_stored"))
        raw_landed = sem("raw_landed")
        gathered = [sem(f"gathered{q}") for q in range(NPAIR)]
        scattered = [sem(f"scattered{q}") for q in range(NPAIR)]
        x1_stored = sem("x1_stored")
        y_landed = [sem(f"y_landed{t}") for t in range(TT)]
        y_stored = sem("y_stored")
        outs_stored = sem("outs_stored")
        dve_step, pool_step = sem("dve_step"), sem("pool_step")
        const_ready, ones_ready = sem("const_ready"), sem("ones_ready")
        unit_done = sem("unit_done")
        evac = [sem(f"evac{n}") for n in range(4)]
        conv_done, kpe_done, squares, wuq_scaled = sem("conv_done"), sem("kpe_done"), sem("squares"), sem("wuq_scaled")
        ckv_done, rq_done = sem("ckv_done"), sem("rq_done")
        a_done, th_done, a2_done, w_done, root_w = (sem(n) for n in (
            "a_done", "th_done", "a2_done", "w_done", "root_w"))
        ix_done, h_done, rec_done = sem("ix_done"), sem("h_done"), sem("rec_done")
        lam_ready, sp_exp = sem("lam_ready"), sem("sp_exp")
        qrope_done, khrope_done = sem("qrope_done"), sem("khrope_done")
        s_done, nm_done, exp_done, p_done, t_done = (sem(n) for n in ("s_done", "nm_done", "exp_done", "p_done", "t_done"))
        out_act, out_dve, pv_done, att_done = sem("out_act"), sem("out_dve"), sem("pv_done"), sem("att_done")
        ql_done, ql_evac, qlT_done, qq_done = sem("ql_done"), sem("ql_evac"), sem("qlT_done"), sem("qq_done")
        qs_done, sc_done, dmx_done, dexp_done = (sem(n) for n in ("qs_done", "sc_done", "dmx_done", "dexp_done"))
        op_done, op_evac = sem("op_done"), sem("op_evac")
        cidx_ready, dmax_raw, diff_ready = sem("cidx_ready"), sem("dmax_raw"), sem("diff_ready")
        wr_landed, idx_half, idx_copied = sem("wr_landed"), sem("idx_half"), sem("idx_copied")
        combine_pe, combine_act, combine_dve = sem("combine_pe"), sem("combine_act"), sem("combine_dve")
        sq_done, wo_scaled, xa_done = sem("sq_done"), sem("wo_scaled"), sem("xa_done")
        outproj_pe, outproj_act = sem("outproj_pe"), sem("outproj_act")
        o_done, o_out, ln_norm, x1_done = (sem(n) for n in ("o_done", "o_out", "ln_norm", "x1_done"))
        ln_var, ln_root = sem("ln_var"), sem("ln_root")
        x1T_ps, x1T_act, x1T_dve = sem("x1T_ps"), sem("x1T_act"), sem("x1T_dve")
        rank_moved, table_step = sem("rank_moved"), sem("table_step")
        route_pe, route_act, route_dve, routed = sem("route_pe"), sem("route_act"), sem("route_dve"), sem("routed")
        xt_ps, xt_sb, gu_ps, silu_done, h_ready, ht_ps, ht_sb, dn_ps, ya_done, yd_done = (sem(n) for n in (
            "xt_ps", "xt_sb", "gu_ps", "silu_done", "h_ready", "ht_ps", "ht_sb", "dn_ps", "ya_done", "yd_done"))
        mixer_in = sem("mixer_in")
        mixer_ready, y_mixed, y_sum, v2_done, root2, n2_done, g2_done, y_dve, y_pool, pool_gain = (sem(n) for n in (
            "mixer_ready", "y_mixed", "y_sum", "v2_done", "root2", "n2_done", "g2_done", "y_dve", "y_pool", "pool_gain"))

        block = ctx.enter_context(nc.Block())

        def landed(eng, s, n=1):
            eng.wait_ge(s, 16 * n)

        def out_of_psum(eng, n):
            eng.wait_ge(out_dve if n % 2 else out_act, n // 2 + 1)

        @block.sync
        def _(sp):
            def chunk(c):
                sp.dma_start(arena_w[:, c * D:(c + 1) * D], w_in[c]).then_inc(win_landed[LAND_OF[c]], 16)
            sp.dma_start(xTv[:, 0:2, :], xT[:, 0:2, :]).then_inc(x_landed[0], 16)
            chunk(0)
            for n in range(1, 4):
                sp.dma_start(xTv[:, 2 * n:2 * n + 2, :], xT[:, 2 * n:2 * n + 2, :]).then_inc(x_landed[n], 16)
            for c in range(1, 6):
                chunk(c)
            sp.dma_start(arena_w[:, N_CHUNKS * D:W_X], w_kpe).then_inc(kpe_w_landed, 16)
            sp.dma_start(arena_o[:, O_GATE:O_GATE + 1024], gates).then_inc(gates_landed, 16)
            for c in range(6, N_CHUNKS):
                chunk(c)
            sp.dma_start(arena_o[:, O_UQ:O_UQ + 3072], w_uq).then_inc(uq_landed, 16)
            sp.dma_start(arena_o[:, O_UK:O_UK + 1024], w_uk).then_inc(ukv_landed, 16)
            sp.dma_start(arena_o[:, O_UV:O_UV + 1024], w_uv).then_inc(ukv_landed, 16)
            sp.dma_start(arena_o[0:NOPE, O_UKT:O_UKT + 2048], w_ukT).then_inc(ukv_landed, 16)
            sp.wait_ge(kpe_done, 1)
            sp.dma_start(kpe_out, kpe[64:96, :]).then_inc(outs_stored, 16)
            sp.wait_ge(ckv_done, 1)
            sp.dma_start(ckv_out, kvz).then_inc(outs_stored, 16)
            sp.wait_ge(h_done, 5)
            sp.dma_start(conv_p_out, conv_tail[:, :, :]).then_inc(outs_stored, 16)
            sp.dma_start(conv_s_out, cdec[:, :, 1:CONV, :]).then_inc(outs_stored, 16)
            sp.dma_start(rec_p_out, rec_last[:, :]).then_inc(outs_stored, 16)
            sp.dma_start(rec_s_out, xc[:, :, SEQ:TOK]).then_inc(outs_stored, 16)
            sp.wait_ge(unit_done, N_UNITS)
            sp.wait_ge(ql_done, 1)
            sp.dma_start(arena_o[:, WO_LATE * D:O_LEN], w_out[:, WO_LATE * D:O_LEN]).then_inc(wo_landed[0], 16)
            sp.wait_ge(op_done, 6)
            sp.dma_start(arena_o[:, 0:WO_LATE * D], w_out[:, 0:WO_LATE * D]).then_inc(wo_landed[1], 16)
            sp.wait_ge(s_done, 4 * NH)
            for t in range(TT):
                sp.dma_start(x1[0:ROWS[t], t, :], x_tok[P * t:P * t + ROWS[t], :]).then_inc(xtok_landed, 16)
            sp.wait_ge(pv_done, NH // 2)
            sp.dma_start(uv2, w_uv.rearrange("p (k n) -> p k n", k=KKV)).then_inc(uv2_landed, 16)
            sp.dma_start(lng, lns[0:2].partition_broadcast(P)).then_inc(ln1_landed, 16)
            sp.wait_ge(combine_pe, 4)
            sp.dma_start(arena_s[:, S_WR:S_WR + 512], w_router).then_inc(wr_landed, 16)

            def gate_up(j, e):
                sp.dma_start(gu_w[j], w_gu[e].rearrange("o (k p) n -> p (o k) n", p=P)).then_inc(gu_landed[j // 2], 16)

            def down(j, e):
                sp.dma_start(dn_w[j], w_dn[e].rearrange("o (k p) n -> p (o k) n", p=P)).then_inc(dn_landed[j // 2], 16)
            for j in (0, 1):
                gate_up(j, slice(j, j + 1))
            for j in (0, 1):
                down(j, slice(j, j + 1))
            gate_up(2, slice(2, 3))
            down(2, slice(2, 3))
            for n, t in enumerate(ORDER):
                if n == TT - 1:
                    sp.wait_ge(o_done, 8)
                    sp.wait_ge(outproj_pe, 4)
                    gate_up(3, slice(3, 4))
                    down(3, slice(3, 4))
                sp.wait_ge(x1_done, n + 1)
                sp.dma_start(x1_rows[P * t:P * t + ROWS[t], :], x1[0:ROWS[t], t, :]).then_inc(x1_stored, 16)
            sp.dma_start(lng2, lns[2:4].partition_broadcast(P)).then_inc(ln2_landed, 16)
            sp.wait_ge(route_pe, 1)
            for j in (4, 5):
                gate_up(j, slice(j, j + 1))
            for q in range(NPAIR):
                landed(sp, gathered[q])
            for j in (4, 5):
                down(j, slice(j, j + 1))
            sp.wait_ge(routed, 1)
            n_rounds = sp.value_load(rounds[0:1, 0:1], min_val=1, max_val=MAXR)

            def refill(q, e, used):
                sp.wait_ge(gu_ps, used)
                for n in range(2):
                    gate_up(2 * q + n, slice(e + n, e + n + 1) if isinstance(e, int) else bass.ds(e + n, 1))
                sp.wait_ge(dn_ps, used)
                for n in range(2):
                    down(2 * q + n, slice(e + n, e + n + 1) if isinstance(e, int) else bass.ds(e + n, 1))
            refill(0, 6, 1)
            refill(1, 8, 2)
            with sp.Fori(0, n_rounds * (NE // 4) - 3) as it:
                refill(0, (it * 4 + 10) % NE, it * 2 + 4)
                refill(1, (it * 4 + 12) % NE, it * 2 + 5)
            refill(0, NE - 2, sp.value_load(rounds[0:1, 1:2], min_val=NE // 2 - 2, max_val=MAXR * NE // 2))
            for q in range(NPAIR):
                sp.wait_ge(scattered[q], n_rounds * (NGRP * 16))
            for t in LAST_ORDER:
                n = ROWS[t]
                sp.dma_start(y1[t][0:n, :], pair_rows[P * t:P * t + n, :]).then_inc(y_landed[t], 16)
                sp.dma_start(y2[t][0:n, :], pair_rows[HALF_ID + P * t:HALF_ID + P * t + n, :]).then_inc(y_landed[t], 16)
            for t in LAST_ORDER:
                if t in POOL_TILES:
                    sp.wait_ge(y_pool, POOL_TILES.index(t) + 1)
                else:
                    sp.wait_ge(y_dve, DVE_TILES.index(t) + 1)
                sp.dma_start(y_out[P * t:P * t + ROWS[t], :], y1[t][0:ROWS[t], :]).then_inc(y_stored, 16)
            landed(sp, y_stored, TT)
            landed(sp, outs_stored, 6)

        def turned(eng, copy, done, s, what):
            n = turn_no(s, what)
            eng.wait_ge(t_done, n + 1)
            cols = 512
            if what == "p":
                dst = dPT
                if s >= 2:
                    eng.wait_ge(op_done, s - 1)
            elif isinstance(what, int):
                dst = ropeT if what == 8 else KT[:, what % 2, (what // 2) * 512:(what // 2 + 1) * 512]
                if s >= 1:
                    eng.wait_ge(sc_done, s)
            else:
                j = int(what[1])
                cols = (4 - j) * P
                dst = PTb[s % 2][:, POFF[j]:POFF[j] + cols]
                if s >= 2:
                    eng.wait_ge(pv_done, s // 2)
            copy(dst, ps[:, 2 + n % 3, 0:cols]).then_inc(done, 1)

        @block.tensor
        def _(pe):
            mm = nc.tensor.matmul

            def unit(u, lhs, rhs, ks, rows=slice(0, P)):
                if u >= 4:
                    pe.wait_ge(evac[u % 4], u // 4)
                b = 2 * (u % 4)
                for k in range(ks):
                    if u == 0 and k % 2 == 0:
                        landed(pe, x_landed[k // 2])
                    for n in range(2):
                        last = mm(ps[rows, b + n, 0:HALF], lhs(k), rhs(k)[:, n * HALF:(n + 1) * HALF],
                                  start=(k == 0), stop=(k == ks - 1))
                last.then_inc(unit_done, 1)

            def project(u):
                c = CHUNK_OF[u]
                landed(pe, win_landed[LAND_OF[c]], LAND_OF.count(LAND_OF[c]))
                unit(u, lambda k: w_chunk[c][:, k, :], lambda k: xTv[:, k, :], KD)

            for u in range(U_RX, U_KPE):
                project(u)
            landed(pe, kpe_w_landed)
            unit(U_KPE, lambda k: w_kpev[:, k, :], lambda k: xTv[:, k, :], KD, slice(64, 128))
            for u in range(U_Q, U_Q + KQ):
                project(u)
            landed(pe, gates_landed)
            for g, u0 in enumerate((U_R, U_I)):
                for c in range(KR):
                    pe.wait_ge(conv_done, c + 1)
                    unit(u0 + c, lambda k: gw[:, g, c, :], lambda k: xc[:, c, :], 1)
            pe.wait_ge(ones_ready, 1)
            pe.wait_ge(squares, 2)
            unit(U_NQ, lambda k: ones[:, :], lambda k: sq0[:, k, :], KQ)
            unit(U_NKV, lambda k: ones[:, :], lambda k: sq0[:, KQ + k, :], KKV)
            for u in range(U_G, U_G + KR):
                project(u)
            pe.wait_ge(wuq_scaled, 1)
            for h in range(NH):
                unit(U_UQ + h, lambda k: uq[:, k, h, :], lambda k: qz[:, k, :], KQ)
            landed(pe, ukv_landed, 3)
            pe.wait_ge(ckv_done, 1)
            for n in range(4):
                u = U_UK + n
                pe.wait_ge(evac[u % 4], u // 4)
                for k in range(KKV):
                    last = mm(ps[:, 2 * (u % 4), :], uk[:, k, n * P:(n + 1) * P], kvz[:, k, 0:SEQ],
                              start=(k == 0), stop=(k == KKV - 1))
                last.then_inc(unit_done, 1)
            for n in range(4):
                u = U_V + n
                pe.wait_ge(evac[u % 4], u // 4)
                for k in range(KKV):
                    last = mm(ps[:, 2 * (u % 4), :], kvz[:, k, n * P:(n + 1) * P], uv[:, k, :],
                              start=(k == 0), stop=(k == KKV - 1))
                last.then_inc(unit_done, 1)
            for n in range(4):
                pe.wait_ge(evac[n], N_UNITS // 4)

            pe.wait_ge(qrope_done, NH)
            for hi in range(2):
                for g in range(4):
                    h = 4 * hi + g
                    last = mm(ps[32 * g:32 * g + 32, 6, hi * KVL:(hi + 1) * KVL], qh[0:NOPE, h, TOK - 32:TOK],
                              ukT[0:NOPE, h, :], start=True, stop=True)
            last.then_inc(ql_done, 1)

            pe.wait_ge(khrope_done, 1)
            pe.wait_ge(const_ready, 4)

            def scores(h, i):
                n = 4 * h + i
                if n >= 2:
                    pe.wait_ge(exp_done, n - 1)
                b = n % 2
                mm(ps[:, b, 0:P * (i + 1)], qh[0:96, h, i * P:(i + 1) * P], kh[0:96, h, 0:P * (i + 1)],
                   start=True, stop=False)
                mm(ps[:, b, P * i:P * (i + 1)], identb[:, :], maskb[:, :], start=False, stop=True,
                   ).then_inc(s_done, 1)

            def turn(n, blocks):
                if n >= 3:
                    out_of_psum(pe, n - 3)
                for m, src in enumerate(blocks):
                    last = nc.tensor.transpose(ps[:, 2 + n % 3, m * P:(m + 1) * P], src, ident[:, :])
                last.then_inc(t_done, 1)

            def turn_head(h, j):
                pe.wait_ge(p_done, 4 * h + 4)
                turn(turn_no(h, f"h{j}"), [Pb[h % 2][:, OFF[i] + j * P:OFF[i] + (j + 1) * P] for i in range(j, 4)])

            def turn_cache(s, b):
                landed(pe, cache_landed[s % 3], 2 * (s // 3 + 1))
                i, kc = b // 2, b % 2
                turn(turn_no(s, b), [crope[s % 3][:, j, :] if b == 8 else cache[s % 3][:, 4 * i + j, kc * P:(kc + 1) * P]
                                     for j in range(4)])

            def turn_cache_probs(s):
                pe.wait_ge(dexp_done, s + 1)
                turn(turn_no(s + 1, "p"), [dP[:, j * P:(j + 1) * P] for j in range(4)])

            def values(hp):
                out_of_psum(pe, turn_no(2 * hp + 1, "h2"))
                out_of_psum(pe, turn_no(2 * hp + 1, "h3"))
                if hp >= 1:
                    pe.wait_ge(att_done, hp)
                for j in range(4):
                    for e in range(2):
                        h = 2 * hp + e
                        last = mm(ps[64 * e:64 * e + 64, 5, j * P:SEQ], v[:, j, h * VH:(h + 1) * VH],
                                  PTb[e][:, POFF[j]:POFF[j] + (4 - j) * P], start=(j == 0), stop=(j == 3))
                last.then_inc(pv_done, 1)

            def cache_scores(s, kc):
                q = qs[:, s % 2, :]
                if kc == 0:
                    out_of_psum(pe, turn_no(s, 4))
                    out_of_psum(pe, turn_no(s, 6))
                    pe.wait_ge(qs_done, s + 1)
                    if s >= 1:
                        pe.wait_ge(dexp_done, s)
                else:
                    out_of_psum(pe, turn_no(s, 7))
                    out_of_psum(pe, turn_no(s, 8))
                for i in range(4):
                    mm(ps[32 * i:32 * i + 32, 6, :], q[:, 32 * kc:32 * kc + 32],
                       KT[:, kc, i * 512:(i + 1) * 512], start=(kc == 0), stop=False, skip_group_check=True)
                if kc == 0:
                    return
                for j in range(4):
                    for i in range(4):
                        last = mm(ps[32 * i:32 * i + 32, 6, j * P:(j + 1) * P], q[:, 64 + 32 * j:96 + 32 * j],
                                  ropeT[:, i * P:(i + 1) * P], start=False, stop=(j == 3), skip_group_check=True)
                last.then_inc(sc_done, 1)

            def cache_values(s):
                out_of_psum(pe, turn_no(s + 1, "p"))
                if s >= 1:
                    pe.wait_ge(op_evac, s)
                for j in range(4):
                    for i in range(4):
                        last = mm(ps[32 * i:32 * i + 32, 7, 0:KVL], dPT[:, j * P + 32 * i:j * P + 32 * i + 32],
                                  cache[s % 3][:, 4 * i + j, :], start=(j == 0), stop=(j == 3))
                last.then_inc(op_done, 1)

            scores(0, 0)
            scores(0, 1)
            turn_cache(0, 0)
            turn_cache(0, 2)
            pe.wait_ge(ql_evac, 1)
            for n in range(4):
                last = nc.tensor.transpose(ps[:, 7, n * P:(n + 1) * P], qlt[:, n * P:(n + 1) * P], ident[:, :])
            last.then_inc(qlT_done, 1)
            scores(0, 2)
            scores(0, 3)
            for s in range(NH):
                more = s + 1 < NH
                if more:
                    scores(s + 1, 0)
                if s >= 2 and s % 2 == 0:
                    values(s // 2 - 1)
                if s >= 1:
                    turn_cache_probs(s - 1)
                if s >= 1:
                    turn_cache(s, 0)
                    turn_cache(s, 2)
                turn_head(s, 0)
                if more:
                    scores(s + 1, 1)
                turn_cache(s, 4)
                turn_cache(s, 6)
                turn_head(s, 1)
                if s >= 1:
                    cache_values(s - 1)
                if more:
                    scores(s + 1, 2)
                turn_cache(s, 1)
                turn_cache(s, 3)
                cache_scores(s, 0)
                turn_cache(s, 5)
                turn_cache(s, 7)
                turn_cache(s, 8)
                if more:
                    scores(s + 1, 3)
                cache_scores(s, 1)
                turn_head(s, 2)
                turn_head(s, 3)
            values(NH // 2 - 1)
            turn_cache_probs(DEC - 1)
            cache_values(DEC - 1)

            def project_out(m):
                t, n = (m - 1) // 2, (m - 1) % 2
                b = 2 * (m % 2)
                if m >= 3:
                    pe.wait_ge(o_out, m - 2)
                for w in range(2):
                    for k in range(KR):
                        last = mm(ps[:, b + w, :], (attT if w == 0 else recT)[:, k, t * P:(t + 1) * P],
                                  wo[:, KR * w + k, n * 512:(n + 1) * 512], start=(k == 0), stop=(k == KR - 1))
                last.then_inc(o_done, 1)

            def turn_x1(m):
                t = ORDER[m]
                pe.wait_ge(x1_done, m + 1)
                if m == 0:
                    pe.wait_ge(outproj_act, 2)
                if m > 0:
                    pe.wait_ge(x1T_act, m)
                    pe.wait_ge(x1T_dve, m)
                n = ROWS[t]
                for k in range(KD):
                    last = nc.tensor.transpose(ps[:, 6 + k // 4, (k % 4) * P:(k % 4) * P + n],
                                               x1[0:n, t, k * P:(k + 1) * P], ident[0:n, 0:n])
                last.then_inc(x1T_ps, 1)

            out_of_psum(pe, turn_no(DEC - 1, "h2"))
            out_of_psum(pe, turn_no(DEC - 1, "h3"))
            pe.wait_ge(att_done, NH // 2)
            nc.tensor.transpose(ps[0:DEC, 4, 0:P], mx[:, :], ident[:, :])
            nc.tensor.transpose(ps[0:DEC, 4, P:2 * P], ls[:, :], ident[:, :])
            for kc in range(KKV):
                mm(ps[0:DEC, 5, 0:64], kvz[:, kc, SEQ:TOK], qq[:, :, 32 * kc:32 * kc + NH], start=(kc == 0), stop=False)
            mm(ps[0:DEC, 5, 0:64], kpn[:, :], qq[0:32, :, 64:64 + NH], start=False, stop=True).then_inc(combine_pe, 1)
            pe.wait_ge(sq_done, 2)
            pe.wait_ge(op_evac, DEC)
            for k in range(KR):
                for g in range(4):
                    w, half = g // 2, g % 2
                    last = mm(ps[32 * g:32 * g + 32, 7, 0:SHIFT], ones[:, 0:32],
                              sq[:, KR * w + k, SHIFT * half:SHIFT * (half + 1)], start=(k == 0), stop=(k == KR - 1))
            last.then_inc(outproj_pe, 1)
            pe.wait_ge(wo_scaled, 1)
            project_out(1)
            pe.wait_ge(combine_dve, 1)
            nc.tensor.transpose(ps[:, 4, 0:DEC], fin[:, 0:P], ident[0:DEC, 0:DEC])
            mm(ps[:, 4, 64:128], ones[0:DEC, :], fin[:, 384:448], start=True, stop=True).then_inc(combine_pe, 1)
            pe.wait_ge(outproj_act, 1)
            for n in range(2):
                last = nc.tensor.transpose(ps[:, 6, n * P:(n + 1) * P], ss[:, n * P:(n + 1) * P], ident[:, :])
            last.then_inc(outproj_pe, 1)
            pe.wait_ge(exp_done, 4 * NH)
            project_out(2)
            pe.wait_ge(combine_dve, 2)
            for g in range(4):
                last = mm(ps[32 * g:32 * g + 32, 5, :], sel[:, :], op[:, 2 * g:2 * g + 2, :].rearrange("p a b -> p (a b)"),
                          start=True, stop=True)
            last.then_inc(combine_pe, 1)
            project_out(3)
            pe.wait_ge(combine_act, 3)
            for n in range(4):
                last = nc.tensor.transpose(ps[:, 4, n * P:(n + 1) * P], osum[:, n * P:(n + 1) * P], ident[:, :])
            last.then_inc(combine_pe, 1)
            project_out(4)
            landed(pe, uv2_landed)
            pe.wait_ge(combine_dve, 3)
            for h in range(NH):
                for kc in range(KKV):
                    last = mm(ps[64 * (h % 2):64 * (h % 2) + 64, 5, 8 * (h // 2):8 * (h // 2) + 8],
                              uv2[:, kc, h * VH:(h + 1) * VH], oT[:, kc, h, :], start=(kc == 0), stop=(kc == KKV - 1))
            last.then_inc(combine_pe, 1)
            project_out(5)
            turn_x1(0)
            pe.wait_ge(sq_done, 3)
            for w in range(2):
                for k in range(KR):
                    last = mm(ps[0:DEC, 5, w:w + 1], sq[:, KR * w + k, SEQ:TOK], ones[:, 0:1],
                              start=(k == 0), stop=(k == KR - 1))
            last.then_inc(outproj_pe, 1)
            for k in range(KR):
                for g in range(4):
                    w, n = g // 2, g % 2
                    last = mm(ps[32 * g:32 * g + DEC, 4, :], (attT if w == 0 else recT)[:, k, SEQ:TOK],
                              wo[:, KR * w + k, n * 512:(n + 1) * 512], start=(k == 0), stop=(k == KR - 1))
            last.then_inc(outproj_pe, 1)
            for m in (1, 2, 3):
                project_out(5 + m)
                turn_x1(m)

            def logits(half):
                landed(pe, wr_landed)
                pe.wait_ge(x1T_act, 4 + half)
                pe.wait_ge(x1T_dve, 4 + half)
                for k in range(KD):
                    last = mm(ps[64 * half:64 * half + 64, 4, 0:WIN], wr[:, k, :],
                              x1T[:, k, SHIFT * half:SHIFT * half + WIN], start=(k == 0), stop=(k == KD - 1))
                return last
            logits(0)
            turn_x1(4)

            logits(1).then_inc(route_pe, 1)
            pe.wait_ge(route_act, 1)
            nc.tensor.transpose(ps[:, 1, 0:P], rt[:, 0:P], ident[:, :])
            nc.tensor.transpose(ps[:, 1, P:2 * P], rt[:, P:2 * P], ident[:, :])
            nc.tensor.transpose(ps[0:DEC, 1, 2 * P:3 * P], rt[:, 2 * P:WIN], ident[:, :]).then_inc(route_pe, 1)
            pe.wait_ge(route_dve, 1)
            for t in range(TT):
                for q in range(t + 1):
                    mm(ps[:, 2, t * NE:(t + 1) * NE], (trib if q == t else onesb)[:, :], ohb[:, q, :],
                       start=(q == 0), stop=(q == t))
            for q in range(TT):
                last = mm(ps[:, 2, TT * NE:(TT + 1) * NE], onesb[:, :], ohb[:, q, :], start=(q == 0), stop=(q == TT - 1))
            last.then_inc(route_pe, 1)

            def slot_numbers():
                for kt in range(2 * TT):
                    for e in range(2):
                        last = mm(ps[64 * e:64 * e + 64, 3, 0:NE], slot_mark[:, kt, :],
                                  pair_parts[:, kt, e, :, :].rearrange("p a b -> p (a b)"),
                                  start=(kt == 0), stop=(kt == 2 * TT - 1))
                last.then_inc(slots_ps, 1)
            pe.wait_ge(slots_ready, 1)
            slot_numbers()
            pe.wait_ge(routed, 1)
            n_rounds = pe.value_load(rounds[0:1, 0:1], min_val=1, max_val=MAXR)
            turn = [ctx.enter_context(pe.register(f"pe_turn{n}")) for n in range(NPAIR + 1)]
            tokens_in = ctx.enter_context(pe.register("pe_tokens"))

            def turn_tokens(q, landings, before):
                pe.wait_ge(routed, 1)
                pe.wait_ge(gathered[q], landings)
                pe.wait_ge(xt_sb, before)
                for k in range(KD):
                    last = nc.tensor.transpose(ps[:, k // 4, (k % 4) * P:(k % 4 + 1) * P],
                                               xg[q][:, k * P:(k + 1) * P], ident[:, :])
                last.then_inc(xt_ps, 1)

            def experts(q, slots, landed_count, this, before, landings):
                pe.wait_ge(xt_sb, this)
                pe.wait_ge(gu_landed[slots], landed_count)
                for k in range(KD):
                    for e in range(2):
                        last = mm(ps[64 * e:64 * e + 64, 2 + q, :], xgT[:, k, CAP * e:CAP * (e + 1)],
                                  gu_w[2 * slots + e][:, k, :], start=(k == 0), stop=(k == KD - 1))
                last.then_inc(gu_ps, 1)
                turn_tokens(1 - q, landings, this)
                pe.wait_ge(routed, 1)
                pe.wait_ge(h_ready, this)
                for f in range(2):
                    last = nc.tensor.transpose(ps[:, 4, f * P:(f + 1) * P], hx[:, f * P:(f + 1) * P], ident[:, :])
                last.then_inc(ht_ps, 1)
                pe.wait_ge(ht_sb, this)
                pe.wait_ge(dn_landed[slots], landed_count)
                pe.wait_ge(ya_done, before)
                pe.wait_ge(yd_done, before)
                for n in range(2):
                    for f in range(2):
                        for e in range(2):
                            last = mm(ps[64 * e:64 * e + 64, 5 + n, :], hT[:, f, CAP * e:CAP * (e + 1)],
                                      dn_w[2 * slots + e][:, f, n * 512:(n + 1) * 512], start=(f == 0), stop=(f == 1))
                last.then_inc(dn_ps, 1)

            turn_tokens(0, 16, 0)
            with pe.Fori(0, n_rounds) as it:
                pe.wait_ge(slots_ready, it + 2)
                slot_numbers()

            experts(0, 0, 32, 1, 0, 16)
            experts(1, 1, 32, 2, 1, 32)
            experts(0, 2, 32, 3, 2, 32)
            with pe.Fori(0, n_rounds * (NE // 4) - 2) as it:
                for n in range(NPAIR + 1):
                    pe.reg_mov(turn[n], it * NPAIR + 3 + n)
                pe.reg_mov(tokens_in, it * 16 + 48)
                experts(1, 0, it * 32 + 64, turn[1], turn[0], tokens_in)
                experts(0, 1, it * 32 + 64, turn[2], turn[1], tokens_in)
            all_but_two = pe.value_load(rounds[0:1, 1:2], min_val=NE // 2 - 2, max_val=MAXR * NE // 2)
            for n in range(2):
                pe.reg_mov(turn[n], all_but_two + n + 1)
            pe.reg_mov(tokens_in, n_rounds * (16 * NGRP) + 16)
            experts(1, 0, n_rounds * (32 * NE // 4), turn[1], turn[0], tokens_in)

            pe.wait_ge(mixer_ready, 1)
            pe.wait_ge(xt_sb, n_rounds * (NGRP * NPAIR) + 1)
            pe.wait_ge(ya_done, n_rounds * (NGRP * NPAIR))
            pe.wait_ge(yd_done, n_rounds * (NGRP * NPAIR))
            for m, t in enumerate(LAST_ORDER):
                if m == 0:
                    continue
                landed(pe, y_landed[t], 2)
                if m >= 3:
                    pe.wait_ge(y_sum, m - 1)
                for h in range(2):
                    for w, y in enumerate((y1, y2)):
                        last = mm(ps[:, 2 * (m % 2) + h, :], mixer[:, w * 4 + t, :], y[t][:, h * 512:(h + 1) * 512],
                                  start=(w == 0), stop=(w == 1))
                last.then_inc(y_mixed, 1)

        @block.scalar
        def _(act):
            fn = nc.scalar.activation
            act.dma_start(vec[:, :], vecs).then_inc(params_landed, 16)
            act.dma_start(cdec[:, :, 0:CONV - 1, :], conv_st).then_inc(params_landed, 16)
            act.dma_start(rst[:, :, :], rec_st).then_inc(params_landed, 16)
            act.dma_start(cs[64:128, :], cs_tab).then_inc(cs_landed, 16)
            act.dma_start(pages[:, :], page_rep).then_inc(pages_landed, 16)
            act.dma_start(lane_sb[:, :], lane).then_inc(pages_landed, 16)
            act.dma_start(id_sb[:, :, :], ids).then_inc(ids_landed, 16)
            act.dma_start(count_sb[:, :], count.partition_broadcast(P)).then_inc(ids_landed, 16)
            act.dma_start(rbias[:, :], r_bias.partition_broadcast(P)).then_inc(ids_landed, 16)
            act.wait_ge(lam_ready, 1)
            fn(lam[:, 1, :], lam[:, 0, :], ACT.Exp).then_inc(sp_exp, 1)
            for c in range(KR):
                u = U_RX + c
                b = 2 * (u % 4)
                act.wait_ge(unit_done, u + 1)
                nc.scalar.copy(xp[:, c, 3:3 + HALF], ps[:, b, 0:HALF])
                nc.scalar.copy(xp[:, c, 3 + HALF:3 + SEQ], ps[:, b + 1, 0:SEQ - HALF])
                nc.scalar.copy(cdec[:, c, CONV - 1, :], ps[:, b + 1, SEQ - HALF:HALF]).then_inc(evac[u % 4], 1)
            for k in range(KKV):
                u = U_KV + k
                act.wait_ge(unit_done, u + 1)
                nc.scalar.copy(kvz[:, k, :].rearrange("p (a b) -> p a b", a=2), pair(u)).then_inc(evac[u % 4], 1)
            for k in range(KQ):
                u = U_Q + k
                act.wait_ge(unit_done, u + 1)
                nc.scalar.copy(qz[:, k, :].rearrange("p (a b) -> p a b", a=2), pair(u)).then_inc(evac[u % 4], 1)
            act.wait_ge(lam_ready, 2)
            for c in range(KR):
                u = U_R + c
                act.wait_ge(unit_done, u + 1)
                fn(tr[:, c, :].rearrange("p (a b) -> p a b", a=2), pair(u), ACT.Tanh, bias=bh[:, 0, c:c + 1],
                   scale=0.5).then_inc(evac[u % 4], 1)
            for c in range(KR):
                u = U_I + c
                act.wait_ge(unit_done, u + 1)
                if c == 3:
                    act.wait_ge(ix_done, 1)
                fn(tmp[:, c % 3, :].rearrange("p (a b) -> p a b", a=2), pair(u), ACT.Tanh, bias=bh[:, 1, c:c + 1],
                   scale=0.5).then_inc(evac[u % 4], 1)
            act.wait_ge(conv_done, KR)
            for c in range(KR):
                act.wait_ge(evac[(U_R + c) % 4], (U_R + c) // 4 + 1)
                fn(xp[:, c, :], tr[:, c, :], ACT.Exp, bias=nsp[:, 0, c:c + 1], scale=nsp[:, 0, c:c + 1]).then_inc(a_done, 1)
                act.wait_ge(a_done, c + 1)
                fn(tr[:, c, :], tr[:, c, :], ACT.Tanh, bias=nsp[:, 1, c:c + 1], scale=nsp[:, 1, c:c + 1]).then_inc(th_done, 1)
            for n, (u, dst, width) in enumerate(((U_NQ, rq, QL), (U_NKV, rkv, KVL))):
                act.wait_ge(unit_done, u + 1)
                if n == 0:
                    act.wait_ge(kpe_done, 1)
                fn(dst.rearrange("p (a b) -> p a b", a=2), pair(u), ACT.Sqrt, bias=eps[:, 0:1],
                   scale=1.0 / width).then_inc(evac[u % 4], 1)
            for c in range(KR):
                act.wait_ge(w_done, c + 1)
                fn(tr[:, c, :], tr[:, c, :], ACT.Sqrt, scale=0.25).then_inc(root_w, 1)
            for c in range(KR):
                u = U_G + c
                act.wait_ge(unit_done, u + 1)
                fn(recT[:, c, :].rearrange("p (a b) -> p a b", a=2), pair(u), ACT.Gelu_apprx_tanh).then_inc(evac[u % 4], 1)
            act.wait_ge(kpe_done, 1)
            nc.scalar.copy(kh[64:96, :, :], kpe[64:96, 0:SEQ].unsqueeze(1).broadcast_to([ROPE, NH, SEQ])).then_inc(khrope_done, 1)
            for n in range(4):
                u = U_UK + n
                act.wait_ge(unit_done, u + 1)
                nc.scalar.copy(kh[0:64, 2 * n, :], ps[0:64, 2 * (u % 4), :])
                nc.scalar.copy(kh[0:64, 2 * n + 1, :], ps[64:128, 2 * (u % 4), :]).then_inc(evac[u % 4], 1)
            act.wait_ge(ql_done, 1)
            nc.scalar.copy(qlt, ps[:, 6, :]).then_inc(ql_evac, 1)

            def prob(h, i):
                n = 4 * h + i
                act.wait_ge(nm_done, n + 1)
                if h == 1:
                    act.wait_ge(h_done, KR + 1)
                if h >= 2:
                    act.wait_ge(t_done, turn_no(h - 2, "h3") + 1)
                if n >= 2:
                    act.wait_ge(p_done, n - 1)
                fn(Pb[h % 2][:, OFF[i]:OFF[i] + P * (i + 1)], ps[:, n % 2, 0:P * (i + 1)], ACT.Exp,
                   bias=stat[:, n % 2, 1:2], scale=SM, accum_out=stat[:, n % 2, 2:3]).then_inc(exp_done, 1)

            def head_out(hp):
                act.wait_ge(pv_done, hp + 1)
                nc.scalar.copy(attT[:, hp, 0:SEQ], ps[:, 5, :]).then_inc(att_done, 1)

            def cache_prob(s):
                act.wait_ge(dmx_done, s + 1)
                if s >= 1:
                    act.wait_ge(t_done, turn_no(s, "p") + 1)
                fn(dP, ps[:, 6, :], ACT.Exp, bias=nmd[:, 0:1], scale=SM, accum_out=ls[:, s:s + 1]).then_inc(dexp_done, 1)

            def part_out(s):
                act.wait_ge(op_done, s + 1)
                nc.scalar.copy(op[:, s, :], ps[:, 7, 0:KVL]).then_inc(op_evac, 1)

            for i in range(4):
                prob(0, i)
            for s in range(NH):
                out = lambda what: turned(act, nc.scalar.copy, out_act, s, what)
                more = s + 1 < NH
                if more:
                    prob(s + 1, 0)
                out(0)
                if s >= 2 and s % 2 == 0:
                    head_out(s // 2 - 1)
                out("h0")
                if more:
                    prob(s + 1, 1)
                out(6)
                if s >= 1:
                    part_out(s - 1)
                if more:
                    prob(s + 1, 2)
                out(1)
                out(5)
                out(8)
                if more:
                    prob(s + 1, 3)
                cache_prob(s)
                out("h3")
            head_out(NH // 2 - 1)
            fn(sq[:, KR:KD, :], recT, ACT.Square).then_inc(sq_done, 1)
            act.wait_ge(att_done, NH // 2)
            fn(sq[:, 0:KR, 0:SEQ], attT[:, :, 0:SEQ], ACT.Square).then_inc(sq_done, 1)
            part_out(DEC - 1)
            act.wait_ge(combine_pe, 1)
            nc.scalar.copy(fin[:, 0:256], ps[0:DEC, 4, 0:256]).then_inc(combine_act, 1)
            act.wait_ge(outproj_pe, 1)
            nc.scalar.copy(ss, ps[:, 7, 0:SHIFT]).then_inc(outproj_act, 1)
            act.wait_ge(diff_ready, 1)
            for n in range(2):
                a = fin[:, 448 + 0:456] if n else fin[:, 256:384].rearrange("p (i h) -> p i h", i=4)[:, :, 0:NH]
                last = fn(a, a, ACT.Exp, scale=SM)
            last.then_inc(combine_act, 1)
            act.wait_ge(outproj_pe, 2)
            for tt in range(2):
                last = fn(rinv[:, :, :, tt], ps[:, 6, tt * P:(tt + 1) * P].rearrange("p (w h x) -> p w h x", w=2, h=2)[:, :, :, 0],
                          ACT.Sqrt, bias=eps[:, 0:1], scale=1.0 / REC)
            last.then_inc(outproj_act, 1)
            act.wait_ge(combine_pe, 3)
            nc.scalar.copy(osum, ps[:, 5, :]).then_inc(combine_act, 1)

            def ln_act(n, rows, root_sem, norm_sem, var_sem, x, out):
                act.wait_ge(var_sem, 2 * n + 1)
                fn(mv[0:rows, n % 2, 2:3], mv[0:rows, n % 2, 1:2], ACT.Sqrt, bias=eps[0:rows, 1:2]).then_inc(root_sem, 1)
                act.wait_ge(var_sem, 2 * n + 2)
                fn(out, x, ACT.Identity, bias=mv[0:rows, n % 2, 3:4], scale=mv[0:rows, n % 2, 2:3]).then_inc(norm_sem, 1)

            def norm1(m):
                x = x1[0:ROWS[ORDER[m]], ORDER[m], :]
                ln_act(m, ROWS[ORDER[m]], ln_root, ln_norm, ln_var, x, x)

            def x1T_out(m):
                t = ORDER[m]
                act.wait_ge(x1T_ps, m + 1)
                nc.scalar.copy(x1T[:, 0:4, P * t:P * t + ROWS[t]],
                               ps[:, 6, :].rearrange("p (k n) -> p k n", k=4)[:, :, 0:ROWS[t]]).then_inc(x1T_act, 1)

            norm1(0)
            norm1(1)
            act.wait_ge(combine_pe, 5)
            for hp in range(4):
                last = nc.scalar.copy(attT[:, hp, SEQ:TOK], ps[:, 5, 8 * hp:8 * hp + 8])
            last.then_inc(combine_act, 1)
            act.wait_ge(combine_act, 4)
            fn(sq[:, 0:KR, SEQ:TOK], attT[:, :, SEQ:TOK], ACT.Square).then_inc(sq_done, 1)
            x1T_out(0)
            act.wait_ge(outproj_pe, 3)
            fn(rinv4[:, :], ps[0:DEC, 5, 0:2], ACT.Sqrt, bias=eps[0:DEC, 0:1], scale=1.0 / REC)
            act.wait_ge(outproj_pe, 4)
            for g in range(4):
                last = nc.scalar.copy(tb[g // 2][0:DEC, (g % 2) * 512:(g % 2 + 1) * 512], ps[32 * g:32 * g + DEC, 4, :])
            last.then_inc(outproj_act, 1)
            norm1(2)
            x1T_out(1)
            norm1(3)
            x1T_out(2)
            x1T_out(3)
            norm1(4)
            x1T_out(4)
            act.wait_ge(route_pe, 1)
            nc.scalar.copy(rt, ps[:, 4, 0:WIN]).then_inc(route_act, 1)

            landed(act, x1_stored, TT)
            act.wait_ge(route_pe, 1)
            for t in range(TT):
                last = nc.scalar.mul(x1[0:ROWS[t], t, :], x1[0:ROWS[t], t, :], ALPHA)
            last.then_inc(mixer_in, 1)

            act.wait_ge(routed, 1)
            n_rounds = act.value_load(rounds[0:1, 0:1], min_val=1, max_val=MAXR)
            with act.Fori(0, n_rounds * NGRP) as it:
                for q in range(NPAIR):
                    t = it * NPAIR + q
                    act.wait_ge(gu_ps, t + 1)
                    fn(sg, ps[:, 2 + q, 0:DE], ACT.Silu).then_inc(silu_done, 1)
                    act.wait_ge(ht_ps, t + 1)
                    nc.scalar.copy(hT, ps[:, 4, 0:2 * P].rearrange("p (f n) -> p f n", f=2)).then_inc(ht_sb, 1)
                    act.wait_ge(dn_ps, t + 1)
                    act.wait_ge(scattered[q], it * 16)
                    nc.scalar.copy(yb[q][:, 0:512], ps[:, 5, :]).then_inc(ya_done, 1)

            act.wait_ge(route_dve, 2)
            fn(rt_t[:, :, 0:NG], rt_t[:, :, 0:NG], ACT.Exp).then_inc(route_act, 1)
            act.wait_ge(route_dve, 3)
            fn(rs[:, 6:8, :], rs[:, 6:8, :], ACT.Exp).then_inc(route_act, 1)

            for m, t in enumerate(LAST_ORDER):
                n = ROWS[t]
                out = y2[t][0:n, :].rearrange("p (a b) -> p a b", a=2)
                if t in DVE_TILES:
                    d = DVE_TILES.index(t)
                    out = ps[0:n, 4 + 2 * (d % 2):6 + 2 * (d % 2), :]
                    if d >= 2:
                        act.wait_ge(g2_done, d - 1)
                ln_act(m, n, root2, n2_done, v2_done, x1[0:n, t, :].rearrange("p (a b) -> p a b", a=2), out)

        @block.vector
        def _(dve):
            steps = [0]

            def step(ins):
                steps[0] += 1
                ins.then_inc(dve_step, 1)

            def settle():
                dve.wait_ge(dve_step, steps[0])

            def link(ins):
                step(ins)
                settle()

            V = nc.vector
            tt, ts, stt = V.tensor_tensor, V.tensor_scalar, V.scalar_tensor_tensor
            V.memset(ones[:, :], 1.0).then_inc(ones_ready, 1)
            step(V.memset(eps[:, 0:1], RMS_EPS))
            step(V.memset(eps[:, 1:2], LN_EPS))
            step(V.memset(xp[:, :, 0:3], 0.0))
            landed(dve, params_landed, 3)
            lam_in = vec[:, V_LAM:V_LAM + KR]
            link(ts(lam[:, 0, :], lam_in, -1.0, None, ALU.mult))
            link(tt(lam[:, 2, :], lam[:, 0, :], lam_in, ALU.max))
            ts(lam[:, 0, :], lam[:, 2, :], -1.0, None, ALU.mult).then_inc(lam_ready, 1)
            dve.wait_ge(sp_exp, 1)
            link(ts(lam[:, 2, :], lam[:, 1, :], 2.0, None, ALU.add))
            link(V.reciprocal(lam[:, 2, :], lam[:, 2, :]))
            link(tt(lam[:, 2, :], lam[:, 1, :], lam[:, 2, :], ALU.mult))
            link(tt(lam[:, 3, :], lam[:, 2, :], lam[:, 2, :], ALU.mult))
            link(V.memset(lam[:, 4, :], 1.0 / 17))
            for n in range(15, 0, -2):
                link(tt(lam[:, 4, :], lam[:, 4, :], lam[:, 3, :], ALU.mult))
                link(ts(lam[:, 4, :], lam[:, 4, :], 1.0 / n, None, ALU.add))
            link(tt(lam[:, 4, :], lam[:, 4, :], lam[:, 2, :], ALU.mult))
            link(ts(lam[:, 5, :], lam_in, -1.0, 0.0, ALU.mult, ALU.max))
            link(stt(lam[:, 4, :], lam[:, 4, :], 2.0, lam[:, 5, :], ALU.mult, ALU.add))
            step(ts(nsp[:, 0, :], lam[:, 4, :], -4.0, None, ALU.mult))
            step(ts(nsp[:, 1, :], lam[:, 4, :], 4.0, None, ALU.mult))
            step(ts(bh[:, 0, :], vec[:, V_BR:V_BR + KR], 0.5, None, ALU.mult))
            ts(bh[:, 1, :], vec[:, V_BI:V_BI + KR], 0.5, None, ALU.mult).then_inc(lam_ready, 1)
            landed(dve, pages_landed, 2)
            link(ts(pages[:, :], pages[:, :], 8, None, ALU.mult))
            tt(pages[:, :], pages[:, :], lane_sb[:, 0:1].broadcast_to([P, DEC]), ALU.add).then_inc(cidx_ready, 1)
            settle()
            for c in range(KR):
                u = U_RX + c
                dve.wait_ge(evac[u % 4], u // 4 + 1)
                step(V.tensor_copy(conv_tail[:, c, :], xp[:, c, SEQ:SEQ + 3]))
                w = vec[:, V_CW + CONV * c:V_CW + CONV * (c + 1)]
                step(ts(xc[:, c, 0:SEQ], xp[:, c, 0:SEQ], w[:, 0:1], vec[:, V_CB + c:V_CB + c + 1], ALU.mult, ALU.add))
                step(ts(xc[:, c, SEQ:TOK], cdec[:, c, 0, :], w[:, 0:1], vec[:, V_CB + c:V_CB + c + 1], ALU.mult, ALU.add))
                for k in range(1, CONV):
                    settle()
                    step(stt(xc[:, c, 0:SEQ], xp[:, c, k:k + SEQ], w[:, k:k + 1], xc[:, c, 0:SEQ], ALU.mult, ALU.add))
                    last = stt(xc[:, c, SEQ:TOK], cdec[:, c, k, :], w[:, k:k + 1], xc[:, c, SEQ:TOK], ALU.mult, ALU.add)
                    if k + 1 < CONV:
                        step(last)
                last.then_inc(conv_done, 1)
            landed(dve, cs_landed)
            dve.wait_ge(unit_done, U_KPE + 1)
            two = lambda a: a.rearrange("p (a b) -> p a b", a=2)
            b = 2 * (U_KPE % 4)
            step(tt(two(rq[64:96, :]), ps[96:128, b:b + 2, 0:HALF], two(cs[96:128, :]), ALU.mult))
            tt(two(kpe[64:96, :]), ps[64:96, b:b + 2, 0:HALF], two(cs[64:96, :]), ALU.mult).then_inc(evac[U_KPE % 4], 1)
            settle()
            dve.wait_ge(evac[U_KPE % 4], U_KPE // 4 + 1)
            tt(kpe[64:96, :], kpe[64:96, :], rq[64:96, :], ALU.add).then_inc(kpe_done, 1)
            for c in range(KR):
                u = U_I + c
                dve.wait_ge(evac[u % 4], u // 4 + 1)
                stt(xc[:, c, :], tmp[:, c % 3, :], 1.0, xc[:, c, :], ALU.add, ALU.mult).then_inc(ix_done, 1)
            for c in range(KR):
                dve.wait_ge(th_done, c + 1)
                dve.wait_ge(a2_done, c + 1)
                stt(tr[:, c, :], tmp[:, c % 3, :], 1.0, tr[:, c, :], ALU.add, ALU.mult).then_inc(w_done, 1)
            dve.wait_ge(evac[U_NQ % 4], U_NQ // 4 + 1)
            link(V.reciprocal(rq, rq))
            tt(rq[64:128, :], rq[64:128, :], cs[64:128, :], ALU.mult).then_inc(rq_done, 1)
            dve.wait_ge(evac[U_NKV % 4], U_NKV // 4 + 1)
            link(V.reciprocal(rkv, rkv))
            step(stt(kvz[:, 0, :], kvz[:, 0, :], vec[:, V_KVG:V_KVG + 1], rkv, ALU.mult, ALU.mult))
            stt(kvz[:, 1, :], kvz[:, 1, :], vec[:, V_KVG + 1:V_KVG + 2], rkv, ALU.mult, ALU.mult).then_inc(ckv_done, 1)
            for c in range(KR):
                dve.wait_ge(root_w, c + 1)
                dve.wait_ge(ix_done, c + 1)
                link(tt(xc[:, c, :], tr[:, c, :], xc[:, c, :], ALU.mult))
                V.tensor_tensor_scan(xc[:, c, 0:SEQ], xp[:, c, 0:SEQ], xc[:, c, 0:SEQ], 0.0, ALU.mult,
                                     ALU.add).then_inc(h_done, 1)
            dve.wait_ge(h_done, KR)
            step(V.tensor_copy(rec_last[:, :], xc[:, :, SEQ - 1]))
            link(tt(rst[:, :, :], xp[:, :, SEQ:TOK], rst[:, :, :], ALU.mult))
            tt(xc[:, :, SEQ:TOK], xc[:, :, SEQ:TOK], rst[:, :, :], ALU.add).then_inc(h_done, 1)
            dve.wait_ge(rq_done, 1)
            for h in range(NH):
                u = U_UQ + h
                b = 2 * (u % 4)
                dve.wait_ge(unit_done, u + 1)
                if h >= 2:
                    dve.wait_ge(qrope_done, h - 1)
                step(tt(two(qh[0:64, h, :]), ps[0:64, b:b + 2, 0:HALF], two(rq[0:64, :]), ALU.mult))
                step(tt(two(tmp[64:96, h % 2, :]), ps[96:128, b:b + 2, 0:HALF], two(rq[96:128, :]), ALU.mult))
                tt(two(qh[64:96, h, :]), ps[64:96, b:b + 2, 0:HALF], two(rq[64:96, :]), ALU.mult).then_inc(evac[u % 4], 1)
            dve.wait_ge(rec_done, KR)
            landed(dve, outs_stored, 6)
            step(V.memset(qq[:, :, :], 0.0))
            dve.wait_ge(qrope_done, NH)
            settle()
            for j in range(4):
                step(V.tensor_copy(qq[32 * j:32 * j + 32, :, 64 + 32 * j:64 + 32 * j + NH],
                                   qh[64:96, :, SEQ:TOK].rearrange("p h s -> p s h")))
            step(V.tensor_copy(kpn[:, :], kpe[64:96, SEQ:TOK]))
            for n in range(4):
                u = U_V + n
                dve.wait_ge(unit_done, u + 1)
                V.tensor_copy(v[:, n, :], ps[:, 2 * (u % 4), :]).then_inc(evac[u % 4], 1)
            def absorbed_queries():
                dve.wait_ge(qlT_done, 1)
                for hi in range(2):
                    for kc in range(KKV):
                        n = 2 * hi + kc
                        last = V.tensor_copy(qq[:, :, 32 * kc + 4 * hi:32 * kc + 4 * hi + 4],
                                             ps[:, 7, n * P:(n + 1) * P].rearrange("p (g x) -> p x g", g=4)[:, 32 - DEC:32, :])
                        if n < 3:
                            step(last)
                last.then_inc(qq_done, 1)

            def row_max(h, i):
                n = 4 * h + i
                dve.wait_ge(s_done, n + 1)
                link(V.tensor_reduce(stat[:, n % 2, 0:1], ps[:, n % 2, 0:P * (i + 1)], AX_X, ALU.max))
                if n >= 2:
                    dve.wait_ge(exp_done, n - 1)
                ts(stat[:, n % 2, 1:2], stat[:, n % 2, 0:1], -SM, None, ALU.mult).then_inc(nm_done, 1)

            def normal(h, i):
                n = 4 * h + i
                dve.wait_ge(exp_done, n + 1)
                link(V.reciprocal(stat[:, n % 2, 3:4], stat[:, n % 2, 2:3]))
                pr = Pb[h % 2][:, OFF[i]:OFF[i] + P * (i + 1)]
                ts(pr, pr, stat[:, n % 2, 3:4], None, ALU.mult).then_inc(p_done, 1)

            def queries_of(s):
                if s >= 2:
                    dve.wait_ge(sc_done, s - 1)
                V.tensor_copy(qs[:, s % 2, :], qq[:, s, :]).then_inc(qs_done, 1)

            def cache_max(s):
                dve.wait_ge(sc_done, s + 1)
                V.tensor_reduce(mx[:, s:s + 1], ps[:, 6, :], AX_X, ALU.max).then_inc(dmax_raw, 1)
                dve.wait_ge(dmax_raw, s + 1)
                if s >= 1:
                    dve.wait_ge(dexp_done, s)
                ts(nmd[:, 0:1], mx[:, s:s + 1], -SM, None, ALU.mult).then_inc(dmx_done, 1)

            row_max(0, 0)
            for i in range(1, 4):
                row_max(0, i)
                normal(0, i - 1)
            absorbed_queries()
            normal(0, 3)
            dve.wait_ge(qq_done, 1)
            for s in range(NH):
                out = lambda what: turned(dve, V.tensor_copy, out_dve, s, what)
                more = s + 1 < NH
                queries_of(s)
                if more:
                    row_max(s + 1, 0)
                if s >= 1:
                    out("p")
                out(2)
                if more:
                    row_max(s + 1, 1)
                    normal(s + 1, 0)
                out(4)
                out("h1")
                if more:
                    row_max(s + 1, 2)
                    normal(s + 1, 1)
                out(3)
                out(7)
                if more:
                    row_max(s + 1, 3)
                    normal(s + 1, 2)
                cache_max(s)
                if more:
                    normal(s + 1, 3)
                out("h2")
            turned(dve, V.tensor_copy, out_dve, DEC, "p")
            dve.wait_ge(const_ready, 4)
            step(V.tensor_reduce(sel[:, :], ident[:, :].rearrange("p (b m) -> p m b", b=4), AX_X, ALU.add))
            e8 = ident[0:DEC, 0:DEC].unsqueeze(2).broadcast_to([DEC, DEC, NH])
            snew, M, LL, wn = fin[:, 448:456], fin[:, 456:464], fin[:, 464:472], fin[:, 448:456]
            sd = fin[:, 384:448].rearrange("p (s h) -> p s h", s=DEC)
            parts = lambda at: fin[:, at:at + P].rearrange("p (i h) -> p i h", i=4)[:, :, 0:NH]
            dve.wait_ge(combine_pe, 1)
            link(tt(sd, ps[0:DEC, 5, 0:64].rearrange("p (s h) -> p s h", s=DEC), e8, ALU.mult))
            link(V.tensor_reduce(snew, sd.rearrange("p s h -> p h s"), AX_X, ALU.add))
            dve.wait_ge(combine_act, 1)
            link(V.tensor_reduce(M, parts(0).rearrange("p i h -> p h i"), AX_X, ALU.max))
            link(tt(M, M, snew, ALU.max))
            step(V.memset(fin[:, 256:384], 0.0))
            settle()
            step(tt(parts(256), parts(0), M.unsqueeze(1).broadcast_to([DEC, 4, NH]), ALU.subtract))
            tt(wn, snew, M, ALU.subtract).then_inc(diff_ready, 1)
            dve.wait_ge(combine_act, 2)
            link(tt(parts(128), parts(128), parts(256), ALU.mult))
            link(V.tensor_reduce(LL, parts(128).rearrange("p i h -> p h i"), AX_X, ALU.add))
            link(tt(LL, LL, wn, ALU.add))
            link(V.reciprocal(LL, LL))
            step(V.memset(fin[:, 0:P], 0.0))
            link(tt(wn, wn, LL, ALU.mult))
            step(tt(parts(0), parts(256), LL.unsqueeze(1).broadcast_to([DEC, 4, NH]), ALU.mult))
            settle()
            tt(sd, e8, wn.unsqueeze(1).broadcast_to([DEC, DEC, NH]), ALU.mult).then_inc(combine_dve, 1)
            dve.wait_ge(combine_pe, 2)
            link(V.tensor_copy(wcol[:, :], ps[:, 4, 0:DEC]))
            for kc in range(KKV):
                step(tt(tn[:, kc, :, :], ps[:, 4, 64:128].rearrange("p (s h) -> p s h", s=DEC),
                        kvz[:, kc, SEQ:TOK].unsqueeze(2).broadcast_to([P, DEC, NH]), ALU.mult))
            dve.wait_ge(op_evac, DEC)
            for s in range(DEC):
                last = ts(op[:, s, :], op[:, s, :], wcol[:, s:s + 1], None, ALU.mult)
                if s < DEC - 1:
                    step(last)
            last.then_inc(combine_dve, 1)
            def latent_outputs():
                dve.wait_ge(combine_pe, 4)
                settle()
                for s1 in range(2):
                    for kc in range(KKV):
                        n = 2 * s1 + kc
                        last = tt(oT[:, kc, :, s1:DEC:2].rearrange("p h g -> p g h"),
                                  ps[:, 4, n * P:(n + 1) * P].rearrange("p (g x) -> p g x", g=4)[:, :, 0:NH],
                                  tn[:, kc, s1:DEC:2, :], ALU.add)
                        if n < 3:
                            step(last)
                last.then_inc(combine_dve, 1)

            dve.wait_ge(outproj_act, 2)
            link(V.reciprocal(rinv[:, :, :, :].rearrange("p a b c -> p (a b c)"), rinv[:, :, :, :].rearrange("p a b c -> p (a b c)")))

            def project_out(m):
                t, n = (m - 1) // 2, (m - 1) % 2
                x = x1[:, t, n * 512:(n + 1) * 512]
                dve.wait_ge(o_done, m)
                for w in range(2):
                    last = stt(x, ps[:, 2 * (m % 2) + w, :], rinv[:, w, t // 2, t % 2:t % 2 + 1], x, ALU.mult, ALU.add)
                    if w == 0:
                        link(last)
                last.then_inc(o_out, 1)

            def ln_stats(x, n, rows, root_sem, var_sem):
                for q in range(2):
                    step(V.bn_stats(bn[0:rows, q, :], x[:, q * 512:(q + 1) * 512]))
                settle()
                V.bn_aggr(mv[0:rows, n % 2, 0:2], bn[0:rows, :, :]).then_inc(var_sem, 1)
                dve.wait_ge(root_sem, n + 1)
                link(V.reciprocal(mv[0:rows, n % 2, 2:3], mv[0:rows, n % 2, 2:3]))
                stt(mv[0:rows, n % 2, 3:4], mv[0:rows, n % 2, 0:1], -1.0, mv[0:rows, n % 2, 2:3], ALU.mult,
                    ALU.mult).then_inc(var_sem, 1)

            def norm1(m):
                rows = ROWS[ORDER[m]]
                x = x1[0:rows, ORDER[m], :]
                ln_stats(x, m, rows, ln_root, ln_var)
                dve.wait_ge(ln_norm, m + 1)
                link(tt(x, x, lng[0:rows, 0, :], ALU.mult))
                tt(x, x, lng[0:rows, 1, :], ALU.add).then_inc(x1_done, 1)

            def x1T_out(m):
                t = ORDER[m]
                dve.wait_ge(x1T_ps, m + 1)
                V.tensor_copy(x1T[:, 4:8, P * t:P * t + ROWS[t]],
                              ps[:, 7, :].rearrange("p (k n) -> p k n", k=4)[:, :, 0:ROWS[t]]).then_inc(x1T_dve, 1)

            dve.wait_ge(xa_done, 1)
            landed(dve, ln1_landed)
            project_out(1)
            project_out(2)
            dve.wait_ge(o_out, 2)
            norm1(0)
            latent_outputs()
            project_out(3)
            project_out(4)
            dve.wait_ge(o_out, 4)
            norm1(1)
            project_out(5)
            x1T_out(0)
            dve.wait_ge(outproj_act, 3)
            link(V.reciprocal(rinv4[:, :], rinv4[:, :]))
            x = x1[0:DEC, 4, :]
            link(stt(x, tb[0][0:DEC, :], rinv4[:, 0:1], x, ALU.mult, ALU.add))
            link(stt(x, tb[1][0:DEC, :], rinv4[:, 1:2], x, ALU.mult, ALU.add))
            norm1(2)
            project_out(6)
            dve.wait_ge(o_out, 6)
            x1T_out(1)
            norm1(3)
            project_out(7)
            x1T_out(2)
            project_out(8)
            dve.wait_ge(o_out, 8)
            x1T_out(3)
            norm1(4)
            x1T_out(4)

            landed(dve, ids_landed, 3)
            link(V.memset(L[:, :, :], 0.0))
            step(V.memset(gpad[:, :, NG:8], -3e38))
            link(V.memset(valid[:, 0:4], 1.0))
            link(V.memset(valid[:, 4:5], 0.0))
            link(V.memset(valid[0:DEC, 4:5], 1.0))
            dve.wait_ge(route_pe, 2)
            for n in range(2):
                step(V.tensor_copy(L[:, 0:4, :].rearrange("p (h t) n -> p t h n", h=2)[:, n],
                                   ps[:, 1, n * P:(n + 1) * P].rearrange("p (h x) -> p h x", h=2)[:, :, 0:NG + NE]))
            link(V.tensor_copy(L[0:DEC, 4, :], ps[0:DEC, 1, 2 * P + 64:2 * P + 64 + NG + NE]))
            bc = lambda a, n: a.unsqueeze(1).broadcast_to([P, TT, n])
            per = lambda a, n: a.unsqueeze(2).broadcast_to([P, TT, n])
            link(tt(Lb, L, bc(rbias[:, :], NG + NE), ALU.add))
            link(V.tensor_copy(gpad[:, :, 0:NG], Lb[:, :, 0:NG]))
            for t in range(TT):
                step(V.max(top8[:, t, :], gpad[:, t, :]))
            settle()
            for t in range(TT):
                step(V.max_index(idx8[:, t, :], top8[:, t, :], gpad[:, t, :]))
            settle()
            link(V.tensor_copy(rs[:, 0, :], idx8[:, :, 0]))
            link(tt(ohg[:, :, :], bc(count_sb[:, 0:NG], NG), per(rs[:, 0, :], NG), ALU.is_equal))
            link(ts(rt_t[:, :, 0:NG], ohg[:, :, :], 1.0, 1e30, ALU.subtract, ALU.mult))
            for t in range(TT):
                step(tt(me[:, t, :].rearrange("p (g e) -> p g e", g=NG), Lb[:, t, NG:].rearrange("p (g e) -> p g e", g=NG),
                        rt_t[:, t, 0:NG].unsqueeze(2).broadcast_to([P, NG, EPG]), ALU.add))
            settle()
            for t in range(TT):
                step(V.max(top8[:, t, :], me[:, t, :]))
            settle()
            for t in range(TT):
                step(V.max_index(idx8[:, t, :], top8[:, t, :], me[:, t, :]))
            settle()
            step(V.tensor_copy(rs[:, 1, :], idx8[:, :, 0]))
            link(V.tensor_copy(rs[:, 2, :], idx8[:, :, 1]))
            step(tt(oh1, bc(count_sb[:, 0:NE], NE), per(rs[:, 1, :], NE), ALU.is_equal))
            link(tt(oh2, bc(count_sb[:, 0:NE], NE), per(rs[:, 2, :], NE), ALU.is_equal))
            both = part(arena_s, S_RT + 520, 2, TT, NE)
            link(tt(both, both, valid[:, :].unsqueeze(1).unsqueeze(3).broadcast_to([P, 2, TT, NE]), ALU.mult))
            tt(ohb[:, :, :], oh1, oh2, ALU.add).then_inc(route_dve, 1)
            dve.wait_ge(route_dve, 1)
            prod = part(arena_s, S_E + 320, 2, TT, NE)
            for h in range(2):
                step(tt(pair_parts[:, :, :, h, :], part(arena_s, S_RT + 520, 2 * TT, NE).rearrange("p a (b q) -> p a q b", q=2),
                        id_sb[:, :, h:h + 1].unsqueeze(3).broadcast_to([P, 2 * TT, 2, NE // 2]), ALU.mult))
            dve.wait_ge(route_pe, 3)
            link(tt(prod, both, ps[:, 2, 0:TT * NE].rearrange("p (t e) -> p t e", t=TT).unsqueeze(1).broadcast_to([P, 2, TT, NE]), ALU.mult))
            link(V.tensor_reduce(rs[:, 14:16, :], prod, AX_X, ALU.add))
            rank = rs[:, 14:16, :].rearrange("p a b -> p (a b)")

            def mark_slots():
                tt(slot_mark, count_sb[:, :].unsqueeze(1).broadcast_to([P, 2 * TT, CAP]),
                   rank.unsqueeze(2).broadcast_to([P, 2 * TT, CAP]), ALU.is_equal).then_inc(slots_ready, 1)

            def slot_table_out():
                hi, lo = ps[:, 3, 0:NE // 2], ps[:, 3, NE // 2:NE]
                link(ts(table[:, 0, :], hi, float(CAP), None, ALU.mult))
                link(tt(table[:, 1, :], table[:, 0, :], lo, ALU.add))
                link(ts(table[:, 2, :], table[:, 1, :], 0.0, float(FREE_SLOT + 1), ALU.is_equal, ALU.mult))
                return stt(table_i[:, :], table[:, 1, :], -1.0, table[:, 2, :], ALU.add, ALU.add)

            mark_slots()
            link(V.tensor_reduce(rs[:, 13, 0:1], ps[:, 2, TT * NE:(TT + 1) * NE], AX_X, ALU.max))
            link(ts(rs[:, 13, 1:2], rs[:, 13, 0:1], float(CAP - 1), None, ALU.add))
            link(V.tensor_copy(rounds[:, 1:2], rs[:, 13, 1:2]))
            link(ts(rounds[:, 0:1], rounds[:, 1:2], 6, None, ALU.arith_shift_right))
            step(ts(rounds[:, 1:2], rounds[:, 0:1], float(NE // 2), -2.0, ALU.mult, ALU.add))
            dve.wait_ge(slots_ps, 1)
            slot_table_out().then_inc(table_ready, 1)
            dve.wait_ge(table_ready, 1)
            V.tensor_copy(raw[:, :, :].rearrange("p a b -> p (a b)"), table_i[:, 0:2 * NPAIR]).then_inc(routed, 1)
            settle()
            dve.wait_ge(routed, 1)
            n_rounds = dve.value_load(rounds[0:1, 0:1], min_val=1, max_val=MAXR)
            def tokens_out(t):
                dve.wait_ge(xt_ps, t + 1)
                dve.wait_ge(gu_ps, t)
                V.tensor_copy(xgT.rearrange("p (a b) n -> p a b n", a=2),
                              ps[:, 0:2, :].rearrange("p a (b n) -> p a b n", b=4)).then_inc(xt_sb, 1)
            tokens_out(0)
            with dve.Fori(0, n_rounds) as it:
                ts(rank, rank, -float(CAP), None, ALU.add).then_inc(rank_moved, 1)
                dve.wait_ge(rank_moved, it + 1)
                mark_slots()
                dve.wait_ge(slots_ps, it + 2)
                hi, lo = ps[:, 3, 0:NE // 2], ps[:, 3, NE // 2:NE]
                ts(table[:, 0, :], hi, float(CAP), None, ALU.mult).then_inc(table_step, 1)
                dve.wait_ge(table_step, it * 3 + 1)
                tt(table[:, 1, :], table[:, 0, :], lo, ALU.add).then_inc(table_step, 1)
                dve.wait_ge(table_step, it * 3 + 2)
                ts(table[:, 2, :], table[:, 1, :], 0.0, float(FREE_SLOT + 1), ALU.is_equal, ALU.mult).then_inc(table_step, 1)
                dve.wait_ge(table_step, it * 3 + 3)
                dve.wait_ge(table_stored, it * 16 + 16)
                stt(table_i[:, :], table[:, 1, :], -1.0, table[:, 2, :], ALU.add, ALU.add).then_inc(table_ready, 1)
            with dve.Fori(0, n_rounds * NGRP) as it:
                for q in range(NPAIR):
                    t = it * NPAIR + q
                    dve.wait_ge(silu_done, t + 1)
                    tt(hx, sg, ps[:, 2 + q, DE:2 * DE], ALU.mult).then_inc(h_ready, 1)
                    tokens_out(t + 1)
                    dve.wait_ge(dn_ps, t + 1)
                    dve.wait_ge(scattered[q], it * 16)
                    V.tensor_copy(yb[q][:, 512:D], ps[:, 6, :]).then_inc(yd_done, 1)

            link(V.tensor_reduce(rs[:, 3, :], L[:, :, 0:NG], AX_X, ALU.max))
            tt(rt_t[:, :, 0:NG], L[:, :, 0:NG], per(rs[:, 3, :], NG), ALU.subtract).then_inc(route_dve, 1)
            link(tt(me, oh1, L[:, :, NG:], ALU.mult))
            link(V.tensor_reduce(rs[:, 4, :], me, AX_X, ALU.add))
            link(tt(me, oh2, L[:, :, NG:], ALU.mult))
            link(V.tensor_reduce(rs[:, 5, :], me, AX_X, ALU.add))
            link(tt(rs[:, 8, :], rs[:, 4, :], rs[:, 5, :], ALU.max))
            step(tt(rs[:, 6, :], rs[:, 4, :], rs[:, 8, :], ALU.subtract))
            tt(rs[:, 7, :], rs[:, 5, :], rs[:, 8, :], ALU.subtract).then_inc(route_dve, 1)
            dve.wait_ge(route_dve, 3)
            dve.wait_ge(route_act, 2)
            link(V.tensor_reduce(rs[:, 8, :], rt_t[:, :, 0:NG], AX_X, ALU.add))
            link(tt(rt_t[:, :, 0:NG], rt_t[:, :, 0:NG], ohg[:, :, :], ALU.mult))
            link(V.tensor_reduce(rs[:, 9, :], rt_t[:, :, 0:NG], AX_X, ALU.add))
            dve.wait_ge(route_act, 3)
            link(tt(rs[:, 12, :], rs[:, 6, :], rs[:, 7, :], ALU.add))
            link(tt(rs[:, 12, :], rs[:, 12, :], rs[:, 8, :], ALU.mult))
            link(V.reciprocal(rs[:, 12, :], rs[:, 12, :]))
            link(tt(rs[:, 12, :], rs[:, 12, :], rs[:, 9, :], ALU.mult))
            step(tt(rs[:, 10, :], rs[:, 12, :], rs[:, 6, :], ALU.mult))
            link(tt(rs[:, 11, :], rs[:, 12, :], rs[:, 7, :], ALU.mult))
            settle()
            for n in range(2):
                for t in range(4):
                    last = ts(mixer[:, n * 4 + t, :], ident[:, :], rs[:, 10 + n, t:t + 1], None, ALU.mult)
                    if n * 4 + t < 7:
                        step(last)
            last.then_inc(mixer_ready, 1)
            landed(dve, ln2_landed)
            dve.wait_ge(mixer_in, 1)

            def total(m):
                t = LAST_ORDER[m]
                n, b = ROWS[t], 2 * (m % 2)
                if m == 0:
                    landed(dve, y_landed[t], 2)
                    for w, y in enumerate((y1, y2)):
                        last = stt(x1[0:n, t, :], y[t][0:n, :], rs[0:n, 10 + w, t:t + 1], x1[0:n, t, :], ALU.mult, ALU.add)
                        if w == 0:
                            link(last)
                else:
                    x = x1[0:n, t, :].rearrange("p (a b) -> p a b", a=2)
                    dve.wait_ge(y_mixed, m)
                    last = tt(x, ps[0:n, b:b + 2, :], x, ALU.add)
                last.then_inc(y_sum, 1)
                dve.wait_ge(y_sum, m + 1)

            def gain(m):
                t = LAST_ORDER[m]
                if t in POOL_TILES:
                    return
                n, d = ROWS[t], DVE_TILES.index(t)
                b = 4 + 2 * (d % 2)
                dve.wait_ge(n2_done, m + 1)
                tt(y1[t][0:n, :].rearrange("p (a b) -> p a b", a=2), ps[0:n, b:b + 2, :],
                   lng2[0:n, 0, :].rearrange("p (a b) -> p a b", a=2), ALU.mult).then_inc(g2_done, 1)
                dve.wait_ge(g2_done, d + 1)
                tt(y1[t][0:n, :], y1[t][0:n, :], lng2[0:n, 1, :], ALU.add).then_inc(y_dve, 1)

            for m, t in enumerate(LAST_ORDER):
                total(m)
                ln_stats(x1[0:ROWS[t], t, :], m, ROWS[t], root2, v2_done)
                if m > 0:
                    gain(m - 1)
            gain(TT - 1)

        @block.gpsimd
        def _(pool):
            G = nc.gpsimd
            steps = [0]

            def step(ins):
                steps[0] += 1
                ins.then_inc(pool_step, 1)

            def settle():
                pool.wait_ge(pool_step, steps[0])

            step(G.memset(ident[:, :], 0.0))
            step(G.memset(identb[:, :], 0.0))
            step(G.memset(maskb[:, :], 0.0))
            step(G.memset(trib[:, :], 1.0))
            step(G.memset(onesb[:, :], 1.0))
            settle()
            for m in (ident, identb):
                G.affine_select(out=m[:, :], in_=m[:, :], compare_op=ALU.not_equal, fill=1.0, base=0,
                                pattern=[[-1, P]], channel_multiplier=1).then_inc(const_ready, 1)
            G.affine_select(out=maskb[:, :], in_=maskb[:, :], compare_op=ALU.is_ge, fill=NEG, base=0,
                            pattern=[[-1, P]], channel_multiplier=1).then_inc(const_ready, 1)
            G.affine_select(out=trib[:, :], in_=trib[:, :], compare_op=ALU.is_gt, fill=0.0, base=0,
                            pattern=[[1, P]], channel_multiplier=-1).then_inc(const_ready, 1)
            landed(pool, params_landed, 3)
            for k in range(KKV):
                u = U_KV + k
                pool.wait_ge(evac[u % 4], u // 4 + 1)
            G.tensor_tensor(sq0[:, KQ:KQ + KKV, :], kvz, kvz, ALU.mult).then_inc(squares, 1)
            for k in range(KQ):
                u = U_Q + k
                pool.wait_ge(evac[u % 4], u // 4 + 1)
            G.tensor_tensor(sq0[:, 0:KQ, :], qz, qz, ALU.mult).then_inc(squares, 1)
            pool.wait_ge(ix_done, KR)
            for c in range(KR):
                pool.wait_ge(a_done, c + 1)
                if c == 3:
                    pool.wait_ge(w_done, 1)
                G.tensor_tensor(tmp[:, c % 3, :], xp[:, c, :], xp[:, c, :], ALU.mult).then_inc(a2_done, 1)
            pool.wait_ge(unit_done, U_Q + KQ)
            pool.wait_ge(cidx_ready, 1)

            def fetch(s):
                for rows, dst in ((kv_rows, buf[s % 3][:, 0:16 * KVL]), (rope_rows, buf[s % 3][:, 16 * KVL:CB])):
                    G.indirect_dma_start(out=dst, out_offset=None, in_=rows,
                                         in_offset=bass.IndirectOffsetOnAxis(ap=pages[:, s:s + 1], axis=0)).then_inc(cache_landed[s % 3], 16)
            fetch(0)
            fetch(1)
            landed(pool, uq_landed)
            for k in range(KQ):
                last = G.tensor_scalar(uq[:, k, :, :], uq[:, k, :, :], vec[:, V_QG + k:V_QG + k + 1], 1.0, ALU.mult, ALU.mult)
                if k < KQ - 1:
                    step(last)
            last.then_inc(wuq_scaled, 1)
            pool.wait_ge(h_done, KR + 1)
            for c in range(KR):
                u = U_G + c
                pool.wait_ge(evac[u % 4], u // 4 + 1)
                G.tensor_tensor(recT[:, c, :], xc[:, c, :], recT[:, c, :], ALU.mult).then_inc(rec_done, 1)
            pool.wait_ge(rec_done, KR)
            for b2 in range(2):
                landed(pool, cache_landed[b2], 2)
            for h in range(NH):
                u = U_UQ + h
                pool.wait_ge(evac[u % 4], u // 4 + 1)
                G.tensor_tensor(qh[64:96, h, :], qh[64:96, h, :], tmp[64:96, h % 2, :], ALU.add).then_inc(qrope_done, 1)
            pool.wait_ge(qrope_done, NH)
            pool.wait_ge(unit_done, N_UNITS)
            fetch(2)
            def gains(k):
                return G.tensor_scalar(wo[:, k, :], wo[:, k, :], vec[:, V_AG + k:V_AG + k + 1], 1.0, ALU.mult, ALU.mult)

            landed(pool, wo_landed[0])
            for k in range(WO_LATE, KD):
                step(gains(k))
            for s in range(3, DEC):
                pool.wait_ge(op_done, s - 2)
                fetch(s)
            landed(pool, wo_landed[1])
            for k in range(WO_LATE):
                last = gains(k)
                if k < WO_LATE - 1:
                    step(last)
            last.then_inc(wo_scaled, 1)
            landed(pool, xtok_landed, TT)
            step(G.tensor_scalar(x1[:, 0:4, :], x1[:, 0:4, :], ALPHA, 1.0, ALU.mult, ALU.mult))
            G.tensor_scalar(x1[0:DEC, 4, :], x1[0:DEC, 4, :], ALPHA, 1.0, ALU.mult, ALU.mult).then_inc(xa_done, 1)

            pool.wait_ge(outproj_pe, 3)
            for j in range(NPAIR):
                step(G.memset(xg[j], 0.0))
            settle()

            pool.wait_ge(routed, 1)
            landed(pool, x1_stored, TT)
            n_rounds = pool.value_load(rounds[0:1, 0:1], min_val=1, max_val=MAXR)

            def load_slots(g, b):
                src = slot_table[g * BLK:(g + 1) * BLK, :] if isinstance(g, int) else slot_table[bass.ds(g * BLK, BLK), :]
                G.dma_start(raw[:, b, :], src.rearrange("(s j) o -> s (j o)", j=NPAIR)).then_inc(raw_landed, 16)

            def gather(q):
                G.indirect_dma_start(out=xg[q], out_offset=None, in_=x1_rows,
                                     in_offset=bass.IndirectOffsetOnAxis(ap=gidx[:, q:q + 1], axis=0),
                                     bounds_check=TOK - 1, oob_is_err=False).then_inc(gathered[q], 16)

            def scatter(q):
                G.indirect_dma_start(out=pair_rows, out_offset=bass.IndirectOffsetOnAxis(ap=sidx[:, q:q + 1], axis=0),
                                     in_=yb[q], in_offset=None, bounds_check=2 * HALF_ID - 1,
                                     oob_is_err=False).then_inc(scattered[q], 16)

            def fixed():
                pool.wait_ge(routed, 1)

            def token_index(b, first, second):
                G.tensor_scalar(gidx[:, :], raw[:, b, :], HALF_ID, -HALF_ID, ALU.is_ge, ALU.mult).then_inc(idx_half, 1)
                fixed()
                pool.wait_ge(idx_half, first)
                G.tensor_tensor(gidx[:, :], gidx[:, :], raw[:, b, :], ALU.add).then_inc(idx_half, 1)
                fixed()
                pool.wait_ge(idx_half, second)

            def store_table(r):
                dst = slot_table[r:r + RBLK, :] if isinstance(r, int) else slot_table[bass.ds(r, RBLK), :]
                G.dma_start(dst.rearrange("(g p q) o -> p g (q o)", g=NGRP, p=P),
                            table_i[:, :].rearrange("p (g q) -> p g q", g=NGRP)).then_inc(table_stored, 16)

            token_index(0, 1, 2)
            for q in range(NPAIR):
                gather(q)
            store_table(0)
            stored = ctx.enter_context(pool.register("stored"))
            with pool.Fori(0, n_rounds) as it:
                pool.reg_mov(stored, it + 2)
                fixed()
                pool.wait_ge(table_ready, stored)
                store_table(it * RBLK + RBLK)
            pool.reg_mov(stored, n_rounds * 16 + 16)
            fixed()
            pool.wait_ge(table_stored, stored)
            turn = [ctx.enter_context(pool.register(f"pool_turn{n}")) for n in range(NPAIR)]
            loads_in, sofar, copied = (ctx.enter_context(pool.register(n)) for n in ("loads_in", "sofar", "copied"))
            tokens_in = ctx.enter_context(pool.register("tokens_in"))
            halves = [ctx.enter_context(pool.register(f"halves{n}")) for n in range(2)]
            with pool.Fori(0, n_rounds * (NGRP // 2)) as it:
                for b in range(2):
                    g = it * 2 + b
                    for q in range(NPAIR):
                        pool.reg_mov(turn[q], g * NPAIR + q + 1)
                    pool.reg_mov(loads_in, g * 16)
                    pool.reg_mov(tokens_in, g * 16 + 16)
                    pool.reg_mov(sofar, g * 16)
                    pool.reg_mov(copied, g + 1)
                    for n in range(2):
                        pool.reg_mov(halves[n], g * 2 + 3 + n)
                    fixed()
                    pool.wait_ge(raw_landed, loads_in)
                    for q in range(NPAIR):
                        pool.wait_ge(gathered[q], tokens_in)
                    token_index(1 - b, *halves)
                    for q in range(NPAIR):
                        fixed()
                        pool.wait_ge(xt_ps, turn[q])
                        gather(q)
                    fixed()
                    for q in range(NPAIR):
                        pool.wait_ge(scattered[q], sofar)
                    G.tensor_copy(sidx[:, :], raw[:, b, :]).then_inc(idx_copied, 1)
                    fixed()
                    pool.wait_ge(idx_copied, copied)
                    load_slots(g + 2, b)
                    for q in range(NPAIR):
                        fixed()
                        pool.wait_ge(ya_done, turn[q])
                        pool.wait_ge(yd_done, turn[q])
                        scatter(q)
            landed(pool, raw_landed, n_rounds * NGRP)
            for q in range(NPAIR):
                landed(pool, gathered[q], n_rounds * NGRP + 1)
            landed(pool, ln2_landed)
            for m, t in enumerate(POOL_TILES):
                pool.wait_ge(n2_done, LAST_ORDER.index(t) + 1)
                G.tensor_tensor(y1[t], y2[t], lng2[:, 0, :], ALU.mult).then_inc(pool_gain, 1)
                pool.wait_ge(pool_gain, m + 1)
                G.tensor_tensor(y1[t], y1[t], lng2[:, 1, :], ALU.add).then_inc(y_pool, 1)


def _lay_out(i):
    f = np.float32
    c = np.ascontiguousarray
    x_tok = np.concatenate([i["x_prompt"].reshape(SEQ, D), i["x_sample"].reshape(DEC, D)], 0)

    def chunks(w, n):
        return w.reshape(n, P, -1).transpose(1, 0, 2)

    w_in = i["w_in"]
    a = QL + KVL
    order = [a + ROPE + P * n for n in range(4)] + [QL, QL + P] + [P * n for n in range(3)] + \
            [a + ROPE + REC + P * n for n in range(4)]
    w_in13 = np.stack([chunks(w_in[:, o:o + P], KD).reshape(P, -1) for o in order])
    hr = ROPE // 2
    kp = w_in[:, a:a + ROPE]
    w_kpe = chunks(np.concatenate([kp, kp[:, hr:], kp[:, :hr]], 1), KD).reshape(P, -1)
    uq = i["w_uq"]
    uq = np.concatenate([uq, uq[:, :, NOPE + hr:], uq[:, :, NOPE:NOPE + hr]], 2)
    w_uq = chunks(uq.reshape(QL, NH * P), KQ).reshape(P, -1)
    w_uk = chunks(i["w_uk"].reshape(KVL, -1), KKV).reshape(P, -1)
    w_uv = chunks(i["w_uv"].reshape(KVL, -1), KKV).reshape(P, -1)
    w_ukT = i["w_uk"].transpose(2, 1, 0).reshape(NOPE, -1)
    cols = lambda v: v.reshape(-1, P).T
    vecs = np.concatenate([cols(i["q_norm_g"]), cols(i["kv_norm_g"]),
                           i["conv_w"].reshape(CONV, KR, P).transpose(2, 1, 0).reshape(P, -1), cols(i["conv_b"]),
                           cols(i["b_rg"]), cols(i["b_ig"]), cols(i["lru_lambda"]), cols(i["att_out_g"]),
                           cols(i["rec_out_g"])], 1)
    gates = np.zeros((P, 2, KR, P), f)
    for g, w in enumerate((i["w_rg"], i["w_ig"])):
        for n in range(2 * KR):
            h = 64 * (n % 2)
            gates[h:h + 64, g, n // 2, h:h + 64] = w[n]
    inv = (10000.0 ** (-(np.arange(hr, dtype=np.float64) * 2.0 / ROPE))).astype(f)
    pos = np.concatenate([np.arange(SEQ), np.full(DEC, PAST)]).astype(f)
    ang = (pos[:, None] * inv[None, :]).astype(f).astype(np.float64)
    co, si = np.cos(ang).astype(f).T, np.sin(ang).astype(f).T
    w_router = np.zeros((D, 64), f)
    w_router[:, :NG] = i["w_group"]
    w_router[:, NG:NG + NE] = i["w_expert"]
    number = np.arange(P)[:, None] + P * np.arange(TT)[None, :] + 1
    number = np.concatenate([number, number + HALF_ID], 1)
    return {
        "xT": x_tok.T.reshape(KD, P, TOK).transpose(1, 0, 2), "x_tok": x_tok,
        "kv_cache": i["cache_kv_latent"], "rope_cache": i["cache_k_rope"],
        "conv_st": i["state_conv"].reshape(DEC, CONV - 1, KR, P).transpose(3, 2, 1, 0),
        "rec_st": i["state_rec"].reshape(DEC, KR, P).transpose(2, 1, 0),
        "page_rep": np.repeat(i["page_table"].T, P // N_PAGES, axis=0).astype(np.int32),
        "lane": (np.arange(P) % 8).astype(np.int32)[:, None],
        "w_in": w_in13, "w_kpe": w_kpe, "w_uq": w_uq, "w_uk": w_uk, "w_uv": w_uv, "w_ukT": w_ukT, "vecs": vecs,
        "gates": gates.reshape(P, -1), "cs_tab": np.concatenate([co, co, -si, si], 0),
        "w_out": chunks(i["w_out"], KD).reshape(P, -1), "w_router": chunks(w_router, KD).reshape(P, -1),
        "r_bias": np.concatenate([i["b_group"], i["b_expert"]]),
        "lns": np.stack([i["ln1_g"], i["ln1_b"], i["ln2_g"], i["ln2_b"]]),
        "ids": np.stack([number // CAP, number % CAP], 2).astype(f),
        "count": np.arange(CAP, dtype=f),
        "w_gu": i["w_gate_up"], "w_dn": i["w_down"],
    }, c


_OUTS = {"y": (TOK, D), "ckv": (P, KKV, TOK), "kpe": (ROPE, TOK), "conv_p": (P, KR, CONV - 1), "rec_p": (P, KR),
         "conv_s": (P, KR, CONV - 1, DEC), "rec_s": (P, KR, DEC)}


def kernel(**inputs):
    import concourse.bacc as _bacc
    from concourse.bass_utils import run_bass_kernel_spmd as _run

    laid, c = _lay_out({k: np.asarray(v) for k, v in inputs.items()})
    nc = _bacc.Bacc("TRN2", target_bir_lowering=False, num_devices=1)
    arrays, args = {}, []
    for name, a in laid.items():
        a = c(a)
        arrays["in_" + name] = a
        args.append(nc.dram_tensor("in_" + name, a.shape, mybir.dt.from_np(a.dtype), kind="ExternalInput").ap())
    for name, shape in _OUTS.items():
        args.append(nc.dram_tensor("out_" + name, shape, F32, kind="ExternalOutput").ap())
    hymba_step(nc, *args)
    r = _run(nc, [arrays], core_ids=[0]).results[0]
    o = {k: np.asarray(r["out_" + k]) for k in _OUTS}
    ckv = o["ckv"].transpose(2, 1, 0).reshape(TOK, KVL)
    kpe = o["kpe"].T
    y = o["y"]
    conv_s = o["conv_s"].transpose(3, 2, 1, 0).reshape(DEC, CONV - 1, REC)
    return (c(y[:SEQ]).reshape(1, SEQ, D), c(y[SEQ:]).reshape(DEC, 1, D),
            c(ckv[:SEQ]).reshape(1, SEQ, KVL), c(kpe[:SEQ]).reshape(1, SEQ, ROPE),
            c(o["conv_p"].transpose(2, 1, 0)).reshape(1, CONV - 1, REC), c(o["rec_p"].T).reshape(1, REC),
            c(ckv[SEQ:]).reshape(DEC, 1, KVL), c(kpe[SEQ:]).reshape(DEC, 1, ROPE),
            c(conv_s), c(o["rec_s"].transpose(2, 1, 0)).reshape(DEC, REC))
```
